# Optimizing a Trainium2 kernel written in Bass

```python
import math
import jax, jax.numpy as jnp
from jax import lax
import numpy as np

D_MODEL = 1024
BATCH = 1
SEQ = 1024
DEPTH = 2

N_A = DEPTH // 2
N_B = DEPTH - N_A
HEAD_DIM = 64
N_MAIN_HEADS = 12
D_MAIN = N_MAIN_HEADS * HEAD_DIM
N_MEM_HEADS = 4
D_MEMH = N_MEM_HEADS * HEAD_DIM
D_MIX = D_MAIN + D_MEMH
MEM_LEN = 256
D_DECAY_LORA = 64
D_AAA_LORA = 64
D_GATE_LORA = 160
D_SHIFT = 3 * D_MAIN + D_DECAY_LORA + D_AAA_LORA + D_GATE_LORA
D_IN_A = D_SHIFT + D_MEMH
D_IN_B = 2 * D_MAIN + D_MEMH
D_KV = 2 * D_MAIN + N_MAIN_HEADS
D_FF = 256 * (-(-8 * D_MODEL // (3 * 256)))
BLOCK_Q = 128
RMS_EPS = 1e-6
GN_EPS = 64e-5
ATTN_SCALE = HEAD_DIM ** -0.5
NEG_INF = -1e30

kernel_name = "rwkv7_fox_yoco_memory_hybrid"

def rms_norm(x, g, eps=RMS_EPS):
    xf = x.astype(jnp.float32)
    y = xf * lax.rsqrt(jnp.mean(xf * xf, axis=-1, keepdims=True) + eps)
    return (y * g.astype(jnp.float32)).astype(x.dtype)

def token_shift(u):
    return jnp.pad(u[:, :-1], ((0, 0), (1, 0), (0, 0)))

def split_heads(u, n):
    return u.reshape(u.shape[:-1] + (n, HEAD_DIM))

def swiglu(h, w_gate_up, w_down):
    gu = h @ w_gate_up
    return (jax.nn.silu(gu[..., :D_FF]) * gu[..., D_FF:]) @ w_down

def memory_attention(q_cols, mem, mem_norm_g, w_mem_kv, q_gain, k_gain):
    bsz, t = q_cols.shape[:2]
    q = rms_norm(split_heads(q_cols, N_MEM_HEADS), q_gain)
    kv = rms_norm(mem, mem_norm_g) @ w_mem_kv
    k = rms_norm(split_heads(kv[..., :D_MEMH], N_MEM_HEADS), k_gain)
    v = split_heads(kv[..., D_MEMH:], N_MEM_HEADS)
    s = jnp.einsum('bthd,bmhd->bhtm', q, k).astype(jnp.float32) * ATTN_SCALE
    p = jax.nn.softmax(s, axis=-1).astype(v.dtype)
    o = jnp.einsum('bhtm,bmhd->bthd', p, v)
    return o.reshape(bsz, t, D_MEMH)

def rwkv7_time_mix(u, mu, w0, w_up, a0, a_up, g_up, k_k, k_a, r_k, lnx_g, lnx_b):
    bsz, t = u.shape[:2]
    f32 = jnp.float32
    us = u + (token_shift(u) - u) * mu
    o = 0
    r = us[..., o:o + D_MAIN]; o += D_MAIN
    k = us[..., o:o + D_MAIN]; o += D_MAIN
    v = us[..., o:o + D_MAIN]; o += D_MAIN
    wd = us[..., o:o + D_DECAY_LORA]; o += D_DECAY_LORA
    ad = us[..., o:o + D_AAA_LORA]; o += D_AAA_LORA
    gd = us[..., o:o + D_GATE_LORA]
    w_log = -jax.nn.softplus(-(w0 + jnp.tanh(wd) @ w_up)) - 0.5
    decay = jnp.exp(-jnp.exp(w_log.astype(f32)))
    a = jax.nn.sigmoid(a0 + ad @ a_up)
    g = jax.nn.sigmoid(gd) @ g_up
    kk = split_heads((k * k_k).astype(f32), N_MAIN_HEADS)
    kk = kk * lax.rsqrt(jnp.maximum(jnp.sum(kk * kk, -1, keepdims=True), 1e-24))
    k = k * (1 + (a - 1) * k_a)
    rh, wh, kh, vh, ah = (split_heads(z.astype(f32), N_MAIN_HEADS) for z in (r, decay, k, v, a))

    def step(state, inp):
        r_t, w_t, k_t, v_t, kk_t, a_t = inp
        sa = jnp.einsum('bhvk,bhk->bhv', state, -kk_t)
        state = (state * w_t[:, :, None, :]
                 + sa[..., None] * (kk_t * a_t)[:, :, None, :]
                 + v_t[..., None] * k_t[:, :, None, :])
        return state, jnp.einsum('bhvk,bhk->bhv', state, r_t)

    xs = tuple(jnp.moveaxis(z, 1, 0) for z in (rh, wh, kh, vh, kk, ah))
    s0 = jnp.zeros((bsz, N_MAIN_HEADS, HEAD_DIM, HEAD_DIM), f32)
    _, y = lax.scan(step, s0, xs)
    y = jnp.moveaxis(y, 0, 1)
    mean = jnp.mean(y, -1, keepdims=True)
    var = jnp.mean(jnp.square(y - mean), -1, keepdims=True)
    yn = ((y - mean) * lax.rsqrt(var + GN_EPS)).reshape(bsz, t, D_MAIN)
    yn = yn * lnx_g.astype(f32) + lnx_b.astype(f32)
    bonus = jnp.sum(rh * kh * r_k.astype(f32), -1, keepdims=True) * vh
    out = (yn + bonus.reshape(bsz, t, D_MAIN)) * g.astype(f32)
    return out.astype(u.dtype)

def shared_kv(h, kv_norm_g, w_kv, b_f, k_gain):
    kvf = rms_norm(h, kv_norm_g) @ w_kv
    k = rms_norm(split_heads(kvf[..., :D_MAIN], N_MAIN_HEADS), k_gain)
    v = split_heads(kvf[..., D_MAIN:2 * D_MAIN], N_MAIN_HEADS)
    log_f = jax.nn.log_sigmoid((kvf[..., 2 * D_MAIN:] + b_f).astype(jnp.float32))
    c = jnp.cumsum(log_f, axis=1)
    return k, v, c

def forgetting_attention(q, k, v, c):
    t = q.shape[1]
    c_h = jnp.transpose(c, (0, 2, 1))
    outs = []
    for blk in range(t // BLOCK_Q):
        q0 = blk * BLOCK_Q
        q1 = q0 + BLOCK_Q
        s = jnp.einsum('bqhd,bkhd->bhqk', q[:, q0:q1], k[:, :q1]).astype(jnp.float32) * ATTN_SCALE
        s = s + c_h[:, :, q0:q1, None] - c_h[:, :, None, :q1]
        causal = jnp.arange(q1)[None, :] <= (q0 + jnp.arange(BLOCK_Q))[:, None]
        s = jnp.where(causal, s, NEG_INF)
        p = jax.nn.softmax(s, axis=-1).astype(v.dtype)
        outs.append(jnp.einsum('bhqk,bkhd->bqhd', p, v[:, :q1]))
    return jnp.concatenate(outs, axis=1)

def setup_inputs(seed: int = 0) -> dict:
    key = jax.random.key(seed)
    ks = iter(jax.random.split(key, 40))
    f32 = jnp.float32

    def nrm(shape, scale):
        return jax.random.normal(next(ks), shape, f32) * scale

    def gain(shape):
        return 1.0 + nrm(shape, 0.02)

    d = D_MODEL
    return {
        "x": nrm((BATCH, SEQ, d), 1.0),
        "mem": nrm((BATCH, MEM_LEN, d), 1.0),
        "mix_norm": gain((DEPTH, d)),
        "w_out": nrm((DEPTH, D_MIX, d), 0.5 * D_MIX ** -0.5),
        "mem_norm": gain((DEPTH, d)),
        "w_mem_kv": nrm((DEPTH, d, 2 * D_MEMH), d ** -0.5),
        "mem_q_gain": gain((DEPTH, HEAD_DIM)),
        "mem_k_gain": gain((DEPTH, HEAD_DIM)),
        "ffn_norm": gain((DEPTH, d)),
        "w_gate_up": nrm((DEPTH, d, 2 * D_FF), d ** -0.5),
        "w_down": nrm((DEPTH, D_FF, d), 0.5 * D_FF ** -0.5),
        "a_w_in": nrm((N_A, d, D_IN_A), d ** -0.5),
        "a_mu": jax.random.uniform(next(ks), (N_A, D_SHIFT), f32),
        "a_w0": nrm((N_A, D_MAIN), 0.5),
        "a_w_up": nrm((N_A, D_DECAY_LORA, D_MAIN), 0.1),
        "a_a0": nrm((N_A, D_MAIN), 0.5),
        "a_a_up": nrm((N_A, D_AAA_LORA, D_MAIN), 0.5 * D_AAA_LORA ** -0.5),
        "a_g_up": nrm((N_A, D_GATE_LORA, D_MAIN), D_GATE_LORA ** -0.5),
        "a_k_k": 0.85 + nrm((N_A, D_MAIN), 0.05),
        "a_k_a": 1.0 + nrm((N_A, D_MAIN), 0.05),
        "a_r_k": nrm((N_A, N_MAIN_HEADS, HEAD_DIM), 0.1),
        "a_lnx_g": gain((N_A, D_MAIN)),
        "a_lnx_b": nrm((N_A, D_MAIN), 0.02),
        "kv_norm": gain((d,)),
        "w_kv": nrm((d, D_KV), d ** -0.5),
        "b_f": 2.0 + nrm((N_MAIN_HEADS,), 0.5),
        "k_gain": gain((HEAD_DIM,)),
        "b_w_in": nrm((N_B, d, D_IN_B), d ** -0.5),
        "b_q_gain": gain((N_B, HEAD_DIM)),
    }

def reference(x, mem, mix_norm, w_out, mem_norm, w_mem_kv, mem_q_gain, mem_k_gain,
              ffn_norm, w_gate_up, w_down, a_w_in, a_mu, a_w0, a_w_up, a_a0, a_a_up,
              a_g_up, a_k_k, a_k_a, a_r_k, a_lnx_g, a_lnx_b, kv_norm, w_kv, b_f, k_gain,
              b_w_in, b_q_gain):
    bsz, t = x.shape[:2]

    def merge_and_ffn(x, l, main_out, mem_cols):
        mem_out = memory_attention(mem_cols, mem, mem_norm[l], w_mem_kv[l], mem_q_gain[l], mem_k_gain[l])
        x = x + jnp.concatenate([main_out, mem_out], axis=-1) @ w_out[l]
        return x + swiglu(rms_norm(x, ffn_norm[l]), w_gate_up[l], w_down[l])

    for i in range(N_A):
        l = i
        u = rms_norm(x, mix_norm[l]) @ a_w_in[i]
        main = rwkv7_time_mix(u[..., :D_SHIFT], a_mu[i], a_w0[i], a_w_up[i], a_a0[i], a_a_up[i],
                              a_g_up[i], a_k_k[i], a_k_a[i], a_r_k[i], a_lnx_g[i], a_lnx_b[i])
        x = merge_and_ffn(x, l, main, u[..., D_SHIFT:])

    k_sh, v_sh, c_sh = shared_kv(x, kv_norm, w_kv, b_f, k_gain)

    for j in range(N_B):
        l = N_A + j
        u = rms_norm(x, mix_norm[l]) @ b_w_in[j]
        q = rms_norm(split_heads(u[..., :D_MAIN], N_MAIN_HEADS), b_q_gain[j])
        o = forgetting_attention(q, k_sh, v_sh, c_sh).reshape(bsz, t, D_MAIN)
        main = o * jax.nn.sigmoid(u[..., D_MAIN:2 * D_MAIN])
        x = merge_and_ffn(x, l, main, u[..., 2 * D_MAIN:])

    return x


_drawn_inputs = setup_inputs


def setup_inputs(seed=0):
    import zlib

    import numpy as np

    out = dict(_drawn_inputs(seed))
    spreads = {}
    factors = {'mix_norm': 5.516,
     'mem_norm': 27.988,
     'mem_q_gain': 27.265,
     'mem_k_gain': 28.731,
     'ffn_norm': 20.93,
     'a_k_k': 64.0,
     'a_k_a': 3.89,
     'a_lnx_g': 64.0,
     'a_lnx_b': 64.0,
     'kv_norm': 50.464,
     'k_gain': 155.452,
     'b_q_gain': 51.049,
     'a_w0': 2.811,
     'a_w_up': 3.545,
     'b_f': 9.479}
    for name, (base, spread) in spreads.items():
        noise = np.random.default_rng([zlib.crc32(name.encode()), seed]).standard_normal(out[name].shape)
        drawn = base * np.exp(spread * noise) if base else spread * noise
        out[name] = __import__('jax').numpy.asarray(drawn.astype(out[name].dtype))
    for name, factor in factors.items():
        out[name] = (out[name] * factor).astype(out[name].dtype)
    return out
```

```python
from contextlib import ExitStack
import math

import numpy as np
import concourse.bass as bass
from concourse import mybir

ALU = mybir.AluOpType
ACT = mybir.ActivationFunctionType
F32 = mybir.dt.float32
F32R = mybir.dt.float32r
AX_X = mybir.AxisListType.X

P = 128
D = 1024
KT = D // P
T = 1024
TT = T // P
HALF = 512
M = 256
HD = 64
D_MAIN = 768
PAIRS = D_MAIN // P
MEM_PAIRS = 2
D_FF = 2816
FT = D_FF // P
FF_GROUPS = [6, 6, 5, 5]
D_SHIFT = 2592
C = 64
RMS_EPS = 1e-6
GN_EPS = 64e-5
DECAY = math.exp(-0.5)
SCALE = HD ** -0.5
RING = 3
LEVELS = 5


def shape_constants():
    i = np.arange(P)
    r, c = i[:, None], i[None, :]
    same = (r // C) == (c // C)
    cols = {
        "ident": (r == c),
        "before": same & (r < c),
        "upto": same & (r <= c),
        "after": same & (r > c),
        "pairsum": (r // HD) == (c // HD),
        "pair0": (r == c + 1) & (r % 2 == 1),
    }
    for l in range(LEVELS + 1):
        b = 1 << l
        cols[f"join{l}"] = ((c // b) % 2 == 1) & ((r // b) == (c // b) - 1)
    out = {k: v.astype(np.float32) for k, v in cols.items()}
    out["future"] = np.where(c > r, np.float32(-1e30), np.float32(0))
    out["heads"] = np.stack([(i < HD), (i >= HD)], 1).astype(np.float32)
    out["ones"] = np.ones((P, 1), np.float32)
    out["minus_half"] = np.full((P, 16), -0.5, np.float32)
    place, at = {}, 0
    for k, v in out.items():
        place[k] = (at, at + v.shape[1])
        at += v.shape[1]
    return np.concatenate(list(out.values()), 1), place


def chunk_starts():
    keep = np.ones((P, T), np.float32)
    keep[:, ::C] = 0.0
    return keep


class Program:
    def __init__(self, nc, ins, out):
        self.nc, self.ins, self.out = nc, ins, out
        self.cleared = []
        self.taken = []
        self.ctx = ExitStack()

    def sem(self, name):
        s = self.nc.alloc_semaphore(f"{self.phase}_{name}")
        self.taken.append(s)
        return s

    def phase_begins(self, name):
        self.phase = name
        self.loaded = self.sem("loaded")
        self.squared = self.sem("squared")
        self.sums = self.sem("sums")
        self.mean_sq = self.sem("mean_sq")
        self.rstd = self.sem("rstd")
        self.spread_done = self.sem("spread")
        self.h_full = self.sem("h_full")
        self.h_hi = self.sem("h_hi")
        self.h_lo = self.sem("h_lo")
        self.psum_free = self.sem("psum_free")
        self.vector_link = self.sem("vector_link")

    def phase_over(self):
        numbers = sorted(s.num for s in self.taken)
        first = 0
        for i in range(1, len(numbers) + 1):
            if i == len(numbers) or numbers[i] != numbers[i - 1] + 1:
                self.nc.gpsimd.sem_clear(range(numbers[first], numbers[i - 1] + 1))
                first = i
        for s in self.cleared:
            self.nc.release_semaphore(s)
        self.cleared, self.taken = self.taken, []

    def linker(self, engine, semaphore):
        done = [0]

        def link(instruction):
            done[0] += 1
            instruction.then_inc(semaphore, 1)
            engine.wait_ge(semaphore, done[0])
        return link

    def sb(self, ctx, name, shape, dt=F32):
        return ctx.enter_context(self.nc.sbuf_tensor(name, shape, dt))


    def strip(self, w, row0, tiles, col0, cols=P):
        return (w[row0:row0 + tiles * P, col0:col0 + cols].rearrange("(k p) c -> p k c", p=P), tiles, cols)

    def list_strips(self):
        i = self.ins
        s = self.strips = []
        self.first = {}

        def mark(name):
            self.first[name] = len(s)

        mark("in_a")
        self.a_plan = []
        mem = [("mem", l, c) for l in range(2) for c in range(4)]
        for c in range(23):
            if c < 21:
                s.append(self.strip(i["a_w_in"][0], 0, KT, c * P))
                self.a_plan.append(("shift", c))
            else:
                s.append(self.strip(i["a_w_in"][0], 0, KT, D_SHIFT + (c - 21) * P))
                self.a_plan.append(("plain", c))
            if c % 2 == 1 and mem:
                _, l, m = mem.pop(0)
                s.append(self.strip(i["w_mem_kv"][l], 0, KT, m * P))
                self.a_plan.append(("memk" if m < 2 else "memv", (l, m % 2)))
        for l in range(2):
            if l == 1:
                mark("kv")
                for c in range(12):
                    s.append(self.strip(i["w_kv"], 0, KT, c * P))
                s.append(self.strip(i["w_kv"], 0, KT, 2 * D_MAIN, 12))
                mark("in_b")
                for c in range(14):
                    s.append(self.strip(i["b_w_in"][0], 0, KT, c * P))
            mark(f"out{l}")
            for c in range(KT):
                s.append(self.strip(i["w_out"][l], 0, KT, c * P))
            f0 = 0
            for g, n in enumerate(FF_GROUPS):
                mark(f"up{l}{g}")
                for f in range(f0, f0 + n):
                    s.append(self.strip(i["w_gate_up"][l], 0, KT, f * P))
                    s.append(self.strip(i["w_gate_up"][l], 0, KT, D_FF + f * P))
                mark(f"down{l}{g}")
                for c in range(KT):
                    s.append(self.strip(i["w_down"][l], f0 * P, n, c * P))
                f0 += n
        self.raw_upto = 0
        self.split_upto = 0

    def load_strip(self, sp, s):
        if s >= len(self.strips):
            return
        src, tiles, cols = self.strips[s]
        if s >= RING:
            sp.wait_ge(self.w_lo, s - RING + 1)
        n = self.w_raw[s % RING]
        sp.dma_start(self.raw[:, s % RING, 0:tiles, 0:cols], src).then_inc(n, 16)

    def split_strip(self, pool, s):
        if s >= len(self.strips):
            return
        _, tiles, _ = self.strips[s]
        pool.wait_ge(self.w_raw[s % RING], 16 * (s // RING + 1))
        if s >= RING:
            pool.wait_ge(self.strip_done, s - RING + 1)
        r = s % RING
        raw = self.raw[:, r, 0:tiles, :]
        self.nc.gpsimd.tensor_copy(self.whi[:, r, 0:tiles, :], raw).then_inc(self.w_hi, 1)
        pool.wait_ge(self.w_hi, s + 1)
        self.nc.gpsimd.tensor_tensor(
            self.wlo[:, r, 0:tiles, :], raw, self.whi[:, r, 0:tiles, :].bitcast(F32), ALU.subtract).then_inc(self.w_lo, 1)

    def gemm_strip(self, pe, s, slot, hh, hl, kind="fm", width=T, before_k=None):
        nc = self.nc
        _, tiles, _ = self.strips[s]
        pe.wait_ge(self.w_lo, s + 1)
        r = s % RING
        wh, wl = self.whi[:, r], self.wlo[:, r]
        bank = self.ps
        mm = None
        if kind == "fm":
            n = min(width, HALF)
            parts = width // n
            for k in range(tiles):
                if before_k is not None:
                    before_k(k)
                for a, w in enumerate((wh, wl)):
                    for b, h in enumerate((hh, hl)[:2 - a]):
                        for j in range(parts):
                            mm = nc.tensor.matmul(bank[:, 2 * slot + j, 0:n], w[:, k, :], h[:, k, j * n:(j + 1) * n],
                                                  start=(k == 0 and a == 0 and b == 0), stop=(k == tiles - 1 and a == 1))
        else:
            for t in range(width // P):
                o = bank[:, 2 * slot + t // 4, (t % 4) * P:(t % 4 + 1) * P]
                for k in range(tiles):
                    for a, h in enumerate((hh, hl)):
                        for b, w in enumerate((wh, wl)[:2 - a]):
                            mm = nc.tensor.matmul(o, h[:, k, t * P:(t + 1) * P], w[:, k, :],
                                                  start=(k == 0 and a == 0 and b == 0), stop=(k == tiles - 1 and a == 1))
        mm.then_inc(self.strip_done, 1)

    def weights_for(self, last):
        return range(self.split_upto, min(last + RING, len(self.strips)))


    def build(self):
        nc, ctx = self.nc, self.ctx
        with ctx:
            ins = self.ins
            self.raw = self.sb(ctx, "w_raw", [P, RING, KT, P])
            self.whi = self.sb(ctx, "w_hi", [P, RING, KT, P], F32R)
            self.wlo = self.sb(ctx, "w_lo", [P, RING, KT, P], F32R)
            self.X = self.sb(ctx, "x_res", [P, KT, T])
            n = ins["consts"].shape[1]
            self.k = self.sb(ctx, "consts_sb", [P, n])
            self.params = self.sb(ctx, "params_sb", [P, 192])
            self.ps = ctx.enter_context(nc.psum_tensor("ps", [P, 8, HALF], F32))
            dram = lambda name, shape: nc.dram_tensor(name, shape, F32, kind="Internal").ap()
            self.x_dram = dram("x_dram", (P, KT, T))
            self.u_dram = dram("u_dram", (23, P, T))
            self.kv_dram = dram("kv_dram", (13, P, T))
            self.memk_dram = dram("memk_dram", (4, P, M))
            self.memv_dram = dram("memv_dram", (4, P, M))
            self.negc_dram = dram("negc_dram", (12, T))

            self.w_raw = [ctx.enter_context(nc.semaphore(f"w_raw{r}")) for r in range(RING)]
            self.w_hi = ctx.enter_context(nc.semaphore("w_hi"))
            self.w_lo = ctx.enter_context(nc.semaphore("w_lo"))
            self.strip_done = ctx.enter_context(nc.semaphore("strip_done"))
            self.params_in = ctx.enter_context(nc.semaphore("params_in"))
            self.out_stored = ctx.enter_context(nc.semaphore("out_stored"))
            self.list_strips()
            self.phase_load()
            with ExitStack() as scope:
                self.alloc_h(scope, "a")
                self.phase_in_a(scope)
            self.phase_rwkv()
            self.phase_mem_attention(0, 21)
            self.phase_out_and_ffn(0)
            with ExitStack() as scope:
                self.alloc_h(scope, "b")
                self.phase_project(scope, "kv", 13, "kv_norm", 0)
                self.phase_project(scope, "in_b", 14, "mix_norm", 1)
            self.phase_fox()
            self.phase_mem_attention(1, 12)
            self.phase_out_and_ffn(1)
            self.phase_store()

    def alloc_h(self, ctx, tag):
        self.hh = self.sb(ctx, f"h_hi_{tag}", [P, KT, T], F32R)
        self.hl = self.sb(ctx, f"h_lo_{tag}", [P, KT, T], F32R)

    def const(self, name):
        a, b = self.place[name]
        return self.k[:, a:b]

    def mask(self, name, n):
        return self.const(name).rearrange("p (a c) -> p a c", a=1).broadcast_to([P, n, P])

    def mask4(self, name):
        return self.const(name).rearrange("p (a b c) -> p a b c", a=1, b=1).broadcast_to([P, 2, 2, P])


    def phase_load(self):
        nc, ins, ps = self.nc, self.ins, self.ps
        with ExitStack() as scope:
            xin = self.sb(scope, "x_in", [P, TT, D])
            stage = self.sb(scope, "param_rows", [P, P])
            self.phase_begins("load")
            consts_in, x_saved, stage_zero = self.sem("consts_in"), self.sem("x_saved"), self.sem("stage_zero")
            turned, params_turned = self.sem("turned"), self.sem("params_turned")
            even_out, odd_out = self.sem("even_out"), self.sem("odd_out")
            block = scope.enter_context(nc.Block())

            self.place_params = {}
            loads = []
            at = 0

            def vec(name, ap, tiles):
                nonlocal at
                self.place_params[name] = at
                loads.append((at, tiles, slice(0, P), ap.rearrange("(n p) -> n p", p=P)))
                at += tiles

            for l in range(2):
                vec(f"mix_norm{l}", ins["mix_norm"][l], KT)
                vec(f"mem_norm{l}", ins["mem_norm"][l], KT)
                vec(f"ffn_norm{l}", ins["ffn_norm"][l], KT)
            vec("kv_norm0", ins["kv_norm"], KT)
            vec("mu", ins["a_mu"][0][0:20 * P], 20)
            for name in ("a_w0", "a_a0", "a_k_k", "a_k_a", "a_lnx_g", "a_lnx_b"):
                vec(name, ins[name][0], PAIRS)
            vec("a_r_k", ins["a_r_k"][0].rearrange("h d -> (h d)"), PAIRS)
            self.place_params["mu_last"] = at
            loads.append((at, 1, slice(0, 32), ins["a_mu"][0][20 * P:D_SHIFT].rearrange("(n p) -> n p", p=32)))
            mu_last = at
            at += 1
            for name, ap in (("mem_q_gain0", ins["mem_q_gain"][0]), ("mem_q_gain1", ins["mem_q_gain"][1]),
                             ("mem_k_gain0", ins["mem_k_gain"][0]), ("mem_k_gain1", ins["mem_k_gain"][1]),
                             ("k_gain", ins["k_gain"]), ("b_q_gain", ins["b_q_gain"][0])):
                self.place_params[name] = at
                for h in range(2):
                    loads.append((at, 1, slice(h * HD, (h + 1) * HD), ap.rearrange("(n p) -> n p", p=HD)))
                at += 1
            self.place_params["b_f"] = at
            loads.append((at, 1, slice(0, 12), ins["b_f"].rearrange("(n p) -> n p", p=12)))
            at += 1
            rows = at
            assert rows <= P
            self.place_params["one_minus_mu"] = at
            at += 21
            assert at <= 192

            @block.sync
            def _(sp):
                for t in range(TT):
                    sp.dma_start(xin[:, t, :], ins["x"][0, t * P:(t + 1) * P, :]).then_inc(self.loaded, 16)
                    sp.wait_ge(self.loaded, 16 * (t + 1))
                for s in range(RING):
                    self.load_strip(sp, s)
                sp.wait_ge(even_out, TT // 2)
                sp.wait_ge(odd_out, TT // 2)
                sp.dma_start(self.x_dram, self.X[:]).then_inc(x_saved, 16)
                sp.wait_ge(x_saved, 16)

            @block.scalar
            def _(act):
                act.dma_start(self.k[:], ins["consts"]).then_inc(consts_in, 16)
                for t in range(1, TT, 2):
                    act.wait_ge(turned, t + 1)
                    nc.scalar.activation(self.X[:, :, t * P:(t + 1) * P],
                                                         ps[:, 2 * (t % 4):2 * (t % 4) + 2, :].rearrange("p b (k c) -> p (b k) c", c=P), ACT.Copy).then_inc(odd_out, 1)

            @block.vector
            def _(dve):
                link = self.linker(dve, self.vector_link)
                nc.vector.memset(stage[:], 0.0).then_inc(stage_zero, 1)
                for t in range(0, TT, 2):
                    dve.wait_ge(turned, t + 1)
                    nc.vector.tensor_copy(self.X[:, :, t * P:(t + 1) * P],
                                                          ps[:, 2 * (t % 4):2 * (t % 4) + 2, :].rearrange("p b (k c) -> p (b k) c", c=P)).then_inc(even_out, 1)
                dve.wait_ge(params_turned, 1)
                link(nc.vector.tensor_copy(self.params[:, 0:rows], ps[:, 0, 0:rows]))
                o, m = self.place_params["one_minus_mu"], self.place_params["mu"]
                nc.vector.tensor_scalar(self.params[:, o:o + 20], self.params[:, m:m + 20], -1.0, 1.0, ALU.mult, ALU.add)
                nc.vector.tensor_scalar(self.params[:, o + 20:o + 21], self.params[:, mu_last:mu_last + 1],
                                                        -1.0, 1.0, ALU.mult, ALU.add).then_inc(stage_zero, 1)

            @block.tensor
            def _(pe):
                pe.wait_ge(consts_in, 16)
                for t in range(TT):
                    pe.wait_ge(self.loaded, 16 * (t + 1))
                    if t >= 4:
                        pe.wait_ge((even_out if t % 2 == 0 else odd_out), (t - 4) // 2 + 1)
                    for k in range(KT):
                        mm = nc.tensor.transpose(ps[:, 2 * (t % 4) + k // 4, (k % 4) * P:(k % 4 + 1) * P],
                                                 xin[:, t, k * P:(k + 1) * P], self.const("ident"))
                    mm.then_inc(turned, 1)
                pe.wait_ge(self.params_in, 16 * len(loads))
                pe.wait_ge(even_out, TT // 2 - 1)
                nc.tensor.transpose(ps[:, 0, 0:rows], stage[0:rows, :], self.const("ident")[0:rows, 0:rows]).then_inc(params_turned, 1)

            @block.gpsimd
            def _(pool):
                pool.wait_ge(stage_zero, 1)
                for row, n, cols, src in loads:
                    pool.dma_start(stage[row:row + n, cols], src).then_inc(self.params_in, 16)
                for s in range(RING):
                    self.split_strip(pool, s)

        self.split_upto = RING
        self.phase_over()

    def param(self, name, i=0):
        a = self.place_params[name] + i
        return self.params[:, a:a + 1]


    def norm_act(self, act, src, width, sq):
        for k in range(KT):
            if k >= 2:
                act.wait_ge(self.sums, k - 1)
            self.nc.scalar.activation(sq[:, k % 2, 0:width], src(k), ACT.Square).then_inc(self.squared, 1)

    def norm_pe(self, pe, width, sq, rs, slot_sum, slot_bc):
        nc, ps = self.nc, self.ps
        n = width // P
        for k in range(KT):
            pe.wait_ge(self.squared, k + 1)
            for t in range(n):
                mm = nc.tensor.matmul(ps[:, slot_sum, k * n + t:k * n + t + 1], sq[:, k % 2, t * P:(t + 1) * P],
                                      self.const("ones"), start=True, stop=True)
            mm.then_inc(self.sums, 1)
        pe.wait_ge(self.rstd, 1)
        for t in range(n):
            mm = nc.tensor.matmul(ps[:, slot_bc + t // 4, (t % 4) * P:(t % 4 + 1) * P],
                                  rs[:, t:t + 1].broadcast_to([P, P]), self.const("ident"), start=True, stop=True)
        mm.then_inc(self.spread_done, 1)

    def norm_dve_sums(self, dve, link, width, small, slot_sum):
        nc, ps = self.nc, self.ps
        n = width // P
        dve.wait_ge(self.sums, KT)
        link(nc.vector.tensor_reduce(small[:, 0, 0:n], ps[:, slot_sum, 0:KT * n].rearrange("p (k t) -> p t k", k=KT),
                                               AX_X, ALU.add))
        nc.vector.tensor_scalar(small[:, 1, 0:n], small[:, 0, 0:n], 1.0 / D, RMS_EPS, ALU.mult, ALU.add).then_inc(self.mean_sq, 1)

    def norm_pool(self, pool, width, small):
        n = width // P
        pool.wait_ge(self.mean_sq, 1)
        self.nc.gpsimd.tensor_tensor(small[:, 2, 0:n], small[:, 1, 0:n], self.const("minus_half")[:, 0:n], ALU.pow).then_inc(self.rstd, 1)


    def phase_in_a(self, scope):
        nc, ins, ps = self.nc, self.ins, self.ps
        plan = self.a_plan
        n = len(plan)
        with ExitStack() as ctx:
            self.mem_norm_phase(scope)
            sq = self.sb(ctx, "sq_a", [P, 2, T])
            small = self.sb(ctx, "small_a", [P, 3, 16])
            full = self.sb(ctx, "full_a", [P, 2, T])
            evac = self.sb(ctx, "evac_a", [P, 3, T])
            self.phase_begins("in_a")
            block = ctx.enter_context(nc.Block())
            self.norm_and_gemm(block, plan, self.first["in_a"], sq, small, full, evac, "mix_norm", 0)
        self.phase_over()

    def mem_norm_phase(self, scope):
        nc, ins, ps = self.nc, self.ins, self.ps
        self.mh = [self.sb(scope, f"mem_hi{l}", [P, KT, M], F32R) for l in range(2)]
        self.ml = [self.sb(scope, f"mem_lo{l}", [P, KT, M], F32R) for l in range(2)]
        with ExitStack() as ctx:
            min_ = self.sb(ctx, "mem_in", [P, M // P, D])
            mT = self.sb(ctx, "mem_T", [P, KT, M])
            sq = self.sb(ctx, "sq_m", [P, 2, M])
            small = self.sb(ctx, "small_m", [P, 3, 16])
            full = self.sb(ctx, "full_m", [P, KT, M])
            self.phase_begins("mem_norm")
            turned, mem_out, normed = self.sem("turned"), self.sem("mem_out"), self.sem("normed")
            block = ctx.enter_context(nc.Block())

            @block.sync
            def _(sp):
                sp.dma_start(min_[:], ins["mem"][0].rearrange("(t p) d -> p t d", p=P)).then_inc(self.loaded, 16)

            @block.tensor
            def _(pe):
                pe.wait_ge(self.loaded, 16)
                for t in range(M // P):
                    for k in range(KT):
                        mm = nc.tensor.transpose(ps[:, 2 * t + k // 4, (k % 4) * P:(k % 4 + 1) * P],
                                                 min_[:, t, k * P:(k + 1) * P], self.const("ident"))
                mm.then_inc(turned, 1)
                self.norm_pe(pe, M, sq, small[:, 2], 4, 6)

            @block.scalar
            def _(act):
                act.wait_ge(mem_out, 1)
                self.norm_act(act, lambda k: mT[:, k, :], M, sq)
                for l in range(2):
                    act.wait_ge(normed, l + 1)
                    nc.scalar.activation(self.mh[l][:], full[:], ACT.Copy).then_inc(self.h_hi, 1)

            @block.vector
            def _(dve):
                link = self.linker(dve, self.vector_link)
                dve.wait_ge(turned, 1)
                nc.vector.tensor_copy(mT[:, :, 0:P], ps[:, 0:2, :].rearrange("p b (k c) -> p (b k) c", c=P))
                nc.vector.tensor_copy(mT[:, :, P:M], ps[:, 2:4, :].rearrange("p b (k c) -> p (b k) c", c=P)).then_inc(mem_out, 1)
                dve.wait_ge(mem_out, 1)
                self.norm_dve_sums(dve, link, M, small, 4)
                dve.wait_ge(self.spread_done, 1)
                for l in range(2):
                    for k in range(KT):
                        i = nc.vector.scalar_tensor_tensor(out=full[:, k, :], in0=mT[:, k, :], scalar=self.param(f"mem_norm{l}", k),
                                                           in1=ps[:, 6, 0:M], op0=ALU.mult, op1=ALU.mult)
                    i.then_inc(normed, 1)
                    dve.wait_ge(self.h_hi, l + 1)
                    dve.wait_ge(normed, l + 1)
                    link(nc.vector.tensor_tensor(self.ml[l][:], full[:], self.mh[l][:].bitcast(F32), ALU.subtract))

            @block.gpsimd
            def _(pool):
                self.norm_pool(pool, M, small)
        self.phase_over()

    def norm_and_gemm(self, block, plan, s0, sq, small, full, evac, gain, layer):
        nc, ps = self.nc, self.ps
        n = len(plan)
        split_from = self.split_upto
        split_to = min(s0 + n + RING, len(self.strips))
        stored = [self.sem(f"stored{r}") for r in range(3)]
        shifted, gate_in, soft = self.sem("shifted"), self.sem("gate_in"), self.sem("soft")

        def target(i):
            kind, c = plan[i]
            if kind in ("shift", "plain"):
                return self.u_dram[c], evac[:, i % 3, :]
            if kind == "kv":
                return self.kv_dram[c], evac[:, i % 3, :]
            if kind == "vt":
                return self.kv_dram[c], evac[:, i % 3, :]
            if kind == "f":
                return self.negc_dram, evac[0:12, i % 3, :]
            d = self.memk_dram if kind == "memk" else self.memv_dram
            return d[2 * c[0] + c[1]], evac[:, i % 3, 0:M]

        @block.sync
        def _(sp):
            for i in range(n):
                if s0 + i + RING >= split_from and s0 + i + RING < split_to:
                    self.load_strip(sp, s0 + i + RING)
                sp.wait_ge(self.psum_free, i + 1)
                dst, src = target(i)
                sp.dma_start(dst, src).then_inc(stored[i % 3], 16)
            for r in range(3):
                sp.wait_ge(stored[r], 16 * len(range(r, n, 3)))

        @block.gpsimd
        def _(pool):
            self.norm_pool(pool, T, small)
            for s in range(split_from, split_to):
                self.split_strip(pool, s)

        @block.scalar
        def _(act):
            link = self.linker(act, shifted if ("f", 12) in plan else None)
            self.norm_act(act, lambda k: self.X[:, k, :], T, sq)
            for k in range(KT):
                act.wait_ge(self.h_full, k + 1)
                nc.scalar.activation(self.hh[:, k, :], full[:, k % 2, :], ACT.Copy).then_inc(self.h_hi, 1)
            for i, (kind, c) in enumerate(plan):
                if kind == "shift":
                    act.wait_ge(self.strip_done, s0 + i + 1)
                    if i >= 3:
                        act.wait_ge(stored[i % 3], 16 * (i // 3))
                    nc.scalar.activation(evac[:, i % 3, :], self.bank2(i % 3), ACT.Copy,
                                                            scale=self.param("one_minus_mu", c)).then_inc(shifted, 1)
                if kind == "f":
                    act.wait_ge(gate_in, 1)
                    link(nc.scalar.activation(sq[0:12, 0, :], sq[0:12, 1, :], ACT.Abs))
                    link(nc.scalar.activation(full[0:12, 0, :], sq[0:12, 0, :], ACT.Exp, scale=-1.0))
                    nc.scalar.activation(full[0:12, 1, :], full[0:12, 0, :], ACT.Ln, bias=1.0).then_inc(soft, 1)

        @block.vector
        def _(dve):
            link = self.linker(dve, self.vector_link)
            if ("f", 12) in plan:
                link(nc.vector.memset(self.ones_row, 1.0))
            self.norm_dve_sums(dve, link, T, small, 4)
            dve.wait_ge(self.spread_done, 1)
            for k in range(KT):
                if k >= 2:
                    dve.wait_ge(self.h_hi, k - 1)
                    dve.wait_ge(self.h_lo, k - 1)
                nc.vector.scalar_tensor_tensor(
                    out=full[:, k % 2, :], in0=self.X[:, k, :], scalar=self.param(f"{gain}{layer}", k),
                    in1=self.bank2(3), op0=ALU.mult, op1=ALU.mult).then_inc(self.h_full, 1)
                dve.wait_ge(self.h_full, k + 1)
                dve.wait_ge(self.h_hi, k + 1)
                nc.vector.tensor_tensor(self.hl[:, k, :], full[:, k % 2, :], self.hh[:, k, :].bitcast(F32), ALU.subtract).then_inc(self.h_lo, 1)
            for i, (kind, c) in enumerate(plan):
                dve.wait_ge(self.strip_done, s0 + i + 1)
                out = evac[:, i % 3, :]
                if i >= 3:
                    dve.wait_ge(stored[i % 3], 16 * (i // 3))
                if kind == "shift":
                    mu = self.param("mu", c) if c < 20 else self.param("mu_last")
                    dve.wait_ge(shifted, sum(1 for q in plan[:i + 1] if q[0] == "shift"))
                    u = self.bank2(i % 3)
                    nc.vector.scalar_tensor_tensor(
                        out=out[:, 1:T], in0=u[:, 0:T - 1], scalar=mu, in1=out[:, 1:T], op0=ALU.mult, op1=ALU.add).then_inc(self.psum_free, 1)
                elif kind in ("memk", "memv"):
                    nc.vector.tensor_copy(out[:, 0:M], ps[:, 2 * (i % 3), 0:M]).then_inc(self.psum_free, 1)
                elif kind == "f":
                    nc.vector.tensor_scalar(sq[0:12, 1, :], self.bank2(i % 3)[0:12, :], self.param("b_f")[0:12, :],
                                                            None, ALU.add).then_inc(gate_in, 1)
                    dve.wait_ge(gate_in, 1)
                    dve.wait_ge(soft, 1)
                    link(nc.vector.scalar_tensor_tensor(out=full[0:12, 0, :], in0=sq[0:12, 1, :], scalar=0.0,
                                                                  in1=full[0:12, 1, :], op0=ALU.min, op1=ALU.subtract))
                    nc.vector.tensor_tensor_scan(out[0:12, :], self.ones_row, full[0:12, 0, :], 0.0,
                                                                     ALU.mult, ALU.subtract).then_inc(self.psum_free, 1)
                else:
                    nc.vector.tensor_copy(out, self.bank2(i % 3)).then_inc(self.psum_free, 1)

        @block.tensor
        def _(pe):
            self.norm_pe(pe, T, sq, small[:, 2], 4, 6)
            for i, (kind, c) in enumerate(plan):
                if i >= 3:
                    pe.wait_ge(self.psum_free, i - 2)
                ready = (lambda k: pe.wait_ge(self.h_lo, k + 1)) if i == 0 else None
                if kind in ("memk", "memv"):
                    self.gemm_strip(pe, s0 + i, i % 3, self.mh[c[0]], self.ml[c[0]], "fm" if kind == "memk" else "tm", M)
                else:
                    self.gemm_strip(pe, s0 + i, i % 3, self.hh, self.hl, "tm" if kind == "vt" else "fm", T, ready)

        self.split_upto = split_to

    def bank2(self, slot):
        return self.ps[:, 2 * slot:2 * slot + 2, :].rearrange("p b c -> p (b c)")

    def phase_project(self, scope, name, n, gain, layer):
        plan = {"kv": [("kv", c) for c in range(6)] + [("vt", 6 + c) for c in range(6)] + [("f", 12)],
                "in_b": [("plain", c) for c in range(14)]}[name]
        with ExitStack() as ctx:
            sq = self.sb(ctx, f"sq_{name}", [P, 2, T])
            small = self.sb(ctx, f"small_{name}", [P, 3, 16])
            full = self.sb(ctx, f"full_{name}", [P, 2, T])
            evac = self.sb(ctx, f"evac_{name}", [P, 3, T])
            if name == "kv":
                ones = self.sb(ctx, "ones_row", [12, T])
                self.ones_row = ones[:]
            self.phase_begins(name)
            block = ctx.enter_context(self.nc.Block())
            self.norm_and_gemm(block, plan, self.first[name], sq, small, full, evac, gain, layer)
        self.phase_over()


    def phase_rwkv(self):
        nc, ins, ps = self.nc, self.ins, self.ps
        STEPS = T // 256
        with ExitStack() as ctx:
            sb = lambda name, shape: self.sb(ctx, name, shape)
            self.phase_begins("rwkv")
            sg = self.sem
            lora = sb("lora_wa", [P, T])
            gate0 = sb("lora_g0", [P, T])
            gate1 = sb("lora_g1", [32, T])
            up_wa = sb("up_wa", [P, D_MAIN])
            up_g0 = sb("up_g0", [P, D_MAIN])
            up_g1 = sb("up_g1", [32, D_MAIN])
            keep = sb("keep", [P, T])
            r, k, v = sb("r", [P, T]), sb("k", [P, T]), sb("v", [P, T])
            cum = sb("cum", [P, T])
            dec = sb("dec", [P, T // C, C + 1])
            inv = sb("inv", [P, T])
            a = sb("a", [P, T])
            g = sb("g", [P, T])
            kk = sb("kk", [P, T])
            tmp, bonus, sq = sb("tmp", [P, T]), sb("bonus", [P, T]), sb("sq_r", [P, T])
            small = sb("small_r", [P, 3, 16])
            tok = [sb(f"tok_{n}", [P, TT, P]) for n in "abkv"]
            aT, bT, kT, vT = tok
            y = sb("y", [P, T])
            mb, mk = sb("mb", [P, 2, 2, 2, P]), sb("mk", [P, 2, 2, 2, P])
            mab = sb("mab", [P, 2, 2, P])
            join = sb("join", [P, 2, 4, P])
            inv_m, inv_t, um = sb("inv_m", [P, 4, P]), sb("inv_t", [P, 4, P]), sb("um", [P, 4, P])
            mv, abar, vbar, sa = sb("mv", [P, 4, HD]), sb("abar", [P, 2, P]), sb("vbar", [P, 4, HD]), sb("sa", [P, 2, P])
            state = sb("state", [P, T // C + 1, HD])
            stmp = sb("stmp", [P, HD])

            lora_in, u_in, lora_ready = sg("lora_in"), sg("u_in"), sg("lora_ready")
            z_done, z_used, cum_done, dec_done = sg("z_done"), sg("z_used"), sg("cum_done"), sg("dec_done")
            kk_raw, kk_sq, kk_sum, kk_ms, kk_rn, kk_bc = (sg("kk_" + n) for n in ("raw", "sq", "sum", "ms", "rn", "bc"))
            rk_done, rk_sum, feat, bonus_done = sg("rk_done"), sg("rk_sum"), sg("feat"), sg("bonus_done")
            turned, turned_a, turned_d = sg("turned"), sg("turned_a"), sg("turned_d")
            scored, masked, join_done, x0 = sg("scored"), sg("masked"), sg("join_done"), sg("x0")
            u_done, u_copied, xt_done, xt_added = sg("u_done"), sg("u_copied"), sg("xt_done"), sg("xt_added")
            mv_done, mv_copied, bars_done, bars_copied = sg("mv_done"), sg("mv_copied"), sg("bars_done"), sg("bars_copied")
            sa_done, sa_added, st_done, st_new = sg("sa_done"), sg("sa_added"), sg("st_done"), sg("st_new")
            y_done, y_copied = sg("y_done"), sg("y_copied")
            gn_mean, gn_centred, gn_sq, gn_sum, gn_ms, gn_rn, gn_bc, pair_done = (
                sg("gn_" + n) for n in ("mean", "centred", "sq", "sum", "ms", "rn", "bc", "pair"))
            block = ctx.enter_context(nc.Block())

            bank2 = self.bank2
            ident = self.const("ident")
            halves = [(0, slice(0, HD)), (1, slice(HD, P))]
            flat = lambda t: t.rearrange("p a c -> p (a c)")
            chunks = lambda t: t.rearrange("p (c n) -> p c n", n=C)
            dec_before = dec[:, :, 0:C]
            dec_upto = dec[:, :, 1:C + 1]

            @block.sync
            def _(sp):
                for dst, src in ((lora[:], self.u_dram[18]), (gate0[:], self.u_dram[19]), (gate1[:], self.u_dram[20][0:32, :]),
                                 (up_wa[0:HD, :], ins["a_w_up"][0]), (up_wa[HD:P, :], ins["a_a_up"][0]),
                                 (up_g0[:], ins["a_g_up"][0][0:P, :]), (up_g1[:], ins["a_g_up"][0][P:160, :]),
                                 (keep[:], ins["chunk_starts"])):
                    sp.dma_start(dst, src).then_inc(lora_in, 16)
                for p in range(PAIRS):
                    if p:
                        sp.wait_ge(y_done, STEPS * p)
                        sp.wait_ge(rk_sum, p)
                        sp.wait_ge(feat, p)
                        sp.wait_ge(turned_d, 2 * p)
                        sp.wait_ge(bonus_done, p)
                    for dst, c in ((r, p), (k, 6 + p), (v, 12 + p)):
                        sp.dma_start(dst[:], self.u_dram[c]).then_inc(u_in, 16)

            @block.tensor
            def _(pe):
                mmul = nc.tensor.matmul
                pe.wait_ge(lora_ready, 1)
                for p in range(PAIRS):
                    cols = slice(p * P, (p + 1) * P)
                    if p:
                        pe.wait_ge(pair_done, p)
                        pe.wait_ge(y_copied, STEPS * p)
                    for j in range(2):
                        t = slice(j * HALF, (j + 1) * HALF)
                        mmul(ps[:, j, :], up_wa[0:HD, cols], lora[0:HD, t], start=True, stop=True)
                        mmul(ps[:, 2 + j, :], up_wa[HD:P, cols], lora[HD:P, t], start=True, stop=True)
                        mmul(ps[:, 4 + j, :], up_g0[:, cols], gate0[:, t], start=True, stop=False)
                        mm = mmul(ps[:, 4 + j, :], up_g1[:, cols], gate1[:, t], start=False, stop=True)
                    mm.then_inc(z_done, 1)
                    pe.wait_ge(kk_sq, p + 1)
                    for t in range(TT):
                        mm = mmul(ps[:, 6, 2 * t:2 * t + 2], sq[:, t * P:(t + 1) * P], self.const("heads"), start=True, stop=True)
                    mm.then_inc(kk_sum, 1)
                    pe.wait_ge(kk_rn, p + 1)
                    pe.wait_ge(z_used, p + 1)
                    self.spread(small[:, 2, :], 0).then_inc(kk_bc, 1)
                    pe.wait_ge(rk_done, p + 1)
                    for j in range(2):
                        mm = mmul(ps[:, 2 + j, :], self.const("pairsum"), tmp[:, j * HALF:(j + 1) * HALF], start=True, stop=True)
                    mm.then_inc(rk_sum, 1)
                    pe.wait_ge(feat, p + 1)
                    pe.wait_ge(bonus_done, p + 1)
                    for n, src in enumerate((kk, a, k, v)):
                        for t in range(TT):
                            mm = nc.tensor.transpose(ps[:, 2 * n + t // 4, (t % 4) * P:(t % 4 + 1) * P], src[:, t * P:(t + 1) * P], ident)
                        mm.then_inc(turned, 1)
                    pe.wait_ge(turned_d, 2 * p + 2)
                    pe.wait_ge(turned_a, 2 * p + 2)
                    for q in range(STEPS):
                        st = STEPS * p + q
                        probs = [(i, i // 2, 2 * q + i % 2, halves[i // 2][1]) for i in range(4)]
                        if q:
                            pe.wait_ge(y_copied, st)
                            pe.wait_ge(st_new, 4 * st + p + 1)
                        for i, hn, t, h in sorted(probs, key=lambda x: x[2]):
                            c = slice(t * P, (t + 1) * P)
                            for bank, at, w, x in ((0, 0, a, kk), (0, 2, a, r), (1, 0, k, kk), (1, 2, k, r), (2, 0, kk, a)):
                                at += t % 2
                                mm = mmul(ps[:, 3 * hn + bank, at * P:(at + 1) * P], w[h, c], x[h, c], start=True, stop=True)
                        mm.then_inc(scored, 1)
                        pe.wait_ge(x0, st + 1)
                        for l in range(1, LEVELS + 1):
                            n = st * LEVELS + l - 1
                            pe.wait_ge(join_done, n + 1)
                            if l > 1:
                                pe.wait_ge(xt_added, n)
                            for i in range(4):
                                mm = mmul(ps[:, 0, i * P:(i + 1) * P], join[:, n % 2, i, :], inv_m[:, i, :], start=True, stop=True)
                            mm.then_inc(u_done, 1)
                            pe.wait_ge(u_copied, n + 1)
                            for i in range(4):
                                if l < LEVELS:
                                    mmul(ps[:, 6, i * P:(i + 1) * P], inv_t[:, i, :], um[:, i, :], start=True, stop=True)
                                mm = mmul(ps[:, 7, i * P:(i + 1) * P], um[:, i, :], inv_t[:, i, :], start=True, stop=True)
                            mm.then_inc(xt_done, 1)
                        for i, hn, t, h in probs:
                            mm = mmul(ps[:, 0, i * HD:(i + 1) * HD], mk[:, hn, 0, i % 2, :], vT[:, t, h], start=True, stop=True)
                        mm.then_inc(mv_done, 1)
                        pe.wait_ge(xt_added, (st + 1) * LEVELS)
                        pe.wait_ge(mv_copied, st + 1)
                        for i, hn, t, h in probs:
                            mmul(ps[h, 6, (i % 2) * P:(i % 2 + 1) * P], aT[:, t, h], inv_t[:, i, :], start=True, stop=True)
                            mm = mmul(ps[:, 7, i * HD:(i + 1) * HD], inv_t[:, i, :], mv[:, i, :], start=True, stop=True)
                        mm.then_inc(bars_done, 1)
                        pe.wait_ge(bars_copied, st + 1)
                        for c in range(4):
                            n = 4 * st + c
                            t, b = c // 2, slice((c % 2) * C, (c % 2 + 1) * C)
                            ci = 4 * q + c
                            pe.wait_ge(st_new, n + p + 1)
                            for h, hs in halves:
                                mm = mmul(ps[b, 1 + h, c * HD:(c + 1) * HD], abar[hs, t, b], state[hs, ci, :], start=True, stop=True)
                            mm.then_inc(sa_done, 1)
                            pe.wait_ge(sa_added, n + 1)
                            for h, hs in halves:
                                mmul(ps[hs, 3, c * HD:(c + 1) * HD], bT[b, 2 * q + t, hs], sa[b, t, hs], start=True, stop=False)
                                mm = mmul(ps[hs, 3, c * HD:(c + 1) * HD], kT[b, 2 * q + t, hs], vT[b, 2 * q + t, hs], start=False, stop=True)
                            mm.then_inc(st_done, 1)
                        for i, hn, t, h in probs:
                            o = ps[h, 4, (i % 2) * P:(i % 2 + 1) * P]
                            mmul(o, sa[:, i % 2, h], mb[:, hn, 1, i % 2, :], start=True, stop=False)
                            mmul(o, vT[:, t, h], mk[:, hn, 1, i % 2, :], start=False, stop=False)
                            for b in range(2):
                                mm = mmul(ps[h, 4, (i % 2) * P + b * C:(i % 2) * P + (b + 1) * C], state[h, 2 * t + b, :],
                                          r[h, t * P + b * C:t * P + (b + 1) * C], start=False, stop=(b == 1))
                        mm.then_inc(y_done, 1)
                    pe.wait_ge(y_copied, STEPS * (p + 1))
                    pe.wait_ge(st_new, 17 * (p + 1))
                    for j in range(2):
                        mm = mmul(ps[:, 4 + j, :], self.const("pairsum"), y[:, j * HALF:(j + 1) * HALF], start=True, stop=True)
                    mm.then_inc(gn_mean, 1)
                    pe.wait_ge(gn_sq, p + 1)
                    for t in range(TT):
                        mm = mmul(ps[:, 6, 2 * t:2 * t + 2], sq[:, t * P:(t + 1) * P], self.const("heads"), start=True, stop=True)
                    mm.then_inc(gn_sum, 1)
                    pe.wait_ge(gn_rn, p + 1)
                    self.spread(small[:, 2, :], 0).then_inc(gn_bc, 1)

            @block.scalar
            def _(act):
                act.wait_ge(lora_in, 8 * 16)
                lora_ready_parts = (nc.scalar.activation(lora[0:HD, :], lora[0:HD, :], ACT.Tanh),
                                    nc.scalar.activation(gate0[:], gate0[:], ACT.Sigmoid))
                nc.scalar.activation(gate1[:], gate1[:], ACT.Sigmoid).then_inc(lora_ready, 1)
                for p in range(PAIRS):
                    act.wait_ge(z_done, p + 1)
                    if p:
                        act.wait_ge(pair_done, p)
                    nc.scalar.activation(cum[:], bank2(0), ACT.Sigmoid, bias=self.param("a_w0", p))
                    nc.scalar.activation(a[:], bank2(1), ACT.Sigmoid, bias=self.param("a_a0", p))
                    nc.scalar.activation(g[:], bank2(2), ACT.Copy).then_inc(z_used, 1)
                    act.wait_ge(kk_raw, p + 1)
                    nc.scalar.activation(sq[:], kk[:], ACT.Square).then_inc(kk_sq, 1)
                    act.wait_ge(cum_done, p + 1)
                    nc.scalar.activation(dec_upto, chunks(inv[:]), ACT.Exp, scale=-DECAY)
                    nc.scalar.activation(inv[:], inv[:], ACT.Exp, scale=DECAY).then_inc(dec_done, 1)
                    for n in (1, 3):
                        act.wait_ge(turned, 4 * p + n + 1)
                        nc.scalar.activation(flat(tok[n][:]), bank2(n), ACT.Copy).then_inc(turned_a, 1)
                    for q in range(STEPS):
                        st = STEPS * p + q
                        for l in range(1, LEVELS + 1):
                            n = st * LEVELS + l - 1
                            act.wait_ge(u_done, n + 1)
                            act.wait_ge(xt_done, n)
                            nc.scalar.activation(flat(um[:]), ps[:, 0, :], ACT.Copy).then_inc(u_copied, 1)
                        act.wait_ge(mv_done, st + 1)
                        nc.scalar.activation(flat(mv[:]), ps[:, 0, 0:4 * HD], ACT.Copy).then_inc(mv_copied, 1)
                        act.wait_ge(bars_done, st + 1)
                        nc.scalar.activation(flat(abar[:]), ps[:, 6, 0:2 * P], ACT.Copy)
                        nc.scalar.activation(flat(vbar[:]), ps[:, 7, 0:4 * HD], ACT.Copy).then_inc(bars_copied, 1)
                        act.wait_ge(y_done, st + 1)
                        nc.scalar.activation(y[:, q * 2 * P:(q + 1) * 2 * P], ps[:, 4, 0:2 * P], ACT.Copy).then_inc(y_copied, 1)
                    act.wait_ge(gn_centred, p + 1)
                    nc.scalar.activation(sq[:], y[:], ACT.Square).then_inc(gn_sq, 1)

            @block.gpsimd
            def _(pool):
                for p in range(PAIRS):
                    pool.wait_ge(kk_ms, p + 1)
                    nc.gpsimd.tensor_tensor(small[:, 2, :], small[:, 1, :], self.const("minus_half"), ALU.pow).then_inc(kk_rn, 1)
                    for q in range(STEPS):
                        st = STEPS * p + q
                        pool.wait_ge(masked, 2 * st + 2)
                        for l in range(1, LEVELS + 1):
                            n = st * LEVELS + l - 1
                            if n >= 2:
                                pool.wait_ge(u_done, n - 1)
                            nc.gpsimd.tensor_tensor(
                                join[:, n % 2].rearrange("p (h t) c -> p h t c", h=2), mb[:, :, 0], self.mask4(f"join{l}"), ALU.mult).then_inc(join_done, 1)
                    pool.wait_ge(gn_ms, p + 1)
                    nc.gpsimd.tensor_tensor(small[:, 2, :], small[:, 1, :], self.const("minus_half"), ALU.pow).then_inc(gn_rn, 1)

            @block.vector
            def _(dve):
                link = self.linker(dve, self.vector_link)
                L = link
                tt, stt, ts = nc.vector.tensor_tensor, nc.vector.scalar_tensor_tensor, nc.vector.tensor_scalar
                nc.vector.memset(dec[:, :, 0:1], 1.0)
                ka, kb = self.place["before"][0], self.place["upto"][1]
                kinds_mask = self.k[:, ka:kb].rearrange("p (a t c) -> p a t c", a=2, t=1).broadcast_to([P, 2, 2, P])
                L(nc.vector.memset(state[:, 0, :], 0.0))
                for p in range(PAIRS):
                    dve.wait_ge(u_in, 48 * (p + 1))
                    if p:
                        dve.wait_ge(y_done, STEPS * p)
                    ts(kk[:], k[:], self.param("a_k_k", p), None, ALU.mult).then_inc(kk_raw, 1)
                    dve.wait_ge(z_used, p + 1)
                    nc.vector.tensor_tensor_scan(inv[:], keep[:], cum[:], 0.0, ALU.mult, ALU.add).then_inc(cum_done, 1)
                    L(ts(tmp[:], a[:], 1.0, self.param("a_k_a", p), ALU.subtract, ALU.mult))
                    L(stt(out=k[:], in0=tmp[:], scalar=1.0, in1=k[:], op0=ALU.add, op1=ALU.mult))
                    stt(out=tmp[:], in0=r[:], scalar=self.param("a_r_k", p), in1=k[:], op0=ALU.mult, op1=ALU.mult).then_inc(rk_done, 1)
                    dve.wait_ge(kk_sum, p + 1)
                    ts(small[:, 1, :], ps[:, 6, 0:16], 1e-24, None, ALU.max).then_inc(kk_ms, 1)
                    dve.wait_ge(kk_bc, p + 1)
                    L(tt(kk[:], kk[:], bank2(0), ALU.mult))
                    L(tt(a[:], kk[:], a[:], ALU.mult))
                    dve.wait_ge(dec_done, p + 1)
                    tt(a[:], a[:], inv[:], ALU.mult)
                    tt(k[:], k[:], inv[:], ALU.mult)
                    tt(chunks(r[:]), chunks(r[:]), dec_upto, ALU.mult)
                    stt(out=chunks(kk[:]), in0=chunks(kk[:]), scalar=-1.0, in1=dec_before, op0=ALU.mult, op1=ALU.mult).then_inc(feat, 1)
                    dve.wait_ge(rk_sum, p + 1)
                    tt(bonus[:], v[:], bank2(1), ALU.mult).then_inc(bonus_done, 1)
                    for n in (0, 2):
                        dve.wait_ge(turned, 4 * p + n + 1)
                        nc.vector.tensor_copy(flat(tok[n][:]), bank2(n)).then_inc(turned_d, 1)
                    nc.vector.memset(state[:, 0, :], 0.0).then_inc(st_new, 1)
                    for q in range(STEPS):
                        st = STEPS * p + q
                        dve.wait_ge(scored, st + 1)
                        b4 = lambda n: ps[:, n, :].rearrange("p (i c) -> p i c", i=4)
                        quad = lambda n, kinds: ps[:, n, 0:kinds * 2 * P].rearrange("p (a t c) -> p a t c", a=kinds, t=2)
                        for h in range(2):
                            tt(mb[:, h], quad(3 * h, 2), kinds_mask, ALU.mult)
                            tt(mk[:, h], quad(3 * h + 1, 2), kinds_mask, ALU.mult)
                            tt(mab[:, h], ps[:, 3 * h + 2, 0:2 * P].rearrange("p (t c) -> p t c", t=2),
                                           self.mask("pair0", 2), ALU.mult).then_inc(masked, 1)
                        dve.wait_ge(masked, 2 * st + 2)
                        four = lambda x: x.rearrange("p (h t) c -> p h t c", h=2)
                        L(tt(four(inv_t[:]), mb[:, :, 0], self.mask4("join0"), ALU.mult))
                        tt(four(inv_m[:]), mab[:], self.mask4("ident"), ALU.add)
                        tt(inv_t[:], inv_t[:], self.mask("ident", 4), ALU.add).then_inc(x0, 1)
                        for l in range(1, LEVELS + 1):
                            n = st * LEVELS + l
                            dve.wait_ge(xt_done, n)
                            if l < LEVELS:
                                tt(inv_m[:], inv_m[:], b4(6), ALU.add)
                            tt(inv_t[:], inv_t[:], b4(7), ALU.add).then_inc(xt_added, 1)
                        dve.wait_ge(bars_copied, st + 1)
                        for c in range(4):
                            n = 4 * st + c
                            t, b = c // 2, slice((c % 2) * C, (c % 2 + 1) * C)
                            ci = 4 * q + c
                            dve.wait_ge(sa_done, n + 1)
                            tt(sa[b, t, :].rearrange("p (h c) -> p h c", h=2), ps[b, 1:3, c * HD:(c + 1) * HD],
                                             vbar[b].rearrange("p (h t) c -> p h t c", h=2)[:, :, t, :], ALU.add).then_inc(sa_added, 1)
                            dve.wait_ge(st_done, n + 1)
                            L(tt(stmp[:], ps[:, 3, c * HD:(c + 1) * HD], state[:, ci, :], ALU.add))
                            ts(state[:, ci + 1, :], stmp[:], dec[:, ci, C:C + 1], None, ALU.mult).then_inc(st_new, 1)
                    dve.wait_ge(gn_mean, p + 1)
                    stt(out=y[:], in0=bank2(2), scalar=-1.0 / HD, in1=y[:], op0=ALU.mult, op1=ALU.add).then_inc(gn_centred, 1)
                    dve.wait_ge(gn_sum, p + 1)
                    ts(small[:, 1, :], ps[:, 6, 0:16], 1.0 / HD, GN_EPS, ALU.mult, ALU.add).then_inc(gn_ms, 1)
                    dve.wait_ge(gn_bc, p + 1)
                    L(tt(y[:], y[:], bank2(0), ALU.mult))
                    L(ts(y[:], y[:], self.param("a_lnx_g", p), self.param("a_lnx_b", p), ALU.mult, ALU.add))
                    L(tt(y[:], y[:], bonus[:], ALU.add))
                    tt(self.X[:, p, :], y[:], g[:], ALU.mult).then_inc(pair_done, 1)
        self.phase_over()

    def spread(self, cols, slot, tiles=TT):
        nc, ps = self.nc, self.ps
        for t in range(tiles):
            for h in range(2):
                mm = nc.tensor.matmul(ps[h * HD:(h + 1) * HD, 2 * slot + t // 4, (t % 4) * P:(t % 4 + 1) * P],
                                      cols[:, 2 * t + h:2 * t + h + 1].broadcast_to([P, HD]), self.const("ident"), start=True, stop=True)
        return mm


    def phase_fox(self):
        pairs = [dict(q=p, k=self.kv_dram[p], v=self.kv_dram[6 + p], gate=6 + p, out=p) for p in range(PAIRS)]
        self.phase_attention("fox", pairs, T, "b_q_gain", "k_gain", causal=True)

    def phase_mem_attention(self, layer, q_at):
        pairs = [dict(q=q_at + p, k=self.memk_dram[2 * layer + p], v=self.memv_dram[2 * layer + p], gate=None, out=PAIRS + p)
                 for p in range(MEM_PAIRS)]
        self.phase_attention(f"mem{layer}", pairs, M, f"mem_q_gain{layer}", f"mem_k_gain{layer}", causal=False)

    def phase_attention(self, name, pairs, width, q_gain, k_gain, causal):
        nc, ps = self.nc, self.ps
        with ExitStack() as ctx:
            sb = lambda n, shape: self.sb(ctx, f"{name}_{n}", shape)
            self.phase_begins(name)
            sg = self.sem
            q, k, v = sb("q", [P, 2, T]), sb("k", [P, 2, width]), sb("v", [P, 2, width // P, P])
            gate = sb("gate", [P, 2, T])
            negc = sb("negc", [P, 2, 2, T if causal else 1])
            sq = sb("sq", [P, 2, T])
            small = sb("small", [P, 2, 3, 16])
            prob = sb("prob", [P, 2, width])
            prob_t = sb("prob_t", [P, 2, width // P, P])
            stat = sb("stat", [P, 4, 4])
            o = sb("o", [P, 2, P])
            loaded, squared, summed, ms, rn, spread, qk = (sg("pair_" + n) for n in ("loaded", "squared", "summed", "ms", "rn", "spread", "qk"))
            scored, maxed, exped, turned, pt_d, pt_a, pv, o_norm, ot, stored = (
                sg(n) for n in ("scored", "maxed", "exped", "turned", "pt_d", "pt_a", "pv", "o_norm", "ot", "stored"))
            gated = sg("gated")
            block = ctx.enter_context(nc.Block())
            N = len(pairs)
            units = [(t, h) for t in range(TT) for h in range(2)]
            U = len(units)
            keys = lambda t: (t + 1) * P if causal else width
            LAG = 4
            second_bank = lambda n: sum(1 for m in range(n) if keys(units[m % U][0]) > HALF)
            loads = 5 if causal else 3
            hs = (slice(0, HD), slice(HD, P))

            @block.sync
            def _(sp):
                for p, pr in enumerate(pairs):
                    b = p % 2
                    if p >= 2:
                        sp.wait_ge(stored, TT * (p - 1))
                    n = 0
                    sp.dma_start(q[:, b, :], self.u_dram[pr["q"]]).then_inc(loaded, 16)
                    sp.dma_start(k[:, b, :], pr["k"]).then_inc(loaded, 16)
                    sp.dma_start(v[:, b].rearrange("p a c -> p (a c)"), pr["v"]).then_inc(loaded, 16)
                    if causal:
                        sp.dma_start(gate[:, b, :], self.u_dram[pr["gate"]]).then_inc(loaded, 16)
                        sp.dma_start(negc[:, b, :, :], self.negc_dram[2 * p:2 * p + 2, :].partition_broadcast(P)).then_inc(loaded, 16)
                    sp.wait_ge(loaded, 16 * loads * (p + 1))

            @block.tensor
            def _(pe):
                mmul = nc.tensor.matmul
                for p in range(N):
                    b = p % 2
                    for n, w in ((0, T), (1, width)):
                        pe.wait_ge(squared, 2 * p + n + 1)
                        if p:
                            pe.wait_ge(stored, TT * p)
                        for t in range(w // P):
                            mm = mmul(ps[:, 6 + n, 2 * t:2 * t + 2], sq[:, n, t * P:(t + 1) * P], self.const("heads"), start=True, stop=True)
                        mm.then_inc(summed, 1)
                    for n, w in ((0, T), (1, width)):
                        pe.wait_ge(rn, 2 * p + n + 1)
                        self.spread(small[:, n, 2, :], n, w // P).then_inc(spread, 1)
                    pe.wait_ge(qk, 2 * (p + 1))
                    for n in range(U + LAG):
                        if n < U:
                            t, h = units[n]
                            g = p * U + n
                            if n >= 2:
                                pe.wait_ge((maxed if causal else exped), g - 1)
                            nk = keys(t)
                            for c in range(0, nk, HALF):
                                w = min(HALF, nk - c)
                                last = c + w == nk
                                mm = mmul(ps[:, 2 * (n % 2) + c // HALF, 0:w], q[hs[h], b, t * P:(t + 1) * P], k[hs[h], b, c:c + w],
                                          start=True, stop=not (causal and last))
                                if causal and last:
                                    mm = mmul(ps[:, 2 * (n % 2) + c // HALF, w - P:w], self.const("ident"), self.const("future"),
                                              start=False, stop=True)
                            mm.then_inc(scored, 1)
                        m = n - 1
                        if 0 <= m < U:
                            g = p * U + m
                            t, h = units[m]
                            pe.wait_ge(exped, g + 1)
                            pe.wait_ge(pt_d, g)
                            pe.wait_ge(pt_a, second_bank(g))
                            for j in range(keys(t) // P):
                                mm = nc.tensor.transpose(ps[:, 4 + j // 4, (j % 4) * P:(j % 4 + 1) * P], prob[:, m % 2, j * P:(j + 1) * P],
                                                         self.const("ident"))
                            mm.then_inc(turned, 1)
                        m = n - 2
                        if 0 <= m < U:
                            g = p * U + m
                            t, h = units[m]
                            pe.wait_ge(pt_d, g + 1)
                            pe.wait_ge(pt_a, second_bank(g + 1))
                            pe.wait_ge(o_norm, g)
                            nj = keys(t) // P
                            for j in range(nj):
                                mm = mmul(ps[:, 6, 0:HD], prob_t[:, m % 2, j, :], v[:, b, j, hs[h]], start=(j == 0), stop=(j == nj - 1))
                            mm.then_inc(pv, 1)
                        m = n - 3
                        if 0 <= m < U and m % 2:
                            g = p * U + m
                            pe.wait_ge(o_norm, g + 1)
                            pe.wait_ge(stored, (g + 1) // 2 - 1)
                            nc.tensor.transpose(ps[:, 7, 0:P], o[:, (m // 2) % 2, :], self.const("ident")).then_inc(ot, 1)

            @block.scalar
            def _(act):
                for p in range(N):
                    b = p % 2
                    act.wait_ge(loaded, 16 * loads * (p + 1))
                    nc.scalar.activation(sq[:, 0, :], q[:, b, :], ACT.Square).then_inc(squared, 1)
                    nc.scalar.activation(sq[:, 1, 0:width], k[:, b, :], ACT.Square).then_inc(squared, 1)
                    if causal:
                        nc.scalar.activation(gate[:, b, :], gate[:, b, :], ACT.Sigmoid).then_inc(gated, 1)
                    for n in range(U + LAG):
                        if n < U:
                            t, h = units[n]
                            g = p * U + n
                            nk = keys(t)
                            act.wait_ge(maxed, g + 1)
                            src = prob[:, n % 2, 0:nk] if causal else ps[:, 2 * (n % 2), 0:nk]
                            if n >= 2 and not causal:
                                act.wait_ge(turned, g - 1)
                            if n >= 4:
                                act.wait_ge(o_norm, g - 3)
                            nc.scalar.activation(prob[:, n % 2, 0:nk], src, ACT.Exp, bias=stat[:, n % 4, 1:2],
                                                            accum_out=stat[:, n % 4, 2:3]).then_inc(exped, 1)
                        m = n - 1
                        if 0 <= m < U and keys(units[m][0]) > HALF:
                            g = p * U + m
                            nj = keys(units[m][0]) // P
                            act.wait_ge(turned, g + 1)
                            if g >= 2:
                                act.wait_ge(pv, g - 1)
                            nc.scalar.activation(prob_t[:, m % 2, 4:nj, :].rearrange("p a c -> p (a c)"), ps[:, 5, 0:(nj - 4) * P], ACT.Copy).then_inc(pt_a, 1)

            @block.gpsimd
            def _(pool):
                for p in range(N):
                    for n, w in ((0, T), (1, width)):
                        pool.wait_ge(ms, 2 * p + n + 1)
                        nc.gpsimd.tensor_tensor(small[:, n, 2, 0:w // HD], small[:, n, 1, 0:w // HD],
                                                        self.const("minus_half")[:, 0:w // HD], ALU.pow).then_inc(rn, 1)

            @block.vector
            def _(dve):
                link = self.linker(dve, self.vector_link)
                for p, pr in enumerate(pairs):
                    b = p % 2
                    dve.wait_ge(loaded, 16 * loads * (p + 1))
                    for n, w in ((0, T), (1, width)):
                        dve.wait_ge(summed, 2 * p + n + 1)
                        nc.vector.tensor_scalar(small[:, n, 1, 0:w // HD], ps[:, 6 + n, 0:w // HD], 1.0 / HD, RMS_EPS, ALU.mult, ALU.add).then_inc(ms, 1)
                    for n, (x, w, gn) in enumerate(((q, T, q_gain), (k, width, k_gain))):
                        dve.wait_ge(spread, 2 * p + n + 1)
                        i = nc.vector.scalar_tensor_tensor(out=x[:, b, :], in0=x[:, b, :], scalar=self.param(gn), in1=self.bank2(n)[:, 0:w],
                                                           op0=ALU.mult, op1=ALU.mult)
                        if n == 0:
                            link(i)
                            i = nc.vector.tensor_scalar(x[:, b, :], x[:, b, :], SCALE, None, ALU.mult)
                        i.then_inc(qk, 1)
                    if causal:
                        dve.wait_ge(gated, p + 1)
                    for n in range(U + LAG):
                        if n < U:
                            t, h = units[n]
                            g = p * U + n
                            nk = keys(t)
                            dve.wait_ge(scored, g + 1)
                            s4 = stat[:, n % 4]
                            if causal:
                                if n >= 2:
                                    dve.wait_ge(turned, g - 1)
                                src = self.bank2(n % 2)[:, 0:nk]
                                link(nc.vector.tensor_tensor_reduce(
                                    out=prob[:, n % 2, 0:nk], in0=src, in1=negc[:, b, h, 0:nk], scale=1.0, scalar=-3e38,
                                    op0=ALU.add, op1=ALU.max, accum_out=s4[:, 0:1]))
                            else:
                                link(nc.vector.tensor_reduce(s4[:, 0:1], ps[:, 2 * (n % 2), 0:nk], AX_X, ALU.max))
                            nc.vector.tensor_scalar(s4[:, 1:2], s4[:, 0:1], -1.0, None, ALU.mult).then_inc(maxed, 1)
                        m = n - 1
                        if 0 <= m < U:
                            g = p * U + m
                            nj = min(4, keys(units[m][0]) // P)
                            dve.wait_ge(turned, g + 1)
                            if g >= 2:
                                dve.wait_ge(pv, g - 1)
                            nc.vector.tensor_copy(prob_t[:, m % 2, 0:nj, :].rearrange("p a c -> p (a c)"), ps[:, 4, 0:nj * P]).then_inc(pt_d, 1)
                        m = n - 2
                        if 0 <= m < U:
                            g = p * U + m
                            t, h = units[m]
                            s4 = stat[:, m % 4]
                            link(nc.vector.reciprocal(s4[:, 3:4], s4[:, 2:3]))
                            dve.wait_ge(pv, g + 1)
                            if h == 0 and g >= 4:
                                dve.wait_ge(ot, g // 2 - 1)
                            nc.vector.tensor_scalar(o[:, (m // 2) % 2, hs[h]], ps[:, 6, 0:HD], s4[:, 3:4], None, ALU.mult).then_inc(o_norm, 1)
                        m = n - 3
                        if 0 <= m < U and m % 2:
                            g = p * U + m
                            t = units[m][0]
                            dve.wait_ge(ot, (g + 1) // 2)
                            dst = self.X[:, pr["out"], t * P:(t + 1) * P]
                            if causal:
                                nc.vector.tensor_tensor(dst, ps[:, 7, 0:P], gate[:, b, t * P:(t + 1) * P], ALU.mult).then_inc(stored, 1)
                            else:
                                nc.vector.tensor_copy(dst, ps[:, 7, 0:P]).then_inc(stored, 1)
        self.phase_over()


    def phase_out_and_ffn(self, l):
        nc, ps = self.nc, self.ps
        with ExitStack() as scope:
            self.alloc_h(scope, f"f{l}")
            s0 = self.first[f"out{l}"]
            split_from, split_to = self.split_upto, s0 + KT + RING
            with ExitStack() as ctx:
                self.phase_begins(f"out{l}")
                block = ctx.enter_context(nc.Block())

                @block.sync
                def _(sp):
                    for i in range(KT):
                        self.load_strip(sp, s0 + i + RING)
                        if i == 0:
                            sp.wait_ge(self.h_hi, KT)
                            sp.wait_ge(self.h_lo, KT)
                            sp.dma_start(self.X[:], self.x_dram).then_inc(self.loaded, 16)
                    sp.wait_ge(self.loaded, 16)

                @block.gpsimd
                def _(pool):
                    for s in range(split_from, split_to):
                        self.split_strip(pool, s)

                @block.scalar
                def _(act):
                    for k in range(KT):
                        nc.scalar.activation(self.hh[:, k, :], self.X[:, k, :], ACT.Copy).then_inc(self.h_hi, 1)

                @block.vector
                def _(dve):
                    link = self.linker(dve, self.vector_link)
                    for k in range(KT):
                        dve.wait_ge(self.h_hi, k + 1)
                        nc.vector.tensor_tensor(self.hl[:, k, :], self.X[:, k, :], self.hh[:, k, :].bitcast(F32), ALU.subtract).then_inc(self.h_lo, 1)
                    dve.wait_ge(self.loaded, 16)
                    for i in range(KT):
                        dve.wait_ge(self.strip_done, s0 + i + 1)
                        nc.vector.tensor_tensor(self.X[:, i, :], self.X[:, i, :], self.bank2(i % 3), ALU.add).then_inc(self.psum_free, 1)

                @block.tensor
                def _(pe):
                    for i in range(KT):
                        if i >= 3:
                            pe.wait_ge(self.psum_free, i - 2)
                        self.gemm_strip(pe, s0 + i, i % 3, self.hh, self.hl, "fm", T,
                                        (lambda k: pe.wait_ge(self.h_lo, k + 1)) if i == 0 else None)
            self.split_upto = split_to
            self.phase_over()
            self.phase_ffn(scope, l)

    def phase_ffn(self, scope, l):
        nc, ps = self.nc, self.ps
        GM = max(FF_GROUPS)
        s0 = self.first[f"up{l}0"]
        plan, f = [], 0
        for g, n in enumerate(FF_GROUPS):
            for j in range(n):
                plan += [("gate", f, j), ("up", f, j)]
                f += 1
            plan += [("down", c, (n, f)) for c in range(KT)]
        with ExitStack() as ctx:
            ah = self.sb(ctx, f"act_hi{l}", [P, GM, T], F32R)
            al = self.sb(ctx, f"act_lo{l}", [P, GM, T], F32R)
            silu = self.sb(ctx, f"silu{l}", [P, 2, T])
            full = self.sb(ctx, f"full_f{l}", [P, 2, T])
            small = self.sb(ctx, f"small_f{l}", [P, 3, 16])
            self.phase_begins(f"ffn{l}")
            sg = self.sem
            silu_done, act_hi, act_lo = sg("silu"), sg("act_hi"), sg("act_lo")
            x_saved = self.sem("x_saved")
            block = ctx.enter_context(nc.Block())
            split_from = self.split_upto
            split_to = min(s0 + len(plan) + RING, len(self.strips))

            @block.sync
            def _(sp):
                for s in range(split_from, split_to):
                    self.load_strip(sp, s)
                if l == 0:
                    sp.wait_ge(self.psum_free, len(plan))
                    sp.dma_start(self.x_dram, self.X[:]).then_inc(x_saved, 16)
                    sp.wait_ge(x_saved, 16)

            @block.gpsimd
            def _(pool):
                self.norm_pool(pool, T, small)
                for s in range(split_from, split_to):
                    self.split_strip(pool, s)

            @block.scalar
            def _(act):
                self.norm_act(act, lambda k: self.X[:, k, :], T, silu)
                for k in range(KT):
                    act.wait_ge(self.h_full, k + 1)
                    nc.scalar.activation(self.hh[:, k, :], full[:, k % 2, :], ACT.Copy).then_inc(self.h_hi, 1)
                for i, (kind, f, j) in enumerate(plan):
                    if kind == "gate":
                        act.wait_ge(self.strip_done, s0 + i + 1)
                        if f == 0:
                            act.wait_ge(self.sums, KT)
                        if f >= 2:
                            act.wait_ge(act_hi, f - 1)
                        nc.scalar.activation(silu[:, f % 2, :], self.bank2(i % 3), ACT.Silu).then_inc(silu_done, 1)
                    elif kind == "up":
                        act.wait_ge(self.psum_free, i + 1)
                        nc.scalar.activation(ah[:, j, :], full[:, f % 2, :], ACT.Copy).then_inc(act_hi, 1)

            @block.vector
            def _(dve):
                link = self.linker(dve, self.vector_link)
                self.norm_dve_sums(dve, link, T, small, 4)
                dve.wait_ge(self.spread_done, 1)
                for k in range(KT):
                    if k >= 2:
                        dve.wait_ge(self.h_lo, k - 1)
                    nc.vector.scalar_tensor_tensor(
                        out=full[:, k % 2, :], in0=self.X[:, k, :], scalar=self.param(f"ffn_norm{l}", k),
                        in1=self.bank2(3), op0=ALU.mult, op1=ALU.mult).then_inc(self.h_full, 1)
                    dve.wait_ge(self.h_full, k + 1)
                    dve.wait_ge(self.h_hi, k + 1)
                    nc.vector.tensor_tensor(self.hl[:, k, :], full[:, k % 2, :], self.hh[:, k, :].bitcast(F32), ALU.subtract).then_inc(self.h_lo, 1)
                dve.wait_ge(self.h_lo, KT)
                for i, (kind, f, j) in enumerate(plan):
                    if kind == "up":
                        dve.wait_ge(silu_done, f + 1)
                        dve.wait_ge(self.strip_done, s0 + i + 1)
                        if f >= 2:
                            dve.wait_ge(act_lo, f - 1)
                        nc.vector.tensor_tensor(full[:, f % 2, :], silu[:, f % 2, :], self.bank2(i % 3), ALU.mult).then_inc(self.psum_free, 2)
                        dve.wait_ge(self.psum_free, i + 1)
                        dve.wait_ge(act_hi, f + 1)
                        nc.vector.tensor_tensor(al[:, j, :], full[:, f % 2, :], ah[:, j, :].bitcast(F32), ALU.subtract).then_inc(act_lo, 1)
                    elif kind == "down":
                        dve.wait_ge(self.strip_done, s0 + i + 1)
                        if j[1] != FF_GROUPS[0]:
                            dve.wait_ge(self.psum_free, i)
                        nc.vector.tensor_tensor(self.X[:, f, :], self.X[:, f, :], self.bank2(i % 3), ALU.add).then_inc(self.psum_free, 1)

            @block.tensor
            def _(pe):
                self.norm_pe(pe, T, silu, small[:, 2], 4, 6)
                for i, (kind, f, j) in enumerate(plan):
                    if i >= 3:
                        pe.wait_ge(self.psum_free, i - 2)
                    if kind != "down":
                        self.gemm_strip(pe, s0 + i, i % 3, self.hh, self.hl, "fm", T,
                                        (lambda k: pe.wait_ge(self.h_lo, k + 1)) if i == 0 else None)
                    else:
                        n, upto = j
                        self.gemm_strip(pe, s0 + i, i % 3, ah, al, "fm", T,
                                        (lambda k: pe.wait_ge(act_lo, upto - n + k + 1)) if f == 0 else None)
        self.split_upto = split_to
        self.phase_over()


    def phase_store(self):
        nc, ps = self.nc, self.ps
        with ExitStack() as ctx:
            xo = self.sb(ctx, "x_out", [P, TT, D])
            self.phase_begins("store")
            turned, even_out, odd_out = (self.sem(n) for n in ("turned", "even_out", "odd_out"))
            out_stored = self.out_stored
            block = ctx.enter_context(nc.Block())

            @block.tensor
            def _(pe):
                for t in range(TT):
                    if t >= 4:
                        pe.wait_ge((even_out if t % 2 == 0 else odd_out), (t - 4) // 2 + 1)
                    for k in range(KT):
                        mm = nc.tensor.transpose(ps[:, 2 * (t % 4) + k // 4, (k % 4) * P:(k % 4 + 1) * P],
                                                 self.X[:, k, t * P:(t + 1) * P], self.const("ident"))
                    mm.then_inc(turned, 1)

            @block.vector
            def _(dve):
                link = self.linker(dve, self.vector_link)
                for t in range(0, TT, 2):
                    dve.wait_ge(turned, t + 1)
                    nc.vector.tensor_copy(xo[:, t, :], self.bank2(t % 4)).then_inc(even_out, 1)

            @block.scalar
            def _(act):
                for t in range(1, TT, 2):
                    act.wait_ge(turned, t + 1)
                    nc.scalar.activation(xo[:, t, :], self.bank2(t % 4), ACT.Copy).then_inc(odd_out, 1)

            @block.sync
            def _(sp):
                for t in range(TT):
                    sp.wait_ge((even_out if t % 2 == 0 else odd_out), t // 2 + 1)
                    sp.dma_start(self.out[0, t * P:(t + 1) * P, :], xo[:, t, :]).then_inc(out_stored, 16)
                sp.wait_ge(out_stored, 16 * TT)


_INS = ["x", "mem", "mix_norm", "w_out", "mem_norm", "w_mem_kv", "mem_q_gain", "mem_k_gain", "ffn_norm", "w_gate_up", "w_down",
        "a_w_in", "a_mu", "a_w0", "a_w_up", "a_a0", "a_a_up", "a_g_up", "a_k_k", "a_k_a", "a_r_k", "a_lnx_g", "a_lnx_b",
        "kv_norm", "w_kv", "b_f", "k_gain", "b_w_in", "b_q_gain"]


def kernel(**inputs):
    import concourse.bacc as bacc
    from concourse.bass_utils import run_bass_kernel_spmd

    nc = bacc.Bacc("TRN2", target_bir_lowering=False, num_devices=1)
    consts, place = shape_constants()
    arrays, aps = {}, {}
    for name, a in [(n, inputs[n]) for n in _INS] + [("consts", consts), ("chunk_starts", chunk_starts())]:
        a = np.ascontiguousarray(a)
        arrays[f"in_{name}"] = a
        aps[name] = nc.dram_tensor(f"in_{name}", a.shape, F32, kind="ExternalInput").ap()
    out = nc.dram_tensor("out_x", (1, T, D), F32, kind="ExternalOutput").ap()
    program = Program(nc, aps, out)
    program.place = place
    program.build()
    result = run_bass_kernel_spmd(nc, [arrays], core_ids=[0])
    return result.results[0]["out_x"]
```

```python
from contextlib import ExitStack
import math

import numpy as np
import concourse.bass as bass
from concourse import mybir

ALU = mybir.AluOpType
ACT = mybir.ActivationFunctionType
F32 = mybir.dt.float32
F32R = mybir.dt.float32r
AX_X = mybir.AxisListType.X

P = 128
D = 1024
KT = D // P
T = 1024
TT = T // P
HALF = 512
M = 256
HD = 64
D_MAIN = 768
PAIRS = D_MAIN // P
MEM_PAIRS = 2
D_FF = 2816
FT = D_FF // P
FF_GROUPS = [6, 6, 5, 5]
D_SHIFT = 2592
C = 64
RMS_EPS = 1e-6
GN_EPS = 64e-5
DECAY = math.exp(-0.5)
SCALE = HD ** -0.5
RING = 3
LEVELS = 5


def shape_constants():
    i = np.arange(P)
    r, c = i[:, None], i[None, :]
    same = (r // C) == (c // C)
    cols = {
        "ident": (r == c),
        "before": same & (r < c),
        "upto": same & (r <= c),
        "pairsum": (r // HD) == (c // HD),
        "pair0": (r == c + 1) & (r % 2 == 1),
    }
    for l in range(LEVELS + 1):
        b = 1 << l
        cols[f"join{l}"] = ((c // b) % 2 == 1) & ((r // b) == (c // b) - 1)
    out = {k: v.astype(np.float32) for k, v in cols.items()}
    out["future"] = np.where(c > r, np.float32(-1e30), np.float32(0))
    out["heads"] = np.stack([(i < HD), (i >= HD)], 1).astype(np.float32)
    out["ones"] = np.ones((P, 1), np.float32)
    out["minus_half"] = np.full((P, 16), -0.5, np.float32)
    place, at = {}, 0
    for k, v in out.items():
        place[k] = (at, at + v.shape[1])
        at += v.shape[1]
    return np.concatenate(list(out.values()), 1), place


def chunk_starts():
    keep = np.ones((P, T), np.float32)
    keep[:, ::C] = 0.0
    return keep


class Program:
    def __init__(self, nc, ins, out):
        self.nc, self.ins, self.out = nc, ins, out
        self.cleared = []
        self.taken = []
        self.ctx = ExitStack()

    def sem(self, name):
        s = self.nc.alloc_semaphore(f"{self.phase}_{name}")
        self.taken.append(s)
        return s

    def phase_begins(self, name):
        self.phase = name
        self.loaded = self.sem("loaded")
        self.squared = self.sem("squared")
        self.sums = self.sem("sums")
        self.mean_sq = self.sem("mean_sq")
        self.rstd = self.sem("rstd")
        self.spread_done = self.sem("spread")
        self.h_full = self.sem("h_full")
        self.h_hi = self.sem("h_hi")
        self.h_lo = self.sem("h_lo")
        self.psum_free = self.sem("psum_free")
        self.vector_link = self.sem("vector_link")

    def phase_over(self):
        numbers = sorted(s.num for s in self.taken)
        first = 0
        for i in range(1, len(numbers) + 1):
            if i == len(numbers) or numbers[i] != numbers[i - 1] + 1:
                self.nc.gpsimd.sem_clear(range(numbers[first], numbers[i - 1] + 1))
                first = i
        for s in self.cleared:
            self.nc.release_semaphore(s)
        self.cleared, self.taken = self.taken, []

    def linker(self, engine, semaphore):
        done = [0]

        def link(instruction):
            done[0] += 1
            instruction.then_inc(semaphore, 1)
            engine.wait_ge(semaphore, done[0])
        return link

    def sb(self, ctx, name, shape, dt=F32):
        return ctx.enter_context(self.nc.sbuf_tensor(name, shape, dt))


    def strip(self, w, row0, tiles, col0, cols=P):
        return (w[row0:row0 + tiles * P, col0:col0 + cols].rearrange("(k p) c -> p k c", p=P), tiles, cols)

    def list_strips(self):
        i = self.ins
        s = self.strips = []
        self.first = {}

        def mark(name):
            self.first[name] = len(s)

        mark("in_a")
        self.a_plan = []
        mem = [("mem", l, c) for l in range(2) for c in range(4)]
        for c in range(23):
            if c < 21:
                s.append(self.strip(i["a_w_in"][0], 0, KT, c * P))
                self.a_plan.append(("shift", c))
            else:
                s.append(self.strip(i["a_w_in"][0], 0, KT, D_SHIFT + (c - 21) * P))
                self.a_plan.append(("plain", c))
            if c % 2 == 1 and mem:
                _, l, m = mem.pop(0)
                s.append(self.strip(i["w_mem_kv"][l], 0, KT, m * P))
                self.a_plan.append(("memk" if m < 2 else "memv", (l, m % 2)))
        for l in range(2):
            if l == 1:
                mark("kv")
                for c in range(12):
                    s.append(self.strip(i["w_kv"], 0, KT, c * P))
                s.append(self.strip(i["w_kv"], 0, KT, 2 * D_MAIN, 12))
                mark("in_b")
                for c in range(14):
                    s.append(self.strip(i["b_w_in"][0], 0, KT, c * P))
            mark(f"out{l}")
            for c in range(KT):
                s.append(self.strip(i["w_out"][l], 0, KT, c * P))
            f0 = 0
            for g, n in enumerate(FF_GROUPS):
                mark(f"up{l}{g}")
                for f in range(f0, f0 + n):
                    s.append(self.strip(i["w_gate_up"][l], 0, KT, f * P))
                    s.append(self.strip(i["w_gate_up"][l], 0, KT, D_FF + f * P))
                mark(f"down{l}{g}")
                for c in range(KT):
                    s.append(self.strip(i["w_down"][l], f0 * P, n, c * P))
                f0 += n
        self.raw_upto = 0
        self.split_upto = 0

    def load_strip(self, sp, s):
        if s >= len(self.strips):
            return
        src, tiles, cols = self.strips[s]
        if s >= RING:
            sp.wait_ge(self.w_lo, s - RING + 1)
        n = self.w_raw[s % RING]
        sp.dma_start(self.raw[:, s % RING, 0:tiles, 0:cols], src).then_inc(n, 16)

    def split_strip(self, pool, s):
        if s >= len(self.strips):
            return
        _, tiles, _ = self.strips[s]
        pool.wait_ge(self.w_raw[s % RING], 16 * (s // RING + 1))
        if s >= RING:
            pool.wait_ge(self.strip_done, s - RING + 1)
        r = s % RING
        raw = self.raw[:, r, 0:tiles, :]
        self.nc.gpsimd.tensor_copy(self.whi[:, r, 0:tiles, :], raw).then_inc(self.w_hi, 1)
        pool.wait_ge(self.w_hi, s + 1)
        self.nc.gpsimd.tensor_tensor(
            self.wlo[:, r, 0:tiles, :], raw, self.whi[:, r, 0:tiles, :].bitcast(F32), ALU.subtract).then_inc(self.w_lo, 1)

    def gemm_strip(self, pe, s, slot, hh, hl, kind="fm", width=T, before_k=None):
        nc = self.nc
        _, tiles, _ = self.strips[s]
        pe.wait_ge(self.w_lo, s + 1)
        r = s % RING
        wh, wl = self.whi[:, r], self.wlo[:, r]
        bank = self.ps
        mm = None
        if kind == "fm":
            n = min(width, HALF)
            parts = width // n
            for k in range(tiles):
                if before_k is not None:
                    before_k(k)
                for a, w in enumerate((wh, wl)):
                    for b, h in enumerate((hh, hl)[:2 - a]):
                        for j in range(parts):
                            mm = nc.tensor.matmul(bank[:, 2 * slot + j, 0:n], w[:, k, :], h[:, k, j * n:(j + 1) * n],
                                                  start=(k == 0 and a == 0 and b == 0), stop=(k == tiles - 1 and a == 1))
        else:
            for t in range(width // P):
                o = bank[:, 2 * slot + t // 4, (t % 4) * P:(t % 4 + 1) * P]
                for k in range(tiles):
                    for a, h in enumerate((hh, hl)):
                        for b, w in enumerate((wh, wl)[:2 - a]):
                            mm = nc.tensor.matmul(o, h[:, k, t * P:(t + 1) * P], w[:, k, :],
                                                  start=(k == 0 and a == 0 and b == 0), stop=(k == tiles - 1 and a == 1))
        mm.then_inc(self.strip_done, 1)

    def weights_for(self, last):
        return range(self.split_upto, min(last + RING, len(self.strips)))


    def build(self):
        nc, ctx = self.nc, self.ctx
        with ctx:
            ins = self.ins
            self.X = self.sb(ctx, "x_res", [P, KT, T])
            n = ins["consts"].shape[1]
            self.k = self.sb(ctx, "consts_sb", [P, n])
            self.params = self.sb(ctx, "params_sb", [P, 192])
            self.ps = ctx.enter_context(nc.psum_tensor("ps", [P, 8, HALF], F32))
            dram = lambda name, shape: nc.dram_tensor(name, shape, F32, kind="Internal").ap()
            self.x_dram = dram("x_dram", (P, KT, T))
            self.u_dram = dram("u_dram", (23, P, T))
            self.kv_dram = dram("kv_dram", (13, P, T))
            self.memk_dram = dram("memk_dram", (4, P, M))
            self.memv_dram = dram("memv_dram", (4, P, M))
            self.negc_dram = dram("negc_dram", (12, T))

            self.w_raw = [ctx.enter_context(nc.semaphore(f"w_raw{r}")) for r in range(RING)]
            self.w_hi = ctx.enter_context(nc.semaphore("w_hi"))
            self.w_lo = ctx.enter_context(nc.semaphore("w_lo"))
            self.strip_done = ctx.enter_context(nc.semaphore("strip_done"))
            self.params_in = ctx.enter_context(nc.semaphore("params_in"))
            self.out_stored = ctx.enter_context(nc.semaphore("out_stored"))
            self.list_strips()
            with ExitStack() as scope:
                self.alloc_ring(scope, "a")
                self.phase_load()
                self.alloc_h(scope, "a")
                self.phase_in_a(scope)
            self.phase_rwkv()
            self.alloc_ring(ctx, "b")
            self.phase_mem_attention(0, 21)
            self.phase_out_and_ffn(0)
            with ExitStack() as scope:
                self.alloc_h(scope, "b")
                self.phase_project(scope, "kv", 13, "kv_norm", 0)
                self.phase_project(scope, "in_b", 14, "mix_norm", 1)
            self.phase_fox()
            self.phase_mem_attention(1, 12)
            self.phase_out_and_ffn(1)
            self.phase_store()

    def alloc_ring(self, ctx, tag):
        self.raw = self.sb(ctx, f"w_raw_{tag}", [P, RING, KT, P])
        self.whi = self.sb(ctx, f"w_hi_{tag}", [P, RING, KT, P], F32R)
        self.wlo = self.sb(ctx, f"w_lo_{tag}", [P, RING, KT, P], F32R)

    def alloc_h(self, ctx, tag):
        self.hh = self.sb(ctx, f"h_hi_{tag}", [P, KT, T], F32R)
        self.hl = self.sb(ctx, f"h_lo_{tag}", [P, KT, T], F32R)

    def const(self, name):
        a, b = self.place[name]
        return self.k[:, a:b]

    def mask(self, name, n):
        return self.const(name).rearrange("p (a c) -> p a c", a=1).broadcast_to([P, n, P])

    def mask4(self, name):
        return self.const(name).rearrange("p (a b c) -> p a b c", a=1, b=1).broadcast_to([P, 2, 2, P])


    def phase_load(self):
        nc, ins, ps = self.nc, self.ins, self.ps
        with ExitStack() as scope:
            xin = self.sb(scope, "x_in", [P, TT, D])
            stage = self.sb(scope, "param_rows", [P, P])
            self.phase_begins("load")
            consts_in, x_saved, stage_zero = self.sem("consts_in"), self.sem("x_saved"), self.sem("stage_zero")
            turned, params_turned = self.sem("turned"), self.sem("params_turned")
            even_out, odd_out = self.sem("even_out"), self.sem("odd_out")
            block = scope.enter_context(nc.Block())

            self.place_params = {}
            loads = []
            at = 0

            def vec(name, ap, tiles):
                nonlocal at
                self.place_params[name] = at
                loads.append((at, tiles, slice(0, P), ap.rearrange("(n p) -> n p", p=P)))
                at += tiles

            for l in range(2):
                vec(f"mix_norm{l}", ins["mix_norm"][l], KT)
                vec(f"mem_norm{l}", ins["mem_norm"][l], KT)
                vec(f"ffn_norm{l}", ins["ffn_norm"][l], KT)
            vec("kv_norm0", ins["kv_norm"], KT)
            vec("mu", ins["a_mu"][0][0:20 * P], 20)
            for name in ("a_w0", "a_a0", "a_k_k", "a_k_a", "a_lnx_g", "a_lnx_b"):
                vec(name, ins[name][0], PAIRS)
            vec("a_r_k", ins["a_r_k"][0].rearrange("h d -> (h d)"), PAIRS)
            self.place_params["mu_last"] = at
            loads.append((at, 1, slice(0, 32), ins["a_mu"][0][20 * P:D_SHIFT].rearrange("(n p) -> n p", p=32)))
            mu_last = at
            at += 1
            for name, ap in (("mem_q_gain0", ins["mem_q_gain"][0]), ("mem_q_gain1", ins["mem_q_gain"][1]),
                             ("mem_k_gain0", ins["mem_k_gain"][0]), ("mem_k_gain1", ins["mem_k_gain"][1]),
                             ("k_gain", ins["k_gain"]), ("b_q_gain", ins["b_q_gain"][0])):
                self.place_params[name] = at
                for h in range(2):
                    loads.append((at, 1, slice(h * HD, (h + 1) * HD), ap.rearrange("(n p) -> n p", p=HD)))
                at += 1
            self.place_params["b_f"] = at
            loads.append((at, 1, slice(0, 12), ins["b_f"].rearrange("(n p) -> n p", p=12)))
            at += 1
            rows = at
            assert rows <= P
            self.place_params["one_minus_mu"] = at
            at += 21
            assert at <= 192

            @block.sync
            def _(sp):
                for t in range(TT):
                    sp.dma_start(xin[:, t, :], ins["x"][0, t * P:(t + 1) * P, :]).then_inc(self.loaded, 16)
                    sp.wait_ge(self.loaded, 16 * (t + 1))
                for s in range(RING):
                    self.load_strip(sp, s)
                sp.wait_ge(even_out, TT // 2)
                sp.wait_ge(odd_out, TT // 2)
                sp.dma_start(self.x_dram, self.X[:]).then_inc(x_saved, 16)
                sp.wait_ge(x_saved, 16)

            @block.scalar
            def _(act):
                act.dma_start(self.k[:], ins["consts"]).then_inc(consts_in, 16)
                for t in range(1, TT, 2):
                    act.wait_ge(turned, t + 1)
                    nc.scalar.activation(self.X[:, :, t * P:(t + 1) * P],
                                                         ps[:, 2 * (t % 4):2 * (t % 4) + 2, :].rearrange("p b (k c) -> p (b k) c", c=P), ACT.Copy).then_inc(odd_out, 1)

            @block.vector
            def _(dve):
                link = self.linker(dve, self.vector_link)
                nc.vector.memset(stage[:], 0.0).then_inc(stage_zero, 1)
                for t in range(0, TT, 2):
                    dve.wait_ge(turned, t + 1)
                    nc.vector.tensor_copy(self.X[:, :, t * P:(t + 1) * P],
                                                          ps[:, 2 * (t % 4):2 * (t % 4) + 2, :].rearrange("p b (k c) -> p (b k) c", c=P)).then_inc(even_out, 1)
                dve.wait_ge(params_turned, 1)
                link(nc.vector.tensor_copy(self.params[:, 0:rows], ps[:, 0, 0:rows]))
                o, m = self.place_params["one_minus_mu"], self.place_params["mu"]
                nc.vector.tensor_scalar(self.params[:, o:o + 20], self.params[:, m:m + 20], -1.0, 1.0, ALU.mult, ALU.add)
                nc.vector.tensor_scalar(self.params[:, o + 20:o + 21], self.params[:, mu_last:mu_last + 1],
                                                        -1.0, 1.0, ALU.mult, ALU.add).then_inc(stage_zero, 1)

            @block.tensor
            def _(pe):
                pe.wait_ge(consts_in, 16)
                for t in range(TT):
                    pe.wait_ge(self.loaded, 16 * (t + 1))
                    if t >= 4:
                        pe.wait_ge((even_out if t % 2 == 0 else odd_out), (t - 4) // 2 + 1)
                    for k in range(KT):
                        mm = nc.tensor.transpose(ps[:, 2 * (t % 4) + k // 4, (k % 4) * P:(k % 4 + 1) * P],
                                                 xin[:, t, k * P:(k + 1) * P], self.const("ident"))
                    mm.then_inc(turned, 1)
                pe.wait_ge(self.params_in, 16 * len(loads))
                pe.wait_ge(even_out, TT // 2 - 1)
                nc.tensor.transpose(ps[:, 0, 0:rows], stage[0:rows, :], self.const("ident")[0:rows, 0:rows]).then_inc(params_turned, 1)

            @block.gpsimd
            def _(pool):
                pool.wait_ge(stage_zero, 1)
                for row, n, cols, src in loads:
                    pool.dma_start(stage[row:row + n, cols], src).then_inc(self.params_in, 16)
                for s in range(RING):
                    self.split_strip(pool, s)

        self.split_upto = RING
        self.phase_over()

    def param(self, name, i=0):
        a = self.place_params[name] + i
        return self.params[:, a:a + 1]


    def norm_act(self, act, src, width, sq):
        for k in range(KT):
            if k >= 2:
                act.wait_ge(self.sums, k - 1)
            self.nc.scalar.activation(sq[:, k % 2, 0:width], src(k), ACT.Square).then_inc(self.squared, 1)

    def norm_pe(self, pe, width, sq, rs, slot_sum, slot_bc):
        nc, ps = self.nc, self.ps
        n = width // P
        for k in range(KT):
            pe.wait_ge(self.squared, k + 1)
            for t in range(n):
                mm = nc.tensor.matmul(ps[:, slot_sum, k * n + t:k * n + t + 1], sq[:, k % 2, t * P:(t + 1) * P],
                                      self.const("ones"), start=True, stop=True)
            mm.then_inc(self.sums, 1)
        pe.wait_ge(self.rstd, 1)
        for t in range(n):
            mm = nc.tensor.matmul(ps[:, slot_bc + t // 4, (t % 4) * P:(t % 4 + 1) * P],
                                  rs[:, t:t + 1].broadcast_to([P, P]), self.const("ident"), start=True, stop=True)
        mm.then_inc(self.spread_done, 1)

    def norm_dve_sums(self, dve, link, width, small, slot_sum):
        nc, ps = self.nc, self.ps
        n = width // P
        dve.wait_ge(self.sums, KT)
        link(nc.vector.tensor_reduce(small[:, 0, 0:n], ps[:, slot_sum, 0:KT * n].rearrange("p (k t) -> p t k", k=KT),
                                               AX_X, ALU.add))
        nc.vector.tensor_scalar(small[:, 1, 0:n], small[:, 0, 0:n], 1.0 / D, RMS_EPS, ALU.mult, ALU.add).then_inc(self.mean_sq, 1)

    def norm_pool(self, pool, width, small):
        n = width // P
        pool.wait_ge(self.mean_sq, 1)
        self.nc.gpsimd.tensor_tensor(small[:, 2, 0:n], small[:, 1, 0:n], self.const("minus_half")[:, 0:n], ALU.pow).then_inc(self.rstd, 1)


    def phase_in_a(self, scope):
        nc, ins, ps = self.nc, self.ins, self.ps
        plan = self.a_plan
        n = len(plan)
        with ExitStack() as ctx:
            self.mem_norm_phase(scope)
            sq = self.sb(ctx, "sq_a", [P, 2, T])
            small = self.sb(ctx, "small_a", [P, 3, 16])
            full = self.sb(ctx, "full_a", [P, 2, T])
            evac = self.sb(ctx, "evac_a", [P, 3, T])
            self.phase_begins("in_a")
            block = ctx.enter_context(nc.Block())
            self.norm_and_gemm(block, plan, self.first["in_a"], sq, small, full, evac, "mix_norm", 0)
        self.phase_over()

    def mem_norm_phase(self, scope):
        nc, ins, ps = self.nc, self.ins, self.ps
        self.mh = [self.sb(scope, f"mem_hi{l}", [P, KT, M], F32R) for l in range(2)]
        self.ml = [self.sb(scope, f"mem_lo{l}", [P, KT, M], F32R) for l in range(2)]
        with ExitStack() as ctx:
            min_ = self.sb(ctx, "mem_in", [P, M // P, D])
            mT = self.sb(ctx, "mem_T", [P, KT, M])
            sq = self.sb(ctx, "sq_m", [P, 2, M])
            small = self.sb(ctx, "small_m", [P, 3, 16])
            full = self.sb(ctx, "full_m", [P, KT, M])
            self.phase_begins("mem_norm")
            turned, mem_out, normed = self.sem("turned"), self.sem("mem_out"), self.sem("normed")
            block = ctx.enter_context(nc.Block())

            @block.sync
            def _(sp):
                sp.dma_start(min_[:], ins["mem"][0].rearrange("(t p) d -> p t d", p=P)).then_inc(self.loaded, 16)

            @block.tensor
            def _(pe):
                pe.wait_ge(self.loaded, 16)
                for t in range(M // P):
                    for k in range(KT):
                        mm = nc.tensor.transpose(ps[:, 2 * t + k // 4, (k % 4) * P:(k % 4 + 1) * P],
                                                 min_[:, t, k * P:(k + 1) * P], self.const("ident"))
                mm.then_inc(turned, 1)
                self.norm_pe(pe, M, sq, small[:, 2], 4, 6)

            @block.scalar
            def _(act):
                act.wait_ge(mem_out, 1)
                self.norm_act(act, lambda k: mT[:, k, :], M, sq)
                for l in range(2):
                    act.wait_ge(normed, l + 1)
                    nc.scalar.activation(self.mh[l][:], full[:], ACT.Copy).then_inc(self.h_hi, 1)

            @block.vector
            def _(dve):
                link = self.linker(dve, self.vector_link)
                dve.wait_ge(turned, 1)
                nc.vector.tensor_copy(mT[:, :, 0:P], ps[:, 0:2, :].rearrange("p b (k c) -> p (b k) c", c=P))
                nc.vector.tensor_copy(mT[:, :, P:M], ps[:, 2:4, :].rearrange("p b (k c) -> p (b k) c", c=P)).then_inc(mem_out, 1)
                dve.wait_ge(mem_out, 1)
                self.norm_dve_sums(dve, link, M, small, 4)
                dve.wait_ge(self.spread_done, 1)
                for l in range(2):
                    for k in range(KT):
                        i = nc.vector.scalar_tensor_tensor(out=full[:, k, :], in0=mT[:, k, :], scalar=self.param(f"mem_norm{l}", k),
                                                           in1=ps[:, 6, 0:M], op0=ALU.mult, op1=ALU.mult)
                    i.then_inc(normed, 1)
                    dve.wait_ge(self.h_hi, l + 1)
                    dve.wait_ge(normed, l + 1)
                    link(nc.vector.tensor_tensor(self.ml[l][:], full[:], self.mh[l][:].bitcast(F32), ALU.subtract))

            @block.gpsimd
            def _(pool):
                self.norm_pool(pool, M, small)
        self.phase_over()

    def norm_and_gemm(self, block, plan, s0, sq, small, full, evac, gain, layer):
        nc, ps = self.nc, self.ps
        n = len(plan)
        split_from = self.split_upto
        ahead = 0 if plan is self.a_plan else RING
        split_to = min(s0 + n + ahead, len(self.strips))
        stored = [self.sem(f"stored{r}") for r in range(3)]
        shifted, gate_in, soft = self.sem("shifted"), self.sem("gate_in"), self.sem("soft")

        def target(i):
            kind, c = plan[i]
            if kind in ("shift", "plain"):
                return self.u_dram[c], evac[:, i % 3, :]
            if kind == "kv":
                return self.kv_dram[c], evac[:, i % 3, :]
            if kind == "vt":
                return self.kv_dram[c], evac[:, i % 3, :]
            if kind == "f":
                return self.negc_dram, evac[0:12, i % 3, :]
            d = self.memk_dram if kind == "memk" else self.memv_dram
            return d[2 * c[0] + c[1]], evac[:, i % 3, 0:M]

        @block.sync
        def _(sp):
            for i in range(n):
                if s0 + i + RING >= split_from and s0 + i + RING < split_to:
                    self.load_strip(sp, s0 + i + RING)
                sp.wait_ge(self.psum_free, i + 1)
                dst, src = target(i)
                sp.dma_start(dst, src).then_inc(stored[i % 3], 16)
            for r in range(3):
                sp.wait_ge(stored[r], 16 * len(range(r, n, 3)))

        @block.gpsimd
        def _(pool):
            self.norm_pool(pool, T, small)
            for s in range(split_from, split_to):
                self.split_strip(pool, s)

        @block.scalar
        def _(act):
            link = self.linker(act, shifted if ("f", 12) in plan else None)
            self.norm_act(act, lambda k: self.X[:, k, :], T, sq)
            for k in range(KT):
                act.wait_ge(self.h_full, k + 1)
                nc.scalar.activation(self.hh[:, k, :], full[:, k % 2, :], ACT.Copy).then_inc(self.h_hi, 1)
            for i, (kind, c) in enumerate(plan):
                if kind == "shift":
                    act.wait_ge(self.strip_done, s0 + i + 1)
                    if i >= 3:
                        act.wait_ge(stored[i % 3], 16 * (i // 3))
                    nc.scalar.activation(evac[:, i % 3, :], self.bank2(i % 3), ACT.Copy,
                                                            scale=self.param("one_minus_mu", c)).then_inc(shifted, 1)
                if kind == "f":
                    act.wait_ge(gate_in, 1)
                    link(nc.scalar.activation(sq[0:12, 0, :], sq[0:12, 1, :], ACT.Abs))
                    link(nc.scalar.activation(full[0:12, 0, :], sq[0:12, 0, :], ACT.Exp, scale=-1.0))
                    nc.scalar.activation(full[0:12, 1, :], full[0:12, 0, :], ACT.Ln, bias=1.0).then_inc(soft, 1)

        @block.vector
        def _(dve):
            link = self.linker(dve, self.vector_link)
            if ("f", 12) in plan:
                link(nc.vector.memset(self.ones_row, 1.0))
            self.norm_dve_sums(dve, link, T, small, 4)
            dve.wait_ge(self.spread_done, 1)
            for k in range(KT):
                if k >= 2:
                    dve.wait_ge(self.h_hi, k - 1)
                    dve.wait_ge(self.h_lo, k - 1)
                nc.vector.scalar_tensor_tensor(
                    out=full[:, k % 2, :], in0=self.X[:, k, :], scalar=self.param(f"{gain}{layer}", k),
                    in1=self.bank2(3), op0=ALU.mult, op1=ALU.mult).then_inc(self.h_full, 1)
                dve.wait_ge(self.h_full, k + 1)
                dve.wait_ge(self.h_hi, k + 1)
                nc.vector.tensor_tensor(self.hl[:, k, :], full[:, k % 2, :], self.hh[:, k, :].bitcast(F32), ALU.subtract).then_inc(self.h_lo, 1)
            for i, (kind, c) in enumerate(plan):
                dve.wait_ge(self.strip_done, s0 + i + 1)
                out = evac[:, i % 3, :]
                if i >= 3:
                    dve.wait_ge(stored[i % 3], 16 * (i // 3))
                if kind == "shift":
                    mu = self.param("mu", c) if c < 20 else self.param("mu_last")
                    dve.wait_ge(shifted, sum(1 for q in plan[:i + 1] if q[0] == "shift"))
                    u = self.bank2(i % 3)
                    nc.vector.scalar_tensor_tensor(
                        out=out[:, 1:T], in0=u[:, 0:T - 1], scalar=mu, in1=out[:, 1:T], op0=ALU.mult, op1=ALU.add).then_inc(self.psum_free, 1)
                elif kind in ("memk", "memv"):
                    nc.vector.tensor_copy(out[:, 0:M], ps[:, 2 * (i % 3), 0:M]).then_inc(self.psum_free, 1)
                elif kind == "f":
                    nc.vector.tensor_scalar(sq[0:12, 1, :], self.bank2(i % 3)[0:12, :], self.param("b_f")[0:12, :],
                                                            None, ALU.add).then_inc(gate_in, 1)
                    dve.wait_ge(gate_in, 1)
                    dve.wait_ge(soft, 1)
                    link(nc.vector.scalar_tensor_tensor(out=full[0:12, 0, :], in0=sq[0:12, 1, :], scalar=0.0,
                                                                  in1=full[0:12, 1, :], op0=ALU.min, op1=ALU.subtract))
                    nc.vector.tensor_tensor_scan(out[0:12, :], self.ones_row, full[0:12, 0, :], 0.0,
                                                                     ALU.mult, ALU.subtract).then_inc(self.psum_free, 1)
                else:
                    nc.vector.tensor_copy(out, self.bank2(i % 3)).then_inc(self.psum_free, 1)

        @block.tensor
        def _(pe):
            self.norm_pe(pe, T, sq, small[:, 2], 4, 6)
            for i, (kind, c) in enumerate(plan):
                if i >= 3:
                    pe.wait_ge(self.psum_free, i - 2)
                ready = (lambda k: pe.wait_ge(self.h_lo, k + 1)) if i == 0 else None
                if kind in ("memk", "memv"):
                    self.gemm_strip(pe, s0 + i, i % 3, self.mh[c[0]], self.ml[c[0]], "fm" if kind == "memk" else "tm", M)
                else:
                    self.gemm_strip(pe, s0 + i, i % 3, self.hh, self.hl, "tm" if kind == "vt" else "fm", T, ready)

        self.split_upto = split_to

    def bank2(self, slot):
        return self.ps[:, 2 * slot:2 * slot + 2, :].rearrange("p b c -> p (b c)")

    def phase_project(self, scope, name, n, gain, layer):
        plan = {"kv": [("kv", c) for c in range(6)] + [("vt", 6 + c) for c in range(6)] + [("f", 12)],
                "in_b": [("plain", c) for c in range(14)]}[name]
        with ExitStack() as ctx:
            sq = self.sb(ctx, f"sq_{name}", [P, 2, T])
            small = self.sb(ctx, f"small_{name}", [P, 3, 16])
            full = self.sb(ctx, f"full_{name}", [P, 2, T])
            evac = self.sb(ctx, f"evac_{name}", [P, 3, T])
            if name == "kv":
                ones = self.sb(ctx, "ones_row", [12, T])
                self.ones_row = ones[:]
            self.phase_begins(name)
            block = ctx.enter_context(self.nc.Block())
            self.norm_and_gemm(block, plan, self.first[name], sq, small, full, evac, gain, layer)
        self.phase_over()


    def phase_rwkv(self):
        nc, ins, ps = self.nc, self.ins, self.ps
        STEPS = T // 256
        S = PAIRS * STEPS
        NC = T // C
        with ExitStack() as ctx:
            sb = lambda name, shape: self.sb(ctx, name, shape)
            self.phase_begins("rwkv")
            sem = self.sem
            lora = sb("lora_wa", [P, T])
            gate0 = sb("lora_g0", [P, T])
            gate1 = sb("lora_g1", [32, T])
            up_wa = sb("up_wa", [P, D_MAIN])
            up_g0 = sb("up_g0", [P, D_MAIN])
            up_g1 = sb("up_g1", [32, D_MAIN])
            ones = sb("ones_c", [P, C])
            r, k, v, kk, a, g, bonus, y = (sb(n, [P, 2, T]) for n in ("r", "k", "v", "kk", "a", "g", "bonus", "y"))
            state = sb("state", [P, 2, NC + 1, HD])
            chunk_decay = sb("chunk_decay", [P, 2, NC])
            cum = sb("cum", [P, T])
            dec = sb("dec", [P, NC, C + 1])
            tmp, sq = sb("tmp", [P, T]), sb("sq_r", [P, T])
            small, small_gn = sb("small_r", [P, 2, 16]), sb("small_gn", [P, 2, 16])
            tok = sb("tok", [P, 3, 4, 2, P])
            m_a = sb("m_a", [P, 2, 2, 3, 2, P])
            m_r = sb("m_r", [P, 3, 2, 2, 2, P])
            join = sb("join", [P, 2, 4, P])
            inv_m, inv_t, um = sb("inv_m", [P, 4, P]), sb("inv_t", [P, 4, P]), sb("um", [P, 4, P])
            mv, abar, vbar, sa = sb("mv", [P, 4, HD]), sb("abar", [P, 2, P]), sb("vbar", [P, 4, HD]), sb("sa", [P, 2, P])
            stmp = sb("stmp", [P, HD])

            lora_in = sem("lora_in")
            kv_in, r_in = sem("kv_in"), sem("r_in")
            lora_ready = sem("lora_ready")
            z_mm, z_act = sem("z_mm"), sem("z_act")
            a_mm, a_act = sem("a_mm"), sem("a_act")
            g_mm, g_act = sem("g_mm"), sem("g_act")
            kk_raw, kk_sq, kk_sum = sem("kk_raw"), sem("kk_sq"), sem("kk_sum")
            kk_ms, kk_rn, kk_bc = sem("kk_ms"), sem("kk_rn"), sem("kk_bc")
            kk_used = sem("kk_used")
            cum_done, dec_done = sem("cum_done"), sem("dec_done")
            rk_done, rk_sum, bonus_done, feat = sem("rk_done"), sem("rk_sum"), sem("bonus_done"), sem("feat")
            piece_mm = sem("piece_mm")
            piece_act, piece_dve = sem("piece_act"), sem("piece_dve")
            join_done, x0 = sem("join_done"), sem("x0")
            u_done, u_copied, xt_done, xt_added = sem("u_done"), sem("u_copied"), sem("xt_done"), sem("xt_added")
            mv_done, mv_copied, bars_done, bars_copied = sem("mv_done"), sem("mv_copied"), sem("bars_done"), sem("bars_copied")
            sa_done, sa_added, st_done, st_new = sem("sa_done"), sem("sa_added"), sem("st_done"), sem("st_new")
            y_done, y_copied = sem("y_done"), sem("y_copied")
            gn_mean, gn_centred, gn_sq, gn_sum = sem("gn_mean"), sem("gn_centred"), sem("gn_sq"), sem("gn_sum")
            gn_ms, gn_rn, gn_bc, gn_scaled, pair_done = sem("gn_ms"), sem("gn_rn"), sem("gn_bc"), sem("gn_scaled"), sem("pair_done")
            block = ctx.enter_context(nc.Block())

            ident = self.const("ident")
            halves = [(0, slice(0, HD)), (1, slice(HD, P))]
            flat = lambda t: t.rearrange("p a c -> p (a c)")
            chunks = lambda t: t.rearrange("p (c n) -> p c n", n=C)
            dec_before = dec[:, :, 0:C]
            dec_upto = dec[:, :, 1:C + 1]
            side = ps[:, 6:8, :].rearrange("p b c -> p (b c)")

            @block.sync
            def _(sp):
                for dst, src in ((lora[:], self.u_dram[18]), (gate0[:], self.u_dram[19]), (gate1[:], self.u_dram[20][0:32, :]),
                                 (up_wa[0:HD, :], ins["a_w_up"][0]), (up_wa[HD:P, :], ins["a_a_up"][0]),
                                 (up_g0[:], ins["a_g_up"][0][0:P, :]), (up_g1[:], ins["a_g_up"][0][P:160, :])):
                    sp.dma_start(dst, src).then_inc(lora_in, 16)
                for p in range(PAIRS):
                    if p >= 1:
                        sp.wait_ge(kv_in, 32 * p)
                        sp.wait_ge(r_in, 16 * p)
                    if p >= 2:
                        sp.wait_ge(piece_mm, 8 * STEPS * (p - 1))
                        sp.wait_ge(bonus_done, p - 1)
                    sp.dma_start(k[:, p % 2, :], self.u_dram[6 + p]).then_inc(kv_in, 16)
                    sp.dma_start(v[:, p % 2, :], self.u_dram[12 + p]).then_inc(kv_in, 16)
                    if p >= 2:
                        sp.wait_ge(y_done, STEPS * (p - 1))
                    sp.dma_start(r[:, p % 2, :], self.u_dram[p]).then_inc(r_in, 16)

            @block.tensor
            def _(pe):
                mmul = nc.tensor.matmul

                def side_halves(parts, semaphore):
                    for j in range(2):
                        for i, (w, x) in enumerate(parts):
                            mm = mmul(ps[:, 6 + j, :], w, x[:, j * HALF:(j + 1) * HALF], start=(i == 0), stop=(i == len(parts) - 1))
                    mm.then_inc(semaphore, 1)

                def head_sums(semaphore):
                    for t in range(TT):
                        mm = mmul(ps[:, 6, 2 * t:2 * t + 2], sq[:, t * P:(t + 1) * P], self.const("heads"), start=True, stop=True)
                    mm.then_inc(semaphore, 1)

                def prepare(p, stage):
                    cols = slice(p * P, (p + 1) * P)
                    if stage == "z":
                        pe.wait_ge(g_act, p)
                        side_halves([(up_wa[0:HD, cols], lora[0:HD, :])], z_mm)
                    elif stage == "a":
                        pe.wait_ge(z_act, p + 1)
                        side_halves([(up_wa[HD:P, cols], lora[HD:P, :])], a_mm)
                    elif stage == "kk_sum":
                        pe.wait_ge(a_act, p + 1)
                        pe.wait_ge(kk_sq, p + 1)
                        head_sums(kk_sum)
                    elif stage == "kk_bc":
                        pe.wait_ge(kk_rn, p + 1)
                        if p >= 2:
                            pe.wait_ge(gn_centred, p - 1)
                        self.spread(small[:, 1, :], 3).then_inc(kk_bc, 1)
                    elif stage == "rk":
                        pe.wait_ge(rk_done, p + 1)
                        pe.wait_ge(kk_used, p + 1)
                        if p >= 2:
                            pe.wait_ge(gn_scaled, p - 1)
                        side_halves([(self.const("pairsum"), tmp)], rk_sum)
                    elif stage == "g":
                        pe.wait_ge(bonus_done, p + 1)
                        side_halves([(up_g0[:, cols], gate0), (up_g1[:, cols], gate1)], g_mm)

                def group_norm(p, stage):
                    if stage == "mean":
                        pe.wait_ge(y_copied, STEPS * (p + 1))
                        pe.wait_ge(g_act, min(p + 2, PAIRS))
                        pe.wait_ge(gn_scaled, p)
                        if p + 2 < PAIRS:
                            pe.wait_ge(kk_ms, p + 3)
                        side_halves([(self.const("pairsum"), y[:, p % 2, :])], gn_mean)
                    elif stage == "sum":
                        pe.wait_ge(gn_sq, p + 1)
                        if p + 2 < PAIRS:
                            pe.wait_ge(kk_used, p + 3)
                        head_sums(gn_sum)
                    elif stage == "bc":
                        pe.wait_ge(gn_rn, p + 1)
                        self.spread(small_gn[:, 1, :], 3).then_inc(gn_bc, 1)

                def piece(s, i):
                    p, q = s // STEPS, s % STEPS
                    b = p % 2
                    if i == 0 and q == 0:
                        pe.wait_ge(feat, p + 1)
                    if i in (1, 2):
                        pe.wait_ge(piece_act, 2 * s + i)
                    else:
                        pe.wait_ge(piece_dve, 6 * s + max(i - 2, 0))
                    if i == 0 and s:
                        pe.wait_ge(mv_copied, s - 1)
                    tiles = (2 * q, 2 * q + 1)
                    if i < 2:
                        for n, src in enumerate(((kk, a), (k, v))[i]):
                            for t in range(2):
                                c = tiles[t] * P
                                mm = nc.tensor.transpose(ps[:, 3, (2 * n + t) * P:(2 * n + t + 1) * P], src[:, b, c:c + P], ident)
                    else:
                        h = halves[(i - 2) // 3][1]
                        products = (((a, kk), (k, kk)), ((kk, a),), ((a, r), (k, r)))[(i - 2) % 3]
                        for n, (w, x) in enumerate(products):
                            for t in range(2):
                                c = slice(tiles[t] * P, (tiles[t] + 1) * P)
                                mm = mmul(ps[:, 3, (2 * n + t) * P:(2 * n + t + 1) * P], w[h, b, c], x[h, b, c], start=True, stop=True)
                    mm.then_inc(piece_mm, 1)

                pe.wait_ge(lora_ready, 1)
                for stage in ("z", "a", "kk_sum", "kk_bc", "rk", "g"):
                    prepare(0, stage)
                for i in range(8):
                    piece(0, i)
                for s in range(S + 1):
                    p, q = s // STEPS, s % STEPS
                    side_work = {(0, 1): "z", (0, 2): "a", (0, 4): "kk_sum", (1, 3): "kk_bc", (2, 3): "rk", (2, 5): "g"}
                    gn_work = {(1, 1): "mean", (1, 5): "sum", (2, 1): "bc"}
                    o, op, oq = s - 1, (s - 1) // STEPS, (s - 1) % STEPS
                    otok = tok[:, o % 3]
                    for l in range(1, LEVELS + 1):
                        n = LEVELS * s + l - 1
                        c = l - 1
                        t, b = c // 2, slice((c % 2) * C, (c % 2 + 1) * C)
                        if s < S:
                            pe.wait_ge(join_done, n + 1)
                            if l == 1:
                                pe.wait_ge(x0, s + 1)
                            else:
                                pe.wait_ge(xt_added, n)
                            for i in range(4):
                                mm = mmul(ps[:, 0, i * P:(i + 1) * P], join[:, n % 2, i, :], inv_m[:, i, :], start=True, stop=True)
                            mm.then_inc(u_done, 1)
                        if s and l <= 4:
                            if c == 0:
                                pe.wait_ge(bars_copied, s)
                            pe.wait_ge(st_new, 4 * o + c + op + 1)
                            if o and c == 0:
                                pe.wait_ge(y_copied, o)
                            for h, hs in halves:
                                mm = mmul(ps[b, 4 + h, c * HD:(c + 1) * HD], abar[hs, t, b], state[hs, op % 2, 4 * oq + c, :], start=True, stop=True)
                            mm.then_inc(sa_done, 1)
                        if s + 1 < S and l <= 4:
                            piece(s + 1, 2 * l - 2)
                        if s < S and l == 5:
                            if s + 1 < S:
                                pe.wait_ge(piece_dve, 6 * (s + 2))
                            for i in range(4):
                                mm = mmul(ps[:, 3, i * HD:(i + 1) * HD], m_a[:, s % 2, i // 2, 1, i % 2, :], tok[:, s % 3, 3, i % 2, halves[i // 2][1]],
                                          start=True, stop=True)
                            mm.then_inc(mv_done, 1)
                        if s < S:
                            pe.wait_ge(u_copied, n + 1)
                            for i in range(4):
                                if l < LEVELS:
                                    mmul(ps[:, 1, i * P:(i + 1) * P], inv_t[:, i, :], um[:, i, :], start=True, stop=True)
                                mm = mmul(ps[:, 2, i * P:(i + 1) * P], um[:, i, :], inv_t[:, i, :], start=True, stop=True)
                            mm.then_inc(xt_done, 1)
                        if s and l <= 4:
                            pe.wait_ge(sa_added, 4 * o + c + 1)
                            for h, hs in halves:
                                mmul(ps[hs, 4, 256 + c * HD:256 + (c + 1) * HD], otok[b, 1, t, hs], sa[b, t, hs], start=True, stop=False)
                                mm = mmul(ps[hs, 4, 256 + c * HD:256 + (c + 1) * HD], otok[b, 2, t, hs], otok[b, 3, t, hs], start=False, stop=True)
                            mm.then_inc(st_done, 1)
                        if s + 1 < S and l <= 4:
                            piece(s + 1, 2 * l - 1)
                        if s < S and (q, l) in side_work and p + 1 < PAIRS:
                            prepare(p + 1, side_work[(q, l)])
                        if s < S and (q, l) in gn_work and p >= 1:
                            group_norm(p - 1, gn_work[(q, l)])
                    if s < S:
                        pe.wait_ge(xt_added, LEVELS * (s + 1))
                        pe.wait_ge(mv_copied, s + 1)
                        for i in range(4):
                            h = halves[i // 2][1]
                            mmul(ps[h, 1, (i % 2) * P:(i % 2 + 1) * P], tok[:, s % 3, 0, i % 2, h], inv_t[:, i, :], start=True, stop=True)
                            mm = mmul(ps[:, 2, i * HD:(i + 1) * HD], inv_t[:, i, :], mv[:, i, :], start=True, stop=True)
                        mm.then_inc(bars_done, 1)
                    if s:
                        pe.wait_ge(st_new, 4 * s + op + 1)
                        for i in range(4):
                            hn, h = halves[i // 2]
                            t = i % 2
                            out = ps[h, 5, 256 + t * P:256 + (t + 1) * P]
                            mmul(out, sa[:, t, h], m_r[:, o % 3, hn, 0, t, :], start=True, stop=False)
                            mmul(out, otok[:, 3, t, h], m_r[:, o % 3, hn, 1, t, :], start=False, stop=False)
                            for b in range(2):
                                at = (2 * oq + t) * P + b * C
                                mm = mmul(ps[h, 5, 256 + t * P + b * C:256 + t * P + (b + 1) * C], state[h, op % 2, 4 * oq + 2 * t + b, :],
                                          r[h, op % 2, at:at + C], start=False, stop=(b == 1))
                        mm.then_inc(y_done, 1)
                for stage in ("mean", "sum", "bc"):
                    group_norm(PAIRS - 1, stage)

            @block.scalar
            def _(act):
                copy = lambda out, x: nc.scalar.activation(out, x, ACT.Copy)

                def prepare(p, stage):
                    b = p % 2
                    if stage == "z":
                        act.wait_ge(z_mm, p + 1)
                        act.wait_ge(feat, p)
                        nc.scalar.activation(cum[:], side, ACT.Sigmoid, bias=self.param("a_w0", p)).then_inc(z_act, 1)
                    elif stage == "a":
                        act.wait_ge(a_mm, p + 1)
                        nc.scalar.activation(a[:, b, :], side, ACT.Sigmoid, bias=self.param("a_a0", p)).then_inc(a_act, 1)
                    elif stage == "sq":
                        act.wait_ge(kk_raw, p + 1)
                        if p >= 3:
                            act.wait_ge(gn_sum, p - 2)
                        nc.scalar.activation(sq[:], kk[:, b, :], ACT.Square).then_inc(kk_sq, 1)
                    elif stage == "exp":
                        act.wait_ge(cum_done, p + 1)
                        nc.scalar.activation(dec_upto, chunks(tmp[:]), ACT.Exp, scale=-DECAY)
                        nc.scalar.activation(cum[:], tmp[:], ACT.Exp, scale=DECAY).then_inc(dec_done, 1)
                    elif stage == "g":
                        act.wait_ge(g_mm, p + 1)
                        if p >= 2:
                            act.wait_ge(pair_done, p - 1)
                        copy(g[:, b, :], side).then_inc(g_act, 1)

                def piece(s, i):
                    act.wait_ge(piece_mm, 8 * s + i + 1)
                    copy(tok[:, s % 3, 2 * i:2 * i + 2].rearrange("p a t c -> p (a t c)"), ps[:, 3, :]).then_inc(piece_act, 1)

                def group_square(p):
                    act.wait_ge(gn_centred, p + 1)
                    if p + 2 < PAIRS:
                        act.wait_ge(kk_sum, p + 3)
                    nc.scalar.activation(sq[:], y[:, p % 2, :], ACT.Square).then_inc(gn_sq, 1)

                act.wait_ge(lora_in, 7 * 16)
                nc.scalar.activation(lora[0:HD, :], lora[0:HD, :], ACT.Tanh)
                nc.scalar.activation(gate0[:], gate0[:], ACT.Sigmoid)
                nc.scalar.activation(gate1[:], gate1[:], ACT.Sigmoid).then_inc(lora_ready, 1)
                for stage in ("z", "a", "sq", "exp", "g"):
                    prepare(0, stage)
                piece(0, 0)
                piece(0, 1)
                for s in range(S + 1):
                    p, q = s // STEPS, s % STEPS
                    side_work = {(0, 1): ("z",), (0, 2): ("a",), (0, 3): ("sq",), (0, 5): ("exp",), (3, 1): ("g",)}
                    for l in range(1, LEVELS + 1):
                        n = LEVELS * s + l - 1
                        if s < S:
                            act.wait_ge(u_done, n + 1)
                            act.wait_ge(xt_done, n)
                            copy(flat(um[:]), ps[:, 0, :]).then_inc(u_copied, 1)
                        if s + 1 < S and l == 1:
                            piece(s + 1, 0)
                            piece(s + 1, 1)
                        if s < S and l == 5:
                            act.wait_ge(mv_done, s + 1)
                            copy(flat(mv[:]), ps[:, 3, 0:4 * HD]).then_inc(mv_copied, 1)
                        if s < S and p + 1 < PAIRS:
                            for stage in side_work.get((q, l), ()):
                                prepare(p + 1, stage)
                        if s < S and (q, l) == (1, 2) and p >= 1:
                            group_square(p - 1)
                    if s < S:
                        act.wait_ge(bars_done, s + 1)
                        if s:
                            act.wait_ge(sa_added, 4 * s)
                        copy(flat(abar[:]), ps[:, 1, 0:2 * P])
                        copy(flat(vbar[:]), ps[:, 2, 0:4 * HD]).then_inc(bars_copied, 1)
                    if s:
                        o = s - 1
                        act.wait_ge(y_done, s)
                        copy(y[:, (o // STEPS) % 2, (o % STEPS) * 2 * P:(o % STEPS + 1) * 2 * P], ps[:, 5, 256:512]).then_inc(y_copied, 1)
                group_square(PAIRS - 1)

            @block.gpsimd
            def _(pool):
                def rsqrt(ready, buffer, done, p):
                    pool.wait_ge(ready, p + 1)
                    nc.gpsimd.tensor_tensor(buffer[:, 1, :], buffer[:, 0, :], self.const("minus_half"), ALU.pow).then_inc(done, 1)

                rsqrt(kk_ms, small, kk_rn, 0)
                for s in range(S):
                    p, q = s // STEPS, s % STEPS
                    pool.wait_ge(piece_dve, 6 * s + 4)
                    for l in range(1, LEVELS + 1):
                        n = LEVELS * s + l - 1
                        if n >= 2:
                            pool.wait_ge(u_done, n - 1)
                        nc.gpsimd.tensor_tensor(join[:, n % 2].rearrange("p (h t) c -> p h t c", h=2), m_a[:, s % 2, :, 0],
                                                self.mask4(f"join{l}"), ALU.mult).then_inc(join_done, 1)
                        if (q, l) == (1, 1) and p + 1 < PAIRS:
                            rsqrt(kk_ms, small, kk_rn, p + 1)
                        if (q, l) == (1, 5) and p >= 1:
                            rsqrt(gn_ms, small_gn, gn_rn, p - 1)
                rsqrt(gn_ms, small_gn, gn_rn, PAIRS - 1)

            @block.vector
            def _(dve):
                link = self.linker(dve, self.vector_link)
                tt, stt, ts = nc.vector.tensor_tensor, nc.vector.scalar_tensor_tensor, nc.vector.tensor_scalar

                def prepare(p, stage):
                    b = p % 2
                    rp, kp, vp, kkp, ap = r[:, b, :], k[:, b, :], v[:, b, :], kk[:, b, :], a[:, b, :]
                    if stage == "kk_raw":
                        dve.wait_ge(kv_in, 32 * (p + 1))
                        ts(kkp, kp, self.param("a_k_k", p), None, ALU.mult).then_inc(kk_raw, 1)
                    elif stage == "scan":
                        dve.wait_ge(z_act, p + 1)
                        dve.wait_ge(rk_sum, p)
                        for c in range(NC):
                            i = nc.vector.tensor_tensor_scan(tmp[:, c * C:(c + 1) * C], ones[:], cum[:, c * C:(c + 1) * C], 0.0, ALU.mult, ALU.add)
                        i.then_inc(cum_done, 1)
                    elif stage == "decay":
                        dve.wait_ge(dec_done, p + 1)
                        nc.vector.tensor_copy(chunk_decay[:, b, :], dec[:, :, C])
                    elif stage == "k":
                        dve.wait_ge(a_act, p + 1)
                        dve.wait_ge(dec_done, p + 1)
                        link(ts(tmp[:], ap, 1.0, self.param("a_k_a", p), ALU.subtract, ALU.mult))
                        link(stt(out=kp, in0=tmp[:], scalar=1.0, in1=kp, op0=ALU.add, op1=ALU.mult))
                    elif stage == "kk_ms":
                        dve.wait_ge(kk_sum, p + 1)
                        ts(small[:, 0, :], ps[:, 6, 0:16], 1e-24, None, ALU.max).then_inc(kk_ms, 1)
                    elif stage == "rk":
                        dve.wait_ge(r_in, 16 * (p + 1))
                        stt(out=tmp[:], in0=rp, scalar=self.param("a_r_k", p), in1=kp, op0=ALU.mult, op1=ALU.mult).then_inc(rk_done, 1)
                    elif stage == "kk":
                        dve.wait_ge(kk_bc, p + 1)
                        tt(kkp, kkp, side, ALU.mult).then_inc(kk_used, 1)
                        dve.wait_ge(kk_used, p + 1)
                    elif stage == "b":
                        link(tt(ap, kkp, ap, ALU.mult))
                        tt(ap, ap, cum[:], ALU.mult)
                    elif stage == "K":
                        tt(kp, kp, cum[:], ALU.mult)
                    elif stage == "R":
                        tt(chunks(rp), chunks(rp), dec_upto, ALU.mult)
                    elif stage == "A":
                        stt(out=chunks(kkp), in0=chunks(kkp), scalar=-1.0, in1=dec_before, op0=ALU.mult, op1=ALU.mult).then_inc(feat, 1)
                    elif stage == "bonus":
                        dve.wait_ge(rk_sum, p + 1)
                        tt(bonus[:, b, :], vp, side, ALU.mult).then_inc(bonus_done, 1)

                def group_norm(p, stage):
                    yp = y[:, p % 2, :]
                    if stage == "centre":
                        dve.wait_ge(gn_mean, p + 1)
                        stt(out=yp, in0=side, scalar=-1.0 / HD, in1=yp, op0=ALU.mult, op1=ALU.add).then_inc(gn_centred, 1)
                    elif stage == "ms":
                        dve.wait_ge(gn_sum, p + 1)
                        ts(small_gn[:, 0, :], ps[:, 6, 0:16], 1.0 / HD, GN_EPS, ALU.mult, ALU.add).then_inc(gn_ms, 1)
                    elif stage == "scale":
                        dve.wait_ge(gn_bc, p + 1)
                        tt(yp, yp, side, ALU.mult).then_inc(gn_scaled, 1)
                        dve.wait_ge(gn_scaled, p + 1)
                        link(ts(yp, yp, self.param("a_lnx_g", p), self.param("a_lnx_b", p), ALU.mult, ALU.add))
                    elif stage == "out":
                        link(tt(yp, yp, bonus[:, p % 2, :], ALU.add))
                        dve.wait_ge(g_act, p + 1)
                        tt(self.X[:, p, :], yp, g[:, p % 2, :], ALU.mult).then_inc(pair_done, 1)

                def piece(s, i):
                    h, kind = (i - 2) // 3, (i - 2) % 3
                    dve.wait_ge(piece_mm, 8 * s + i + 1)
                    quad = ps[:, 3, :].rearrange("p (a t c) -> p a t c", a=2, t=2)
                    if kind == 0:
                        done = tt(m_a[:, s % 2, h, 0:2], quad, self.mask4("before"), ALU.mult)
                    elif kind == 1:
                        done = tt(m_a[:, s % 2, h, 2], quad[:, 0], self.mask("pair0", 2), ALU.mult)
                    else:
                        done = tt(m_r[:, s % 3, h], quad, self.mask4("upto"), ALU.mult)
                    done.then_inc(piece_dve, 1)

                def zero_state(p):
                    nc.vector.memset(state[:, p % 2, 0, :], 0.0).then_inc(st_new, 1)

                nc.vector.memset(dec[:, :, 0:1], 1.0)
                link(nc.vector.memset(ones[:], 1.0))
                for stage in ("kk_raw", "scan", "k", "kk_ms", "rk", "kk", "decay", "b", "K", "bonus", "R", "A"):
                    prepare(0, stage)
                for i in range(2, 8):
                    piece(0, i)
                for s in range(S + 1):
                    p, q = s // STEPS, s % STEPS
                    side_work = {(0, 1): ("kk_raw",), (0, 3): ("scan",), (0, 5): ("kk_ms",), (1, 1): ("k",), (1, 2): ("decay",),
                                 (1, 3): ("rk",), (1, 4): ("kk",), (1, 5): ("b",), (2, 1): ("K",), (2, 4): ("bonus", "R"), (2, 5): ("A",)}
                    gn_work = {(1, 2): ("centre",), (1, 5): ("ms",), (2, 2): ("scale",), (2, 3): ("out",)}
                    o, op, oq = s - 1, (s - 1) // STEPS, (s - 1) % STEPS
                    if s < S:
                        dve.wait_ge(piece_dve, 6 * (s + 1))
                        if s:
                            dve.wait_ge(bars_done, s)
                        four = lambda x: x.rearrange("p (h t) c -> p h t c", h=2)
                        link(tt(four(inv_t[:]), m_a[:, s % 2, :, 0], self.mask4("join0"), ALU.mult))
                        tt(four(inv_m[:]), m_a[:, s % 2, :, 2], self.mask4("ident"), ALU.add)
                        tt(four(inv_t[:]), four(inv_t[:]), self.mask4("ident"), ALU.add).then_inc(x0, 1)
                    if o >= 0 and oq == 0:
                        zero_state(op)
                    for l in range(1, LEVELS + 1):
                        n = LEVELS * s + l
                        c = l - 1
                        t, b = c // 2, slice((c % 2) * C, (c % 2 + 1) * C)
                        if s and l <= 4:
                            dve.wait_ge(sa_done, 4 * o + c + 1)
                            if c == 0:
                                dve.wait_ge(bars_copied, s)
                            tt(sa[b, t, :].rearrange("p (h c) -> p h c", h=2), ps[b, 4:6, c * HD:(c + 1) * HD],
                               vbar[b].rearrange("p (h t) c -> p h t c", h=2)[:, :, t, :], ALU.add).then_inc(sa_added, 1)
                        if s + 1 < S and 2 <= l <= 4:
                            piece(s + 1, 2 * l - 2)
                        if s < S:
                            dve.wait_ge(xt_done, n)
                            if l < LEVELS:
                                tt(inv_m[:], inv_m[:], ps[:, 1, :].rearrange("p (i c) -> p i c", i=4), ALU.add)
                            tt(inv_t[:], inv_t[:], ps[:, 2, :].rearrange("p (i c) -> p i c", i=4), ALU.add).then_inc(xt_added, 1)
                        if s and l <= 4:
                            ci = 4 * oq + c
                            dve.wait_ge(st_done, 4 * o + c + 1)
                            link(tt(stmp[:], ps[:, 4, 256 + c * HD:256 + (c + 1) * HD], state[:, op % 2, ci, :], ALU.add))
                            ts(state[:, op % 2, ci + 1, :], stmp[:], chunk_decay[:, op % 2, ci:ci + 1], None, ALU.mult).then_inc(st_new, 1)
                            dve.wait_ge(st_new, 4 * o + c + op + 2)
                        if s + 1 < S and 2 <= l <= 4:
                            piece(s + 1, 2 * l - 1)
                        if s < S and p + 1 < PAIRS:
                            for stage in side_work.get((q, l), ()):
                                prepare(p + 1, stage)
                        if s < S and p >= 1:
                            for stage in gn_work.get((q, l), ()):
                                group_norm(p - 1, stage)
                for stage in ("centre", "ms", "scale", "out"):
                    group_norm(PAIRS - 1, stage)
        self.phase_over()

    def spread(self, cols, slot, tiles=TT):
        nc, ps = self.nc, self.ps
        for t in range(tiles):
            for h in range(2):
                mm = nc.tensor.matmul(ps[h * HD:(h + 1) * HD, 2 * slot + t // 4, (t % 4) * P:(t % 4 + 1) * P],
                                      cols[:, 2 * t + h:2 * t + h + 1].broadcast_to([P, HD]), self.const("ident"), start=True, stop=True)
        return mm


    def phase_fox(self):
        pairs = [dict(q=p, k=self.kv_dram[p], v=self.kv_dram[6 + p], gate=6 + p, out=p) for p in range(PAIRS)]
        self.phase_attention("fox", pairs, T, "b_q_gain", "k_gain", causal=True)

    def phase_mem_attention(self, layer, q_at):
        pairs = [dict(q=q_at + p, k=self.memk_dram[2 * layer + p], v=self.memv_dram[2 * layer + p], gate=None, out=PAIRS + p)
                 for p in range(MEM_PAIRS)]
        self.phase_attention(f"mem{layer}", pairs, M, f"mem_q_gain{layer}", f"mem_k_gain{layer}", causal=False)

    def phase_attention(self, name, pairs, width, q_gain, k_gain, causal):
        nc, ps = self.nc, self.ps
        with ExitStack() as ctx:
            sb = lambda n, shape: self.sb(ctx, f"{name}_{n}", shape)
            self.phase_begins(name)
            sg = self.sem
            q, k, v = sb("q", [P, 2, T]), sb("k", [P, 2, width]), sb("v", [P, 2, width // P, P])
            gate = sb("gate", [P, 2, T])
            negc = sb("negc", [P, 2, 2, T if causal else 1])
            sq = sb("sq", [P, 2, T])
            small = sb("small", [P, 2, 3, 16])
            prob = sb("prob", [P, 2, width])
            prob_t = sb("prob_t", [P, 2, width // P, P])
            stat = sb("stat", [P, 4, 4])
            o = sb("o", [P, 2, P])
            loaded, squared, summed, ms, rn, spread, qk = (sg("pair_" + n) for n in ("loaded", "squared", "summed", "ms", "rn", "spread", "qk"))
            scored, maxed, exped, turned, pt_d, pt_a, pv, o_norm, ot, stored = (
                sg(n) for n in ("scored", "maxed", "exped", "turned", "pt_d", "pt_a", "pv", "o_norm", "ot", "stored"))
            gated = sg("gated")
            block = ctx.enter_context(nc.Block())
            N = len(pairs)
            refill = range(self.split_upto, self.first["out0"] + RING) if name == "mem0" else range(0)
            units = [(t, h) for t in range(TT) for h in range(2)]
            U = len(units)
            keys = lambda t: (t + 1) * P if causal else width
            LAG = 4
            second_bank = lambda n: sum(1 for m in range(n) if keys(units[m % U][0]) > HALF)
            loads = 5 if causal else 3
            hs = (slice(0, HD), slice(HD, P))

            @block.sync
            def _(sp):
                for strip in refill:
                    self.load_strip(sp, strip)
                for p, pr in enumerate(pairs):
                    b = p % 2
                    if p >= 2:
                        sp.wait_ge(stored, TT * (p - 1))
                    n = 0
                    sp.dma_start(q[:, b, :], self.u_dram[pr["q"]]).then_inc(loaded, 16)
                    sp.dma_start(k[:, b, :], pr["k"]).then_inc(loaded, 16)
                    sp.dma_start(v[:, b].rearrange("p a c -> p (a c)"), pr["v"]).then_inc(loaded, 16)
                    if causal:
                        sp.dma_start(gate[:, b, :], self.u_dram[pr["gate"]]).then_inc(loaded, 16)
                        sp.dma_start(negc[:, b, :, :], self.negc_dram[2 * p:2 * p + 2, :].partition_broadcast(P)).then_inc(loaded, 16)
                    sp.wait_ge(loaded, 16 * loads * (p + 1))

            @block.tensor
            def _(pe):
                mmul = nc.tensor.matmul
                for p in range(N):
                    b = p % 2
                    for n, w in ((0, T), (1, width)):
                        pe.wait_ge(squared, 2 * p + n + 1)
                        if p:
                            pe.wait_ge(stored, TT * p)
                        for t in range(w // P):
                            mm = mmul(ps[:, 6 + n, 2 * t:2 * t + 2], sq[:, n, t * P:(t + 1) * P], self.const("heads"), start=True, stop=True)
                        mm.then_inc(summed, 1)
                    for n, w in ((0, T), (1, width)):
                        pe.wait_ge(rn, 2 * p + n + 1)
                        self.spread(small[:, n, 2, :], n, w // P).then_inc(spread, 1)
                    pe.wait_ge(qk, 2 * (p + 1))
                    for n in range(U + LAG):
                        if n < U:
                            t, h = units[n]
                            g = p * U + n
                            if n >= 2:
                                pe.wait_ge((maxed if causal else exped), g - 1)
                            nk = keys(t)
                            for c in range(0, nk, HALF):
                                w = min(HALF, nk - c)
                                last = c + w == nk
                                mm = mmul(ps[:, 2 * (n % 2) + c // HALF, 0:w], q[hs[h], b, t * P:(t + 1) * P], k[hs[h], b, c:c + w],
                                          start=True, stop=not (causal and last))
                                if causal and last:
                                    mm = mmul(ps[:, 2 * (n % 2) + c // HALF, w - P:w], self.const("ident"), self.const("future"),
                                              start=False, stop=True)
                            mm.then_inc(scored, 1)
                        m = n - 1
                        if 0 <= m < U:
                            g = p * U + m
                            t, h = units[m]
                            pe.wait_ge(exped, g + 1)
                            pe.wait_ge(pt_d, g)
                            pe.wait_ge(pt_a, second_bank(g))
                            for j in range(keys(t) // P):
                                mm = nc.tensor.transpose(ps[:, 4 + j // 4, (j % 4) * P:(j % 4 + 1) * P], prob[:, m % 2, j * P:(j + 1) * P],
                                                         self.const("ident"))
                            mm.then_inc(turned, 1)
                        m = n - 2
                        if 0 <= m < U:
                            g = p * U + m
                            t, h = units[m]
                            pe.wait_ge(pt_d, g + 1)
                            pe.wait_ge(pt_a, second_bank(g + 1))
                            pe.wait_ge(o_norm, g)
                            nj = keys(t) // P
                            for j in range(nj):
                                mm = mmul(ps[:, 6, 0:HD], prob_t[:, m % 2, j, :], v[:, b, j, hs[h]], start=(j == 0), stop=(j == nj - 1))
                            mm.then_inc(pv, 1)
                        m = n - 3
                        if 0 <= m < U and m % 2:
                            g = p * U + m
                            pe.wait_ge(o_norm, g + 1)
                            pe.wait_ge(stored, (g + 1) // 2 - 1)
                            nc.tensor.transpose(ps[:, 7, 0:P], o[:, (m // 2) % 2, :], self.const("ident")).then_inc(ot, 1)

            @block.scalar
            def _(act):
                for p in range(N):
                    b = p % 2
                    act.wait_ge(loaded, 16 * loads * (p + 1))
                    nc.scalar.activation(sq[:, 0, :], q[:, b, :], ACT.Square).then_inc(squared, 1)
                    nc.scalar.activation(sq[:, 1, 0:width], k[:, b, :], ACT.Square).then_inc(squared, 1)
                    if causal:
                        nc.scalar.activation(gate[:, b, :], gate[:, b, :], ACT.Sigmoid).then_inc(gated, 1)
                    for n in range(U + LAG):
                        if n < U:
                            t, h = units[n]
                            g = p * U + n
                            nk = keys(t)
                            act.wait_ge(maxed, g + 1)
                            src = prob[:, n % 2, 0:nk] if causal else ps[:, 2 * (n % 2), 0:nk]
                            if n >= 2 and not causal:
                                act.wait_ge(turned, g - 1)
                            if n >= 4:
                                act.wait_ge(o_norm, g - 3)
                            nc.scalar.activation(prob[:, n % 2, 0:nk], src, ACT.Exp, bias=stat[:, n % 4, 1:2],
                                                            accum_out=stat[:, n % 4, 2:3]).then_inc(exped, 1)
                        m = n - 1
                        if 0 <= m < U and keys(units[m][0]) > HALF:
                            g = p * U + m
                            nj = keys(units[m][0]) // P
                            act.wait_ge(turned, g + 1)
                            if g >= 2:
                                act.wait_ge(pv, g - 1)
                            nc.scalar.activation(prob_t[:, m % 2, 4:nj, :].rearrange("p a c -> p (a c)"), ps[:, 5, 0:(nj - 4) * P], ACT.Copy).then_inc(pt_a, 1)

            @block.gpsimd
            def _(pool):
                for p in range(N):
                    for n, w in ((0, T), (1, width)):
                        pool.wait_ge(ms, 2 * p + n + 1)
                        nc.gpsimd.tensor_tensor(small[:, n, 2, 0:w // HD], small[:, n, 1, 0:w // HD],
                                                        self.const("minus_half")[:, 0:w // HD], ALU.pow).then_inc(rn, 1)
                for strip in refill:
                    self.split_strip(pool, strip)

            @block.vector
            def _(dve):
                link = self.linker(dve, self.vector_link)
                for p, pr in enumerate(pairs):
                    b = p % 2
                    dve.wait_ge(loaded, 16 * loads * (p + 1))
                    for n, w in ((0, T), (1, width)):
                        dve.wait_ge(summed, 2 * p + n + 1)
                        nc.vector.tensor_scalar(small[:, n, 1, 0:w // HD], ps[:, 6 + n, 0:w // HD], 1.0 / HD, RMS_EPS, ALU.mult, ALU.add).then_inc(ms, 1)
                    for n, (x, w, gn) in enumerate(((q, T, q_gain), (k, width, k_gain))):
                        dve.wait_ge(spread, 2 * p + n + 1)
                        i = nc.vector.scalar_tensor_tensor(out=x[:, b, :], in0=x[:, b, :], scalar=self.param(gn), in1=self.bank2(n)[:, 0:w],
                                                           op0=ALU.mult, op1=ALU.mult)
                        if n == 0:
                            link(i)
                            i = nc.vector.tensor_scalar(x[:, b, :], x[:, b, :], SCALE, None, ALU.mult)
                        i.then_inc(qk, 1)
                    if causal:
                        dve.wait_ge(gated, p + 1)
                    for n in range(U + LAG):
                        if n < U:
                            t, h = units[n]
                            g = p * U + n
                            nk = keys(t)
                            dve.wait_ge(scored, g + 1)
                            s4 = stat[:, n % 4]
                            if causal:
                                if n >= 2:
                                    dve.wait_ge(turned, g - 1)
                                src = self.bank2(n % 2)[:, 0:nk]
                                link(nc.vector.tensor_tensor_reduce(
                                    out=prob[:, n % 2, 0:nk], in0=src, in1=negc[:, b, h, 0:nk], scale=1.0, scalar=-3e38,
                                    op0=ALU.add, op1=ALU.max, accum_out=s4[:, 0:1]))
                            else:
                                link(nc.vector.tensor_reduce(s4[:, 0:1], ps[:, 2 * (n % 2), 0:nk], AX_X, ALU.max))
                            nc.vector.tensor_scalar(s4[:, 1:2], s4[:, 0:1], -1.0, None, ALU.mult).then_inc(maxed, 1)
                        m = n - 1
                        if 0 <= m < U:
                            g = p * U + m
                            nj = min(4, keys(units[m][0]) // P)
                            dve.wait_ge(turned, g + 1)
                            if g >= 2:
                                dve.wait_ge(pv, g - 1)
                            nc.vector.tensor_copy(prob_t[:, m % 2, 0:nj, :].rearrange("p a c -> p (a c)"), ps[:, 4, 0:nj * P]).then_inc(pt_d, 1)
                        m = n - 2
                        if 0 <= m < U:
                            g = p * U + m
                            t, h = units[m]
                            s4 = stat[:, m % 4]
                            link(nc.vector.reciprocal(s4[:, 3:4], s4[:, 2:3]))
                            dve.wait_ge(pv, g + 1)
                            if h == 0 and g >= 4:
                                dve.wait_ge(ot, g // 2 - 1)
                            nc.vector.tensor_scalar(o[:, (m // 2) % 2, hs[h]], ps[:, 6, 0:HD], s4[:, 3:4], None, ALU.mult).then_inc(o_norm, 1)
                        m = n - 3
                        if 0 <= m < U and m % 2:
                            g = p * U + m
                            t = units[m][0]
                            dve.wait_ge(ot, (g + 1) // 2)
                            dst = self.X[:, pr["out"], t * P:(t + 1) * P]
                            if causal:
                                nc.vector.tensor_tensor(dst, ps[:, 7, 0:P], gate[:, b, t * P:(t + 1) * P], ALU.mult).then_inc(stored, 1)
                            else:
                                nc.vector.tensor_copy(dst, ps[:, 7, 0:P]).then_inc(stored, 1)
        self.split_upto = max(self.split_upto, refill.stop)
        self.phase_over()


    def phase_out_and_ffn(self, l):
        nc, ps = self.nc, self.ps
        with ExitStack() as scope:
            self.alloc_h(scope, f"f{l}")
            s0 = self.first[f"out{l}"]
            split_from, split_to = self.split_upto, s0 + KT + RING
            with ExitStack() as ctx:
                self.phase_begins(f"out{l}")
                block = ctx.enter_context(nc.Block())

                @block.sync
                def _(sp):
                    for i in range(KT):
                        self.load_strip(sp, s0 + i + RING)
                        if i == 0:
                            sp.wait_ge(self.h_hi, KT)
                            sp.wait_ge(self.h_lo, KT)
                            sp.dma_start(self.X[:], self.x_dram).then_inc(self.loaded, 16)
                    sp.wait_ge(self.loaded, 16)

                @block.gpsimd
                def _(pool):
                    for s in range(split_from, split_to):
                        self.split_strip(pool, s)

                @block.scalar
                def _(act):
                    for k in range(KT):
                        nc.scalar.activation(self.hh[:, k, :], self.X[:, k, :], ACT.Copy).then_inc(self.h_hi, 1)

                @block.vector
                def _(dve):
                    link = self.linker(dve, self.vector_link)
                    for k in range(KT):
                        dve.wait_ge(self.h_hi, k + 1)
                        nc.vector.tensor_tensor(self.hl[:, k, :], self.X[:, k, :], self.hh[:, k, :].bitcast(F32), ALU.subtract).then_inc(self.h_lo, 1)
                    dve.wait_ge(self.loaded, 16)
                    for i in range(KT):
                        dve.wait_ge(self.strip_done, s0 + i + 1)
                        nc.vector.tensor_tensor(self.X[:, i, :], self.X[:, i, :], self.bank2(i % 3), ALU.add).then_inc(self.psum_free, 1)

                @block.tensor
                def _(pe):
                    for i in range(KT):
                        if i >= 3:
                            pe.wait_ge(self.psum_free, i - 2)
                        self.gemm_strip(pe, s0 + i, i % 3, self.hh, self.hl, "fm", T,
                                        (lambda k: pe.wait_ge(self.h_lo, k + 1)) if i == 0 else None)
            self.split_upto = split_to
            self.phase_over()
            self.phase_ffn(scope, l)

    def phase_ffn(self, scope, l):
        nc, ps = self.nc, self.ps
        GM = max(FF_GROUPS)
        s0 = self.first[f"up{l}0"]
        plan, f = [], 0
        for g, n in enumerate(FF_GROUPS):
            for j in range(n):
                plan += [("gate", f, j), ("up", f, j)]
                f += 1
            plan += [("down", c, (n, f)) for c in range(KT)]
        with ExitStack() as ctx:
            ah = self.sb(ctx, f"act_hi{l}", [P, GM, T], F32R)
            al = self.sb(ctx, f"act_lo{l}", [P, GM, T], F32R)
            silu = self.sb(ctx, f"silu{l}", [P, 2, T])
            full = self.sb(ctx, f"full_f{l}", [P, 2, T])
            small = self.sb(ctx, f"small_f{l}", [P, 3, 16])
            self.phase_begins(f"ffn{l}")
            sg = self.sem
            silu_done, act_hi, act_lo = sg("silu"), sg("act_hi"), sg("act_lo")
            x_saved = self.sem("x_saved")
            block = ctx.enter_context(nc.Block())
            split_from = self.split_upto
            split_to = min(s0 + len(plan) + RING, len(self.strips))

            @block.sync
            def _(sp):
                for s in range(split_from, split_to):
                    self.load_strip(sp, s)
                if l == 0:
                    sp.wait_ge(self.psum_free, len(plan))
                    sp.dma_start(self.x_dram, self.X[:]).then_inc(x_saved, 16)
                    sp.wait_ge(x_saved, 16)

            @block.gpsimd
            def _(pool):
                self.norm_pool(pool, T, small)
                for s in range(split_from, split_to):
                    self.split_strip(pool, s)

            @block.scalar
            def _(act):
                self.norm_act(act, lambda k: self.X[:, k, :], T, silu)
                for k in range(KT):
                    act.wait_ge(self.h_full, k + 1)
                    nc.scalar.activation(self.hh[:, k, :], full[:, k % 2, :], ACT.Copy).then_inc(self.h_hi, 1)
                for i, (kind, f, j) in enumerate(plan):
                    if kind == "gate":
                        act.wait_ge(self.strip_done, s0 + i + 1)
                        if f == 0:
                            act.wait_ge(self.sums, KT)
                        if f >= 2:
                            act.wait_ge(act_hi, f - 1)
                        nc.scalar.activation(silu[:, f % 2, :], self.bank2(i % 3), ACT.Silu).then_inc(silu_done, 1)
                    elif kind == "up":
                        act.wait_ge(self.psum_free, i + 1)
                        nc.scalar.activation(ah[:, j, :], full[:, f % 2, :], ACT.Copy).then_inc(act_hi, 1)

            @block.vector
            def _(dve):
                link = self.linker(dve, self.vector_link)
                self.norm_dve_sums(dve, link, T, small, 4)
                dve.wait_ge(self.spread_done, 1)
                for k in range(KT):
                    if k >= 2:
                        dve.wait_ge(self.h_lo, k - 1)
                    nc.vector.scalar_tensor_tensor(
                        out=full[:, k % 2, :], in0=self.X[:, k, :], scalar=self.param(f"ffn_norm{l}", k),
                        in1=self.bank2(3), op0=ALU.mult, op1=ALU.mult).then_inc(self.h_full, 1)
                    dve.wait_ge(self.h_full, k + 1)
                    dve.wait_ge(self.h_hi, k + 1)
                    nc.vector.tensor_tensor(self.hl[:, k, :], full[:, k % 2, :], self.hh[:, k, :].bitcast(F32), ALU.subtract).then_inc(self.h_lo, 1)
                dve.wait_ge(self.h_lo, KT)
                for i, (kind, f, j) in enumerate(plan):
                    if kind == "up":
                        dve.wait_ge(silu_done, f + 1)
                        dve.wait_ge(self.strip_done, s0 + i + 1)
                        if f >= 2:
                            dve.wait_ge(act_lo, f - 1)
                        nc.vector.tensor_tensor(full[:, f % 2, :], silu[:, f % 2, :], self.bank2(i % 3), ALU.mult).then_inc(self.psum_free, 2)
                        dve.wait_ge(self.psum_free, i + 1)
                        dve.wait_ge(act_hi, f + 1)
                        nc.vector.tensor_tensor(al[:, j, :], full[:, f % 2, :], ah[:, j, :].bitcast(F32), ALU.subtract).then_inc(act_lo, 1)
                    elif kind == "down":
                        dve.wait_ge(self.strip_done, s0 + i + 1)
                        if j[1] != FF_GROUPS[0]:
                            dve.wait_ge(self.psum_free, i)
                        nc.vector.tensor_tensor(self.X[:, f, :], self.X[:, f, :], self.bank2(i % 3), ALU.add).then_inc(self.psum_free, 1)

            @block.tensor
            def _(pe):
                self.norm_pe(pe, T, silu, small[:, 2], 4, 6)
                for i, (kind, f, j) in enumerate(plan):
                    if i >= 3:
                        pe.wait_ge(self.psum_free, i - 2)
                    if kind != "down":
                        self.gemm_strip(pe, s0 + i, i % 3, self.hh, self.hl, "fm", T,
                                        (lambda k: pe.wait_ge(self.h_lo, k + 1)) if i == 0 else None)
                    else:
                        n, upto = j
                        self.gemm_strip(pe, s0 + i, i % 3, ah, al, "fm", T,
                                        (lambda k: pe.wait_ge(act_lo, upto - n + k + 1)) if f == 0 else None)
        self.split_upto = split_to
        self.phase_over()


    def phase_store(self):
        nc, ps = self.nc, self.ps
        with ExitStack() as ctx:
            xo = self.sb(ctx, "x_out", [P, TT, D])
            self.phase_begins("store")
            turned, even_out, odd_out = (self.sem(n) for n in ("turned", "even_out", "odd_out"))
            out_stored = self.out_stored
            block = ctx.enter_context(nc.Block())

            @block.tensor
            def _(pe):
                for t in range(TT):
                    if t >= 4:
                        pe.wait_ge((even_out if t % 2 == 0 else odd_out), (t - 4) // 2 + 1)
                    for k in range(KT):
                        mm = nc.tensor.transpose(ps[:, 2 * (t % 4) + k // 4, (k % 4) * P:(k % 4 + 1) * P],
                                                 self.X[:, k, t * P:(t + 1) * P], self.const("ident"))
                    mm.then_inc(turned, 1)

            @block.vector
            def _(dve):
                link = self.linker(dve, self.vector_link)
                for t in range(0, TT, 2):
                    dve.wait_ge(turned, t + 1)
                    nc.vector.tensor_copy(xo[:, t, :], self.bank2(t % 4)).then_inc(even_out, 1)

            @block.scalar
            def _(act):
                for t in range(1, TT, 2):
                    act.wait_ge(turned, t + 1)
                    nc.scalar.activation(xo[:, t, :], self.bank2(t % 4), ACT.Copy).then_inc(odd_out, 1)

            @block.sync
            def _(sp):
                for t in range(TT):
                    sp.wait_ge((even_out if t % 2 == 0 else odd_out), t // 2 + 1)
                    sp.dma_start(self.out[0, t * P:(t + 1) * P, :], xo[:, t, :]).then_inc(out_stored, 16)
                sp.wait_ge(out_stored, 16 * TT)


_INS = ["x", "mem", "mix_norm", "w_out", "mem_norm", "w_mem_kv", "mem_q_gain", "mem_k_gain", "ffn_norm", "w_gate_up", "w_down",
        "a_w_in", "a_mu", "a_w0", "a_w_up", "a_a0", "a_a_up", "a_g_up", "a_k_k", "a_k_a", "a_r_k", "a_lnx_g", "a_lnx_b",
        "kv_norm", "w_kv", "b_f", "k_gain", "b_w_in", "b_q_gain"]


def kernel(**inputs):
    import concourse.bacc as bacc
    from concourse.bass_utils import run_bass_kernel_spmd

    nc = bacc.Bacc("TRN2", target_bir_lowering=False, num_devices=1)
    consts, place = shape_constants()
    arrays, aps = {}, {}
    for name, a in [(n, inputs[n]) for n in _INS] + [("consts", consts), ("chunk_starts", chunk_starts())]:
        a = np.ascontiguousarray(a)
        arrays[f"in_{name}"] = a
        aps[name] = nc.dram_tensor(f"in_{name}", a.shape, F32, kind="ExternalInput").ap()
    out = nc.dram_tensor("out_x", (1, T, D), F32, kind="ExternalOutput").ap()
    program = Program(nc, aps, out)
    program.place = place
    program.build()
    result = run_bass_kernel_spmd(nc, [arrays], core_ids=[0])
    return result.results[0]["out_x"]
```

```python
from contextlib import ExitStack
import math

import numpy as np
import concourse.bass as bass
from concourse import mybir

ALU = mybir.AluOpType
ACT = mybir.ActivationFunctionType
F32 = mybir.dt.float32
F32R = mybir.dt.float32r
AX_X = mybir.AxisListType.X

P = 128
D = 1024
KT = D // P
T = 1024
TT = T // P
HALF = 512
M = 256
HD = 64
D_MAIN = 768
PAIRS = D_MAIN // P
MEM_PAIRS = 2
D_FF = 2816
FT = D_FF // P
FF_GROUPS = [6, 6, 5, 5]
D_SHIFT = 2592
C = 64
RMS_EPS = 1e-6
GN_EPS = 64e-5
DECAY = math.exp(-0.5)
SCALE = HD ** -0.5
RING = 3
B_PLAN = [("gate" if PAIRS <= c < 2 * PAIRS else "head", c) for c in [6, 7, 0, 1, 2, 3, 4, 5, 12, 13, 8, 9, 10, 11]]
KV_PLAN = [("vt", 6), ("vt", 7)] + [("keys", c) for c in range(PAIRS)] + [("vt", c) for c in range(8, 12)] + [("f", 12)]
LEVELS = 5


def shape_constants():
    i = np.arange(P)
    r, c = i[:, None], i[None, :]
    same = (r // C) == (c // C)
    cols = {
        "ident": (r == c),
        "before": same & (r < c),
        "upto": same & (r <= c),
        "pairsum": (r // HD) == (c // HD),
        "pair0": (r == c + 1) & (r % 2 == 1),
    }
    for l in range(LEVELS + 1):
        b = 1 << l
        cols[f"join{l}"] = ((c // b) % 2 == 1) & ((r // b) == (c // b) - 1)
    out = {k: v.astype(np.float32) for k, v in cols.items()}
    out["future"] = np.where(c > r, np.float32(-1e30), np.float32(0))
    out["heads"] = np.stack([(i < HD), (i >= HD)], 1).astype(np.float32)
    out["rms_eps"] = np.full((P, 1), RMS_EPS, np.float32)
    out["ones"] = np.ones((P, 1), np.float32)
    out["minus_half"] = np.full((P, 16), -0.5, np.float32)
    place, at = {}, 0
    for k, v in out.items():
        place[k] = (at, at + v.shape[1])
        at += v.shape[1]
    return np.concatenate(list(out.values()), 1), place


class Program:
    def __init__(self, nc, ins, out):
        self.nc, self.ins, self.out = nc, ins, out
        self.cleared = []
        self.taken = []
        self.ctx = ExitStack()

    def sem(self, name):
        s = self.nc.alloc_semaphore(f"{self.phase}_{name}")
        self.taken.append(s)
        return s

    def phase_begins(self, name):
        self.phase = name
        self.loaded = self.sem("loaded")
        self.squared = self.sem("squared")
        self.added = self.sem("added")
        self.sums = self.sem("sums")
        self.root = self.sem("root")
        self.rms_out = self.sem("rms_out")
        self.h_hi = self.sem("h_hi")
        self.h_lo = self.sem("h_lo")
        self.psum_free = self.sem("psum_free")
        self.vector_link = self.sem("vector_link")

    def phase_over(self):
        numbers = sorted(s.num for s in self.taken)
        first = 0
        for i in range(1, len(numbers) + 1):
            if i == len(numbers) or numbers[i] != numbers[i - 1] + 1:
                self.nc.gpsimd.sem_clear(range(numbers[first], numbers[i - 1] + 1))
                first = i
        for s in self.cleared:
            self.nc.release_semaphore(s)
        self.cleared, self.taken = self.taken, []

    def linker(self, engine, semaphore):
        done = [0]

        def link(instruction):
            done[0] += 1
            instruction.then_inc(semaphore, 1)
            engine.wait_ge(semaphore, done[0])
        return link

    def sb(self, ctx, name, shape, dt=F32):
        return ctx.enter_context(self.nc.sbuf_tensor(name, shape, dt))


    def strip(self, w, row0, tiles, col0, cols=P):
        return (w[row0:row0 + tiles * P, col0:col0 + cols].rearrange("(k p) c -> p k c", p=P), tiles, cols)

    def list_strips(self):
        i = self.ins
        s = self.strips = []
        self.first = {}

        def mark(name):
            self.first[name] = len(s)

        mark("in_a")
        self.a_plan = []
        mem = {9 + 5 * l + m: (l, m) for l in range(2) for m in range(4)}
        for c in [*range(18), 21, 22, 18, 19, 20]:
            if c < 21:
                s.append(self.strip(i["a_w_in"][0], 0, KT, c * P))
                self.a_plan.append(("shift", c))
            else:
                s.append(self.strip(i["a_w_in"][0], 0, KT, D_SHIFT + (c - 21) * P))
                self.a_plan.append(("head", c))
            if c in mem:
                l, m = mem[c]
                s.append(self.strip(i["w_mem_kv"][l], 0, KT, m * P))
                self.a_plan.append(("memk" if m < 2 else "memv", (l, m % 2)))
        for l in range(2):
            if l == 1:
                mark("kv")
                for _, c in KV_PLAN[:-1]:
                    s.append(self.strip(i["w_kv"], 0, KT, c * P))
                s.append(self.strip(i["w_kv"], 0, KT, 2 * D_MAIN, 12))
                mark("in_b")
                for _, c in B_PLAN:
                    s.append(self.strip(i["b_w_in"][0], 0, KT, c * P))
            mark(f"out{l}")
            for c in range(KT):
                s.append(self.strip(i["w_out"][l], 0, KT, c * P))
            f0 = 0
            for g, n in enumerate(FF_GROUPS):
                mark(f"up{l}{g}")
                for f in range(f0, f0 + n):
                    s.append(self.strip(i["w_gate_up"][l], 0, KT, f * P))
                    s.append(self.strip(i["w_gate_up"][l], 0, KT, D_FF + f * P))
                mark(f"down{l}{g}")
                for c in range(KT):
                    s.append(self.strip(i["w_down"][l], f0 * P, n, c * P))
                f0 += n
        self.raw_upto = 0
        self.split_upto = 0

    def load_strip(self, sp, s):
        if s >= len(self.strips):
            return
        src, tiles, cols = self.strips[s]
        if s >= RING:
            sp.wait_ge(self.w_lo, s - RING + 1)
        n = self.w_raw[s % RING]
        sp.dma_start(self.raw[:, s % RING, 0:tiles, 0:cols], src).then_inc(n, 16)

    def split_strip(self, pool, s):
        if s >= len(self.strips):
            return
        _, tiles, _ = self.strips[s]
        pool.wait_ge(self.w_raw[s % RING], 16 * (s // RING + 1))
        if s >= RING:
            pool.wait_ge(self.strip_done, s - RING + 1)
        r = s % RING
        raw = self.raw[:, r, 0:tiles, :]
        self.nc.gpsimd.tensor_copy(self.whi[:, r, 0:tiles, :], raw).then_inc(self.w_hi, 1)
        pool.wait_ge(self.w_hi, s + 1)
        self.nc.gpsimd.tensor_tensor(
            self.wlo[:, r, 0:tiles, :], raw, self.whi[:, r, 0:tiles, :].bitcast(F32), ALU.subtract).then_inc(self.w_lo, 1)

    def gemm_strip(self, pe, s, slot, hh, hl, kind="fm", width=T, before_k=None):
        nc = self.nc
        _, tiles, _ = self.strips[s]
        pe.wait_ge(self.w_lo, s + 1)
        r = s % RING
        wh, wl = self.whi[:, r], self.wlo[:, r]
        bank = self.ps
        mm = None
        if kind == "fm":
            n = min(width, HALF)
            parts = width // n
            for k in range(tiles):
                if before_k is not None:
                    before_k(k)
                for a, w in enumerate((wh, wl)):
                    for b, h in enumerate((hh, hl)[:2 - a]):
                        for j in range(parts):
                            mm = nc.tensor.matmul(bank[:, 2 * slot + j, 0:n], w[:, k, :], h[:, k, j * n:(j + 1) * n],
                                                  start=(k == 0 and a == 0 and b == 0), stop=(k == tiles - 1 and a == 1))
        else:
            for t in range(width // P):
                o = bank[:, 2 * slot + t // 4, (t % 4) * P:(t % 4 + 1) * P]
                for k in range(tiles):
                    for a, h in enumerate((hh, hl)):
                        for b, w in enumerate((wh, wl)[:2 - a]):
                            mm = nc.tensor.matmul(o, h[:, k, t * P:(t + 1) * P], w[:, k, :],
                                                  start=(k == 0 and a == 0 and b == 0), stop=(k == tiles - 1 and a == 1))
        mm.then_inc(self.strip_done, 1)


    def build(self):
        nc, ctx = self.nc, self.ctx
        with ctx:
            ins = self.ins
            self.X = self.sb(ctx, "x_res", [P, KT, T])
            n = ins["consts"].shape[1]
            self.k = self.sb(ctx, "consts_sb", [P, n])
            self.params = self.sb(ctx, "params_sb", [P, 192])
            self.ps = ctx.enter_context(nc.psum_tensor("ps", [P, 8, HALF], F32))
            dram = lambda name, shape: nc.dram_tensor(name, shape, F32, kind="Internal").ap()
            self.x_dram = dram("x_dram", (P, KT, T))
            self.u_dram = dram("u_dram", (23, P, T))
            self.kv_dram = dram("kv_dram", (13, P, T))
            self.memk_dram = dram("memk_dram", (4, P, M))
            self.memv_dram = dram("memv_dram", (4, P, M))
            self.negc_dram = dram("negc_dram", (12, T))

            self.w_raw = [ctx.enter_context(nc.semaphore(f"w_raw{r}")) for r in range(RING)]
            self.w_hi = ctx.enter_context(nc.semaphore("w_hi"))
            self.w_lo = ctx.enter_context(nc.semaphore("w_lo"))
            self.strip_done = ctx.enter_context(nc.semaphore("strip_done"))
            self.params_in = ctx.enter_context(nc.semaphore("params_in"))
            self.out_stored = ctx.enter_context(nc.semaphore("out_stored"))
            self.list_strips()
            with ExitStack() as scope:
                self.alloc_ring(scope, "a")
                self.mem_t = self.sb(scope, "mem_t", [P, KT, M])
                self.phase_load()
                self.alloc_h(scope, "a")
                self.phase_in_a(scope)
            self.phase_rwkv()
            self.alloc_ring(ctx, "b")
            self.phase_mem_attention(0, 21)
            self.phase_out_and_ffn(0)
            with ExitStack() as scope:
                self.alloc_h(scope, "b")
                self.phase_project(scope, "kv", 13, "kv_norm", 0)
                self.phase_project(scope, "in_b", 14, "mix_norm", 1)
            self.phase_fox()
            self.phase_mem_attention(1, 12)
            self.phase_out_and_ffn(1)
            self.phase_store()

    def alloc_ring(self, ctx, tag):
        self.raw = self.sb(ctx, f"w_raw_{tag}", [P, RING, KT, P])
        self.whi = self.sb(ctx, f"w_hi_{tag}", [P, RING, KT, P], F32R)
        self.wlo = self.sb(ctx, f"w_lo_{tag}", [P, RING, KT, P], F32R)

    def alloc_h(self, ctx, tag):
        self.hh = self.sb(ctx, f"h_hi_{tag}", [P, KT, T], F32R)
        self.hl = self.sb(ctx, f"h_lo_{tag}", [P, KT, T], F32R)

    def const(self, name):
        a, b = self.place[name]
        return self.k[:, a:b]

    def mask(self, name, n):
        return self.const(name).rearrange("p (a c) -> p a c", a=1).broadcast_to([P, n, P])

    def mask4(self, name):
        return self.const(name).rearrange("p (a b c) -> p a b c", a=1, b=1).broadcast_to([P, 2, 2, P])


    def phase_load(self):
        nc, ins, ps = self.nc, self.ins, self.ps
        with ExitStack() as scope:
            xin = self.sb(scope, "x_in", [P, TT + M // P, D])
            stage = self.sb(scope, "param_rows", [P, P])
            self.phase_begins("load")
            consts_in, stage_zero = self.sem("consts_in"), self.sem("stage_zero")
            turned, params_turned = self.sem("turned"), self.sem("params_turned")
            tile_in = [self.sem(f"tile_in{t}") for t in range(TT + M // P)]
            rows_in = self.sem("rows_in")
            even_out, odd_out = self.sem("even_out"), self.sem("odd_out")
            block = scope.enter_context(nc.Block())

            self.place_params = {}
            loads = []
            at = 0

            def vec(name, ap, tiles):
                nonlocal at
                self.place_params[name] = at
                loads.append((at, tiles, slice(0, P), ap.rearrange("(n p) -> n p", p=P)))
                at += tiles

            for l in range(2):
                vec(f"mix_norm{l}", ins["mix_norm"][l], KT)
                vec(f"mem_norm{l}", ins["mem_norm"][l], KT)
                vec(f"ffn_norm{l}", ins["ffn_norm"][l], KT)
            vec("kv_norm0", ins["kv_norm"], KT)
            vec("mu", ins["a_mu"][0][0:20 * P], 20)
            for name in ("a_w0", "a_a0", "a_k_k", "a_k_a", "a_lnx_g", "a_lnx_b"):
                vec(name, ins[name][0], PAIRS)
            vec("a_r_k", ins["a_r_k"][0].rearrange("h d -> (h d)"), PAIRS)
            self.place_params["mu_last"] = at
            loads.append((at, 1, slice(0, 32), ins["a_mu"][0][20 * P:D_SHIFT].rearrange("(n p) -> n p", p=32)))
            mu_last = at
            at += 1
            for name, ap in (("mem_q_gain0", ins["mem_q_gain"][0]), ("mem_q_gain1", ins["mem_q_gain"][1]),
                             ("mem_k_gain0", ins["mem_k_gain"][0]), ("mem_k_gain1", ins["mem_k_gain"][1]),
                             ("k_gain", ins["k_gain"]), ("b_q_gain", ins["b_q_gain"][0])):
                self.place_params[name] = at
                for h in range(2):
                    loads.append((at, 1, slice(h * HD, (h + 1) * HD), ap.rearrange("(n p) -> n p", p=HD)))
                at += 1
            self.place_params["b_f"] = at
            loads.append((at, 1, slice(0, 12), ins["b_f"].rearrange("(n p) -> n p", p=12)))
            at += 1
            rows = at
            assert rows <= P
            self.place_params["one_minus_mu"] = at
            at += 21
            assert at <= 192

            def turned_to(t):
                return self.X[:, :, t * P:(t + 1) * P] if t < TT else self.mem_t[:, :, (t - TT) * P:(t - TT + 1) * P]

            @block.sync
            def _(sp):
                for t in range(TT):
                    sp.dma_start(xin[:, t, :], ins["x"][0, t * P:(t + 1) * P, :]).then_inc(tile_in[t], 16)
                for t in range(M // P):
                    sp.dma_start(xin[:, TT + t, :], ins["mem"][0, t * P:(t + 1) * P, :]).then_inc(tile_in[TT + t], 16)
                for s in range(RING):
                    self.load_strip(sp, s)
            @block.scalar
            def _(act):
                act.dma_start(self.k[:], ins["consts"]).then_inc(consts_in, 16)
                act.wait_ge(stage_zero, 1)
                for row, n, cols, src in loads[1::2]:
                    act.dma_start(stage[row:row + n, cols], src).then_inc(rows_in, 16)
                for t in range(1, TT + M // P, 2):
                    act.wait_ge(turned, t + 1)
                    nc.scalar.activation(turned_to(t),
                                                         ps[:, 2 * (t % 4):2 * (t % 4) + 2, :].rearrange("p b (k c) -> p (b k) c", c=P), ACT.Copy).then_inc(odd_out, 1)

            @block.vector
            def _(dve):
                link = self.linker(dve, self.vector_link)
                nc.vector.memset(stage[:], 0.0).then_inc(stage_zero, 1)
                for t in range(0, TT + M // P, 2):
                    dve.wait_ge(turned, t + 1)
                    nc.vector.tensor_copy(turned_to(t),
                                                          ps[:, 2 * (t % 4):2 * (t % 4) + 2, :].rearrange("p b (k c) -> p (b k) c", c=P)).then_inc(even_out, 1)
                dve.wait_ge(params_turned, 1)
                link(nc.vector.tensor_copy(self.params[:, 0:rows], ps[:, 4, 0:rows]))
                for name in ("mem_q_gain0", "mem_q_gain1", "b_q_gain"):
                    nc.vector.tensor_scalar(self.param(name), self.param(name), SCALE, None, ALU.mult)
                o, m = self.place_params["one_minus_mu"], self.place_params["mu"]
                nc.vector.tensor_scalar(self.params[:, o:o + 20], self.params[:, m:m + 20], -1.0, 1.0, ALU.mult, ALU.add)
                nc.vector.tensor_scalar(self.params[:, o + 20:o + 21], self.params[:, mu_last:mu_last + 1],
                                                        -1.0, 1.0, ALU.mult, ALU.add).then_inc(stage_zero, 1)

            @block.tensor
            def _(pe):
                pe.wait_ge(consts_in, 16)
                for t in range(TT + M // P):
                    pe.wait_ge(tile_in[t], 16)
                    if t >= 4:
                        pe.wait_ge((even_out if t % 2 == 0 else odd_out), (t - 4) // 2 + 1)
                    for k in range(KT):
                        mm = nc.tensor.transpose(ps[:, 2 * (t % 4) + k // 4, (k % 4) * P:(k % 4 + 1) * P],
                                                 xin[:, t, k * P:(k + 1) * P], self.const("ident"))
                    mm.then_inc(turned, 1)
                pe.wait_ge(self.params_in, 16 * len(loads[0::2]))
                pe.wait_ge(rows_in, 16 * len(loads[1::2]))
                pe.wait_ge(even_out, TT // 2)
                nc.tensor.transpose(ps[:, 4, 0:rows], stage[0:rows, :], self.const("ident")[0:rows, 0:rows]).then_inc(params_turned, 1)

            @block.gpsimd
            def _(pool):
                pool.wait_ge(stage_zero, 1)
                for row, n, cols, src in loads[0::2]:
                    pool.dma_start(stage[row:row + n, cols], src).then_inc(self.params_in, 16)
                self.split_strip(pool, 0)

        self.split_upto, self.raw_upto = 1, RING
        self.phase_over()

    def param(self, name, i=0):
        a = self.place_params[name] + i
        return self.params[:, a:a + 1]


    def norm_act(self, act, gain, sq):
        for k in range(KT):
            self.nc.scalar.activation(self.hh[:, k, :], self.X[:, k, :], ACT.Copy, scale=self.param(gain, k)).then_inc(self.h_hi, 1)
        for k in range(KT):
            if k >= 2:
                act.wait_ge(self.added, max(k - 2, 1))
            self.nc.scalar.activation(sq[:, k % 2, :], self.X[:, k, :], ACT.Square).then_inc(self.squared, 1)
        act.wait_ge(self.sums, 1)
        self.nc.scalar.activation(sq[:, 0, :], self.bank2(3), ACT.Sqrt, scale=1.0 / D, bias=self.const("rms_eps")).then_inc(self.root, 1)

    def norm_dve(self, dve, gain, sq, rms):
        nc, ps = self.nc, self.ps
        for k in range(KT):
            dve.wait_ge(self.h_hi, k + 1)
            nc.vector.scalar_tensor_tensor(out=self.hl[:, k, :], in0=self.X[:, k, :], scalar=self.param(gain, k),
                                           in1=self.hh[:, k, :].bitcast(F32), op0=ALU.mult, op1=ALU.subtract).then_inc(self.h_lo, 1)
        for k in range(1, KT):
            dve.wait_ge(self.squared, k + 1)
            if k > 1:
                dve.wait_ge(self.added, k - 1)
            nc.vector.tensor_tensor(rms[:], sq[:, 0, :] if k == 1 else rms[:], sq[:, k % 2, :], ALU.add).then_inc(self.added, 1)
        dve.wait_ge(self.root, 1)
        nc.vector.reciprocal(rms[:], sq[:, 0, :]).then_inc(self.rms_out, 1)
        dve.wait_ge(self.rms_out, 1)

    def norm_before(self, pe, i, rms):
        def before(k):
            if i == 0:
                pe.wait_ge(self.h_lo, k + 1)
            elif k == 0:
                pe.wait_ge(self.added, KT - 1)
                for j in range(2):
                    mm = self.nc.tensor.matmul(self.ps[:, 6 + j, :], self.const("ones").broadcast_to([P, P]),
                                               rms[:, j * HALF:(j + 1) * HALF], start=True, stop=True)
                mm.then_inc(self.sums, 1)
        return before if i in (0, 2) else None


    def phase_in_a(self, scope):
        plan = self.a_plan
        with ExitStack() as ctx:
            self.mem_h = [self.sb(ctx, f"mem_{n}", [P, KT, M], F32R) for n in ("hi", "lo")]
            self.mem_rms = self.sb(ctx, "mem_rms", [P, M])
            self.mem_small = self.sb(ctx, "mem_small", [P, 3, 2])
            work = self.norm_work(ctx, "a")
            self.phase_begins("in_a")
            block = ctx.enter_context(self.nc.Block())
            self.norm_and_gemm(block, "in_a", plan, work, "mix_norm0")
        self.phase_over()

    def norm_work(self, ctx, name):
        return dict(sq=self.sb(ctx, f"sq_{name}", [P, 2, T]), 
                    rms=self.sb(ctx, f"rms_{name}", [P, T]), scaled=self.sb(ctx, f"scaled_{name}", [P, 2, T]),
                    evac=self.sb(ctx, f"evac_{name}", [P, 3, T]))

    def norm_and_gemm(self, block, name, plan, work, gain):
        nc, ps = self.nc, self.ps
        sq, rms, scaled, evac = (work[n] for n in ("sq", "rms", "scaled", "evac"))
        n, s0 = len(plan), self.first[name]
        split_from = self.split_upto
        has_mem = plan is self.a_plan
        load_from, load_to = self.raw_upto, s0 + n + (0 if has_mem else RING)
        split_to = s0 + n + (0 if has_mem else RING - 1)
        save_x = has_mem or name == "kv"
        sem = self.sem
        stored = [sem(f"stored{r}") for r in range(3)]
        shifted, formed = sem("shifted"), sem("formed")
        v_turned, act_formed = sem("v_turned"), sem("act_formed")
        head_sq, head_sums, head_root, head_rn, head_out = (sem("head_" + m) for m in ("sq", "sums", "root", "rn", "out"))
        gate_in, soft = sem("gate_in"), sem("soft")
        mem_sq, mem_sums, mem_ms, mem_rn, mem_bc, mem_hi, mem_lo, mem_out = (
            sem("mem_" + m) for m in ("sq", "sums", "ms", "rn", "bc", "hi", "lo", "out"))
        kinds = [kind for kind, _ in plan]
        before = lambda i, kind: kinds[:i].count(kind)
        heads = [i for i in range(n) if kinds[i] in ("head", "keys", "memk")]
        assert 2 <= heads[0] and heads[-1] < n - 2
        turned_after = lambda i: [v for v in range(n) if kinds[v] == "vt" and i == (v + 2 if v < 2 else v + 1)]
        turned_before = lambda i: sum(len(turned_after(e)) for e in range(i))

        def head_gain(i):
            kind, c = plan[i]
            if kind == "keys":
                return self.param("k_gain")
            if kind == "memk":
                return self.param(f"mem_k_gain{c[0]}")
            if has_mem:
                return self.param("mem_q_gain0")
            return self.param("b_q_gain" if c < PAIRS else "mem_q_gain1")
        if has_mem:
            mem_of = [[i for i, (kind, c) in enumerate(plan) if kind in ("memk", "memv") and c[0] == l] for l in range(2)]
            mem_prep = {3: 0, mem_of[0][-1] + 1: 1}
            MEM_SUM, MEM_SPREAD = 4, 7
        else:
            mem_prep, MEM_SUM, MEM_SPREAD = {}, n, n

        def target(i):
            kind, c = plan[i]
            if kind in ("shift", "head", "gate"):
                return self.u_dram[c], evac[:, i % 3, :]
            if kind in ("keys", "vt"):
                return self.kv_dram[c], evac[:, i % 3, :]
            if kind == "f":
                return self.negc_dram, evac[0:12, i % 3, :]
            d = self.memk_dram if kind == "memk" else self.memv_dram
            return d[2 * c[0] + c[1]], evac[:, i % 3, 0:M]

        @block.sync
        def _(sp):
            for i in range(n + 2):
                if load_from <= s0 + i + RING < load_to:
                    self.load_strip(sp, s0 + i + RING)
                if i == 0 and save_x:
                    sp.dma_start(self.x_dram, self.X[:]).then_inc(self.loaded, 16)
                i -= 2
                if i < 0:
                    continue
                if kinds[i] in ("vt", "gate"):
                    sp.wait_ge(act_formed, before(i, kinds[i]) + 1)
                elif kinds[i] == "shift":
                    sp.wait_ge(formed, before(i, "shift") + 1)
                elif i in heads:
                    sp.wait_ge(head_out, heads.index(i) + 1)
                else:
                    sp.wait_ge(self.psum_free, i + 1)
                dst, src = target(i)
                sp.dma_start(dst, src).then_inc(stored[i % 3], 16)
            if save_x:
                sp.wait_ge(self.loaded, 16)
            for r in range(3):
                sp.wait_ge(stored[r], 16 * len(range(r, n, 3)))

        @block.gpsimd
        def _(pool):
            for s in range(split_from, split_to):
                if has_mem and s == s0 + RING + MEM_SUM + 2:
                    pool.wait_ge(mem_ms, 1)
                    nc.gpsimd.tensor_tensor(self.mem_small[:, 2, :], self.mem_small[:, 1, :], self.const("minus_half")[:, 0:2], ALU.pow).then_inc(mem_rn, 1)
                self.split_strip(pool, s)

        @block.scalar
        def _(act):
            link = self.linker(act, soft)
            self.norm_act(act, gain, sq)
            for i, (kind, c) in enumerate(plan):
                if i in mem_prep:
                    l = mem_prep[i]
                    if l == 0:
                        act.wait_ge(self.rms_out, 1)
                        for b in range(2):
                            nc.scalar.activation(sq[:, b, :], self.mem_t[:, 4 * b:4 * b + 4, :].rearrange("p k m -> p (k m)"), ACT.Square).then_inc(mem_sq, 1)
                    else:
                        act.wait_ge(self.strip_done, s0 + mem_of[0][-1] + 1)
                    for k in range(KT):
                        q = nc.scalar.activation(self.mem_h[0][:, k, :], self.mem_t[:, k, :], ACT.Copy, scale=self.param(f"mem_norm{l}", k))
                    q.then_inc(mem_hi, 1)
                if kind == "shift":
                    act.wait_ge(self.psum_free, i + 1)
                    if i >= 3:
                        act.wait_ge(stored[i % 3], 16 * (i // 3))
                    nc.scalar.activation(evac[:, i % 3, :], scaled[:, before(i, "shift") % 2, :], ACT.Copy,
                                         scale=self.param("one_minus_mu", c)).then_inc(shifted, 1)
                if kind == "gate":
                    act.wait_ge(self.psum_free, i + 1)
                    nc.scalar.activation(evac[:, i % 3, :], evac[:, i % 3, :], ACT.Sigmoid).then_inc(act_formed, 1)
                if i in heads:
                    j, w = heads.index(i), M if kind == "memk" else T
                    act.wait_ge(self.psum_free, i + 1)
                    if j == 0:
                        act.wait_ge(self.rms_out, 1)
                        if has_mem:
                            act.wait_ge(mem_sums, 1)
                    if j >= 2:
                        act.wait_ge(head_out, j - 1)
                    nc.scalar.activation(sq[:, j % 2, 0:w], evac[:, i % 3, 0:w], ACT.Square).then_inc(head_sq, 1)
                for v in turned_after(i):
                    act.wait_ge(v_turned, before(v, "vt") + 1)
                    if v >= 3:
                        act.wait_ge(stored[v % 3], 16 * (v // 3))
                    nc.scalar.activation(evac[:, v % 3, :], self.bank2(3), ACT.Copy).then_inc(act_formed, 1)
                if i in heads:
                    act.wait_ge(head_sums, j + 1)
                    nc.scalar.activation(sq[:, j % 2, 0:w], self.bank2(3)[:, 0:w], ACT.Sqrt, scale=1.0 / HD,
                                         bias=self.const("rms_eps")).then_inc(head_root, 1)
                if kind == "f":
                    act.wait_ge(gate_in, 2)
                    link(nc.scalar.activation(sq[0:12, 0, :], sq[0:12, 1, :], ACT.Abs))
                    link(nc.scalar.activation(sq[0:12, 0, :], sq[0:12, 0, :], ACT.Exp, scale=-1.0))
                    nc.scalar.activation(sq[0:12, 0, :], sq[0:12, 0, :], ACT.Ln, bias=1.0).then_inc(soft, 1)

        @block.vector
        def _(dve):
            link = self.linker(dve, self.vector_link)

            if "f" in kinds:
                link(nc.vector.memset(self.ones_row, 1.0))
            self.norm_dve(dve, gain, sq, rms)
            for i, (kind, c) in enumerate(plan):
                if i in mem_prep:
                    l = mem_prep[i]
                    dve.wait_ge(mem_hi, l + 1)
                    for k in range(KT):
                        q = nc.vector.scalar_tensor_tensor(out=self.mem_h[1][:, k, :], in0=self.mem_t[:, k, :], scalar=self.param(f"mem_norm{l}", k),
                                                           in1=self.mem_h[0][:, k, :].bitcast(F32), op0=ALU.mult, op1=ALU.subtract)
                    q.then_inc(mem_lo, 1)
                if i == MEM_SUM + 1 and has_mem:
                    dve.wait_ge(mem_sums, 1)
                    link(nc.vector.tensor_reduce(self.mem_small[:, 0, :], ps[:, 6, 0:2 * KT].rearrange("p (k t) -> p t k", k=KT), AX_X, ALU.add))
                    nc.vector.tensor_scalar(self.mem_small[:, 1, :], self.mem_small[:, 0, :], 1.0 / D, RMS_EPS, ALU.mult, ALU.add).then_inc(mem_ms, 1)
                if i == MEM_SPREAD + 1 and has_mem:
                    dve.wait_ge(mem_bc, 1)
                    nc.vector.tensor_copy(self.mem_rms[:], ps[:, 6, 0:M]).then_inc(mem_out, 1)
                    dve.wait_ge(mem_out, 1)
                dve.wait_ge(self.strip_done, s0 + i + 1)
                out, u = evac[:, i % 3, :], self.bank2(i % 3)
                if i >= 3 and kind not in ("shift", "vt"):
                    dve.wait_ge(stored[i % 3], 16 * (i // 3))
                if kind == "shift":
                    mu = self.param("mu", c) if c < 20 else self.param("mu_last")
                    j = before(i, "shift")
                    nc.vector.tensor_tensor(scaled[:, j % 2, :], u, rms[:], ALU.mult).then_inc(self.psum_free, 1)
                    dve.wait_ge(self.psum_free, i + 1)
                    dve.wait_ge(shifted, j + 1)
                    nc.vector.scalar_tensor_tensor(
                        out=out[:, 1:T], in0=scaled[:, j % 2, 0:T - 1], scalar=mu, in1=out[:, 1:T], op0=ALU.mult, op1=ALU.add).then_inc(formed, 1)
                elif kind == "memk":
                    nc.vector.tensor_tensor(out[:, 0:M], ps[:, 2 * (i % 3), 0:M], self.mem_rms[:], ALU.mult).then_inc(self.psum_free, 1)
                elif kind == "memv":
                    for t in range(2):
                        q = nc.vector.tensor_scalar(out[:, t * P:(t + 1) * P], ps[:, 2 * (i % 3), t * P:(t + 1) * P],
                                                    self.mem_small[:, 2, t:t + 1], None, ALU.mult)
                    q.then_inc(self.psum_free, 1)
                elif kind == "vt":
                    j = before(i, "vt")
                    if j >= 2:
                        dve.wait_ge(v_turned, j - 1)
                    nc.vector.tensor_tensor(scaled[:, j % 2, :], u, rms[:], ALU.mult).then_inc(self.psum_free, 1)
                elif kind == "f":
                    nc.vector.tensor_tensor(sq[0:12, 1, :], u[0:12, :], rms[0:12, :], ALU.mult).then_inc(gate_in, 1)
                    dve.wait_ge(gate_in, 1)
                    nc.vector.tensor_scalar(sq[0:12, 1, :], sq[0:12, 1, :], self.param("b_f")[0:12, :], None, ALU.add).then_inc(gate_in, 1)
                    dve.wait_ge(gate_in, 2)
                    dve.wait_ge(soft, 3)
                    link(nc.vector.scalar_tensor_tensor(out=sq[0:12, 1, :], in0=sq[0:12, 1, :], scalar=0.0,
                                                        in1=sq[0:12, 0, :], op0=ALU.min, op1=ALU.subtract))
                    nc.vector.tensor_tensor_scan(out[0:12, :], self.ones_row, sq[0:12, 1, :], 0.0,
                                                 ALU.mult, ALU.subtract).then_inc(self.psum_free, 1)
                else:
                    nc.vector.tensor_tensor(out, u, rms[:], ALU.mult).then_inc(self.psum_free, 1)
                if i in heads:
                    j, w = heads.index(i), M if kind == "memk" else T
                    dve.wait_ge(head_root, j + 1)
                    nc.vector.reciprocal(sq[:, j % 2, 0:w], sq[:, j % 2, 0:w]).then_inc(head_rn, 1)
                    dve.wait_ge(head_rn, j + 1)
                    nc.vector.scalar_tensor_tensor(out=out[:, 0:w], in0=out[:, 0:w], scalar=head_gain(i), in1=sq[:, j % 2, 0:w],
                                                   op0=ALU.mult, op1=ALU.mult).then_inc(head_out, 1)

        @block.tensor
        def _(pe):
            def head_sum(i):
                j, w = heads.index(i), M if kinds[i] == "memk" else T
                pe.wait_ge(head_sq, j + 1)
                pe.wait_ge(head_root, j)
                if turned_before(i + 1):
                    pe.wait_ge(act_formed, turned_before(i + 1))
                for at in range(0, w, HALF):
                    mm = nc.tensor.matmul(ps[:, 6 + at // HALF, 0:min(HALF, w)], self.const("pairsum"), sq[:, j % 2, at:min(at + HALF, w)], start=True, stop=True)
                mm.then_inc(head_sums, 1)

            def before_k(i):
                norm = self.norm_before(pe, i, rms)

                def before(k):
                    if norm:
                        norm(k)
                    if k == 4 and i - 1 in heads:
                        head_sum(i - 1)
                return before

            for i, (kind, c) in enumerate(plan):
                if i >= 3:
                    pe.wait_ge(self.psum_free, i - 2)
                if kind in ("memk", "memv"):
                    pe.wait_ge(mem_lo, c[0] + 1)
                    self.gemm_strip(pe, s0 + i, i % 3, self.mem_h[0], self.mem_h[1], "fm" if kind == "memk" else "tm", M)
                    if i - 1 in heads:
                        head_sum(i - 1)
                else:
                    self.gemm_strip(pe, s0 + i, i % 3, self.hh, self.hl, "fm", T, before_k(i))
                for v in turned_after(i):
                    j = before(v, "vt")
                    pe.wait_ge(self.psum_free, v + 1)
                    pe.wait_ge(act_formed, j)
                    pe.wait_ge(head_root, sum(1 for h in heads if h + 1 <= i))
                    for t in range(TT):
                        mm = nc.tensor.transpose(ps[:, 6 + t // 4, (t % 4) * P:(t % 4 + 1) * P], scaled[:, j % 2, t * P:(t + 1) * P], self.const("ident"))
                    mm.then_inc(v_turned, 1)
                if i == MEM_SUM:
                    pe.wait_ge(mem_sq, 2)
                    pe.wait_ge(self.rms_out, 1)
                    for k in range(KT):
                        for t in range(2):
                            at = (k % 4) * M + t * P
                            mm = nc.tensor.matmul(ps[:, 6, 2 * k + t:2 * k + t + 1], sq[:, k // 4, at:at + P], self.const("ones"), start=True, stop=True)
                    mm.then_inc(mem_sums, 1)
                if i == MEM_SPREAD:
                    pe.wait_ge(mem_rn, 1)
                    for t in range(2):
                        mm = nc.tensor.matmul(ps[:, 6, t * P:(t + 1) * P], self.mem_small[:, 2, t:t + 1].broadcast_to([P, P]),
                                              self.const("ident"), start=True, stop=True)
                    mm.then_inc(mem_bc, 1)

        self.split_upto, self.raw_upto = split_to, load_to

    def bank2(self, slot):
        return self.ps[:, 2 * slot:2 * slot + 2, :].rearrange("p b c -> p (b c)")

    def phase_project(self, scope, name, n, gain, layer):
        plan = {"kv": KV_PLAN, "in_b": B_PLAN}[name]
        with ExitStack() as ctx:
            work = self.norm_work(ctx, name)
            if name == "kv":
                ones = self.sb(ctx, "ones_row", [12, T])
                self.ones_row = ones[:]
            self.phase_begins(name)
            block = ctx.enter_context(self.nc.Block())
            self.norm_and_gemm(block, name, plan, work, f"{gain}{layer}")
        self.phase_over()


    def phase_rwkv(self):
        nc, ins, ps = self.nc, self.ins, self.ps
        STEPS = T // 256
        S = PAIRS * STEPS
        NC = T // C
        with ExitStack() as ctx:
            sb = lambda name, shape: self.sb(ctx, name, shape)
            self.phase_begins("rwkv")
            sem = self.sem
            lora = sb("lora_wa", [P, T])
            gate0 = sb("lora_g0", [P, T])
            gate1 = sb("lora_g1", [32, T])
            up_wa = sb("up_wa", [P, D_MAIN])
            up_g0 = sb("up_g0", [P, D_MAIN])
            up_g1 = sb("up_g1", [32, D_MAIN])
            ones = sb("ones_c", [P, C])
            r, k, v, kk, a, g, bonus, y = (sb(n, [P, 2, T]) for n in ("r", "k", "v", "kk", "a", "g", "bonus", "y"))
            state = sb("state", [P, 2, NC + 1, HD])
            chunk_decay = sb("chunk_decay", [P, 2, NC])
            cum = sb("cum", [P, T])
            dec = sb("dec", [P, NC, C + 1])
            tmp, sq = sb("tmp", [P, T]), sb("sq_r", [P, T])
            small, small_gn = sb("small_r", [P, 2, 16]), sb("small_gn", [P, 2, 16])
            tok = sb("tok", [P, 3, 4, 2, P])
            m_a = sb("m_a", [P, 2, 2, 3, 2, P])
            m_r = sb("m_r", [P, 3, 2, 2, 2, P])
            join = sb("join", [P, 2, 4, P])
            inv_m, inv_t, um = sb("inv_m", [P, 4, P]), sb("inv_t", [P, 4, P]), sb("um", [P, 4, P])
            mv, abar, vbar, sa = sb("mv", [P, 4, HD]), sb("abar", [P, 2, P]), sb("vbar", [P, 4, HD]), sb("sa", [P, 2, P])
            stmp = sb("stmp", [P, HD])

            lora_in = sem("lora_in")
            kv_in, r_in = sem("kv_in"), sem("r_in")
            lora_ready = sem("lora_ready")
            z_mm, z_act = sem("z_mm"), sem("z_act")
            a_mm, a_act = sem("a_mm"), sem("a_act")
            g_mm, g_act = sem("g_mm"), sem("g_act")
            kk_raw, kk_sq, kk_sum = sem("kk_raw"), sem("kk_sq"), sem("kk_sum")
            kk_ms, kk_rn, kk_bc = sem("kk_ms"), sem("kk_rn"), sem("kk_bc")
            kk_used = sem("kk_used")
            cum_done, dec_done = sem("cum_done"), sem("dec_done")
            rk_done, rk_sum, bonus_done, feat = sem("rk_done"), sem("rk_sum"), sem("bonus_done"), sem("feat")
            piece_mm = sem("piece_mm")
            piece_act, piece_dve = sem("piece_act"), sem("piece_dve")
            join_done, x0 = sem("join_done"), sem("x0")
            xm_done, xm_added = sem("xm_done"), sem("xm_added")
            u_done, u_copied, xt_done, xt_added = sem("u_done"), sem("u_copied"), sem("xt_done"), sem("xt_added")
            mv_done, mv_copied, bars_done, bars_copied = sem("mv_done"), sem("mv_copied"), sem("bars_done"), sem("bars_copied")
            sa_done, sa_added, st_done, st_new = sem("sa_done"), sem("sa_added"), sem("st_done"), sem("st_new")
            y_done, y_copied = sem("y_done"), sem("y_copied")
            gn_mean, gn_centred, gn_sq, gn_sum = sem("gn_mean"), sem("gn_centred"), sem("gn_sq"), sem("gn_sum")
            gn_ms, gn_rn, gn_bc, gn_scaled, pair_done = sem("gn_ms"), sem("gn_rn"), sem("gn_bc"), sem("gn_scaled"), sem("pair_done")
            block = ctx.enter_context(nc.Block())

            ident = self.const("ident")
            halves = [(0, slice(0, HD)), (1, slice(HD, P))]
            flat = lambda t: t.rearrange("p a c -> p (a c)")
            chunks = lambda t: t.rearrange("p (c n) -> p c n", n=C)
            dec_before = dec[:, :, 0:C]
            dec_upto = dec[:, :, 1:C + 1]
            side = ps[:, 6:8, :].rearrange("p b c -> p (b c)")

            @block.sync
            def _(sp):
                for dst, src in ((lora[:], self.u_dram[18]), (gate0[:], self.u_dram[19]), (gate1[:], self.u_dram[20][0:32, :]),
                                 (up_wa[0:HD, :], ins["a_w_up"][0]), (up_wa[HD:P, :], ins["a_a_up"][0]),
                                 (up_g0[:], ins["a_g_up"][0][0:P, :]), (up_g1[:], ins["a_g_up"][0][P:160, :])):
                    sp.dma_start(dst, src).then_inc(lora_in, 16)
                for p in range(PAIRS):
                    if p >= 1:
                        sp.wait_ge(kv_in, 32 * p)
                        sp.wait_ge(r_in, 16 * p)
                    if p >= 2:
                        sp.wait_ge(piece_mm, 8 * STEPS * (p - 1))
                        sp.wait_ge(bonus_done, p - 1)
                    sp.dma_start(k[:, p % 2, :], self.u_dram[6 + p]).then_inc(kv_in, 16)
                    sp.dma_start(v[:, p % 2, :], self.u_dram[12 + p]).then_inc(kv_in, 16)
                    if p >= 2:
                        sp.wait_ge(y_done, STEPS * (p - 1))
                    sp.dma_start(r[:, p % 2, :], self.u_dram[p]).then_inc(r_in, 16)

            @block.tensor
            def _(pe):
                mmul = nc.tensor.matmul

                def side_halves(parts, semaphore):
                    for j in range(2):
                        for i, (w, x) in enumerate(parts):
                            mm = mmul(ps[:, 6 + j, :], w, x[:, j * HALF:(j + 1) * HALF], start=(i == 0), stop=(i == len(parts) - 1))
                    mm.then_inc(semaphore, 1)

                def head_sums(semaphore):
                    for t in range(TT):
                        mm = mmul(ps[:, 6, 2 * t:2 * t + 2], sq[:, t * P:(t + 1) * P], self.const("heads"), start=True, stop=True)
                    mm.then_inc(semaphore, 1)

                def prepare(p, stage):
                    cols = slice(p * P, (p + 1) * P)
                    if stage == "z":
                        pe.wait_ge(g_act, p)
                        side_halves([(up_wa[0:HD, cols], lora[0:HD, :])], z_mm)
                    elif stage == "a":
                        pe.wait_ge(z_act, p + 1)
                        side_halves([(up_wa[HD:P, cols], lora[HD:P, :])], a_mm)
                    elif stage == "kk_sum":
                        pe.wait_ge(a_act, p + 1)
                        pe.wait_ge(kk_sq, p + 1)
                        head_sums(kk_sum)
                    elif stage == "kk_bc":
                        pe.wait_ge(kk_rn, p + 1)
                        if p >= 2:
                            pe.wait_ge(gn_centred, p - 1)
                        self.spread(small[:, 1, :], 3).then_inc(kk_bc, 1)
                    elif stage == "rk":
                        pe.wait_ge(rk_done, p + 1)
                        pe.wait_ge(kk_used, p + 1)
                        if p >= 2:
                            pe.wait_ge(gn_scaled, p - 1)
                        side_halves([(self.const("pairsum"), tmp)], rk_sum)
                    elif stage == "g":
                        pe.wait_ge(bonus_done, p + 1)
                        side_halves([(up_g0[:, cols], gate0), (up_g1[:, cols], gate1)], g_mm)

                def group_norm(p, stage):
                    if stage == "mean":
                        pe.wait_ge(y_copied, STEPS * (p + 1))
                        pe.wait_ge(g_act, min(p + 2, PAIRS))
                        pe.wait_ge(gn_scaled, p)
                        if p + 2 < PAIRS:
                            pe.wait_ge(kk_ms, p + 3)
                        side_halves([(self.const("pairsum"), y[:, p % 2, :])], gn_mean)
                    elif stage == "sum":
                        pe.wait_ge(gn_sq, p + 1)
                        if p + 2 < PAIRS:
                            pe.wait_ge(kk_used, p + 3)
                        head_sums(gn_sum)
                    elif stage == "bc":
                        pe.wait_ge(gn_rn, p + 1)
                        self.spread(small_gn[:, 1, :], 3).then_inc(gn_bc, 1)

                def piece(s, i):
                    p, q = s // STEPS, s % STEPS
                    b = p % 2
                    if i == 0 and q == 0:
                        pe.wait_ge(feat, p + 1)
                    if i in (1, 2):
                        pe.wait_ge(piece_act, 2 * s + i)
                    else:
                        pe.wait_ge(piece_dve, 6 * s + max(i - 2, 0))
                    if i == 0 and s:
                        pe.wait_ge(mv_copied, s - 1)
                    tiles = (2 * q, 2 * q + 1)
                    if i < 2:
                        for n, src in enumerate(((kk, a), (k, v))[i]):
                            for t in range(2):
                                c = tiles[t] * P
                                mm = nc.tensor.transpose(ps[:, 3, (2 * n + t) * P:(2 * n + t + 1) * P], src[:, b, c:c + P], ident)
                    else:
                        h = halves[(i - 2) // 3][1]
                        products = (((a, kk), (k, kk)), ((kk, a),), ((a, r), (k, r)))[(i - 2) % 3]
                        for n, (w, x) in enumerate(products):
                            for t in range(2):
                                c = slice(tiles[t] * P, (tiles[t] + 1) * P)
                                mm = mmul(ps[:, 3, (2 * n + t) * P:(2 * n + t + 1) * P], w[h, b, c], x[h, b, c], start=True, stop=True)
                    mm.then_inc(piece_mm, 1)

                pe.wait_ge(lora_ready, 1)
                for stage in ("z", "a", "kk_sum", "kk_bc", "rk", "g"):
                    prepare(0, stage)
                for i in range(8):
                    piece(0, i)
                for s in range(S + 1):
                    p, q = s // STEPS, s % STEPS
                    side_work = {(0, 1): "z", (0, 2): "a", (0, 4): "kk_sum", (1, 3): "kk_bc", (2, 3): "rk", (2, 5): "g"}
                    gn_work = {(1, 1): "mean", (1, 5): "sum", (2, 1): "bc"}
                    o, op, oq = s - 1, (s - 1) // STEPS, (s - 1) % STEPS
                    otok = tok[:, o % 3]
                    for l in range(1, LEVELS + 1):
                        n = LEVELS * s + l - 1
                        c = l - 1
                        t, b = c // 2, slice((c % 2) * C, (c % 2 + 1) * C)
                        if s < S:
                            pe.wait_ge(join_done, n + 1)
                            if l == 1:
                                pe.wait_ge(x0, s + 1)
                            else:
                                pe.wait_ge(xm_added, (LEVELS - 1) * s + l - 1)
                            for i in range(4):
                                mm = mmul(ps[:, 0, i * P:(i + 1) * P], join[:, n % 2, i, :], inv_m[:, i, :], start=True, stop=True)
                            mm.then_inc(u_done, 1)
                        if s and l <= 4:
                            if c == 0:
                                pe.wait_ge(bars_copied, s)
                            pe.wait_ge(st_new, 4 * o + c + op + 1)
                            if o and c == 0:
                                pe.wait_ge(y_copied, o)
                            for h, hs in halves:
                                mm = mmul(ps[b, 4 + h, c * HD:(c + 1) * HD], abar[hs, t, b], state[hs, op % 2, 4 * oq + c, :], start=True, stop=True)
                            mm.then_inc(sa_done, 1)
                        if s + 1 < S and l <= 4:
                            piece(s + 1, 2 * l - 2)
                        if s < S and l == 5:
                            if s + 1 < S:
                                pe.wait_ge(piece_dve, 6 * (s + 2))
                            for i in range(4):
                                mm = mmul(ps[:, 3, i * HD:(i + 1) * HD], m_a[:, s % 2, i // 2, 1, i % 2, :], tok[:, s % 3, 3, i % 2, halves[i // 2][1]],
                                          start=True, stop=True)
                            mm.then_inc(mv_done, 1)
                        if s < S:
                            pe.wait_ge(u_copied, n + 1)
                            if l > 1:
                                pe.wait_ge(xt_added, n)
                            if l < LEVELS:
                                for i in range(4):
                                    mm = mmul(ps[:, 1, i * P:(i + 1) * P], inv_t[:, i, :], um[:, i, :], start=True, stop=True)
                                mm.then_inc(xm_done, 1)
                            for i in range(4):
                                mm = mmul(ps[:, 2, i * P:(i + 1) * P], um[:, i, :], inv_t[:, i, :], start=True, stop=True)
                            mm.then_inc(xt_done, 1)
                        if s and l <= 4:
                            pe.wait_ge(sa_added, 4 * o + c + 1)
                            for h, hs in halves:
                                mmul(ps[hs, 4, 256 + c * HD:256 + (c + 1) * HD], otok[b, 1, t, hs], sa[b, t, hs], start=True, stop=False)
                                mm = mmul(ps[hs, 4, 256 + c * HD:256 + (c + 1) * HD], otok[b, 2, t, hs], otok[b, 3, t, hs], start=False, stop=True)
                            mm.then_inc(st_done, 1)
                        if s + 1 < S and l <= 4:
                            piece(s + 1, 2 * l - 1)
                        if s < S and (q, l) in side_work and p + 1 < PAIRS:
                            prepare(p + 1, side_work[(q, l)])
                        if s < S and (q, l) in gn_work and p >= 1:
                            group_norm(p - 1, gn_work[(q, l)])
                    if s < S:
                        pe.wait_ge(xt_added, LEVELS * (s + 1))
                        pe.wait_ge(mv_copied, s + 1)
                        for i in range(4):
                            h = halves[i // 2][1]
                            mmul(ps[h, 1, (i % 2) * P:(i % 2 + 1) * P], tok[:, s % 3, 0, i % 2, h], inv_t[:, i, :], start=True, stop=True)
                            mm = mmul(ps[:, 2, i * HD:(i + 1) * HD], inv_t[:, i, :], mv[:, i, :], start=True, stop=True)
                        mm.then_inc(bars_done, 1)
                    if s:
                        pe.wait_ge(st_new, 4 * s + op + 1)
                        for i in range(4):
                            hn, h = halves[i // 2]
                            t = i % 2
                            out = ps[h, 5, 256 + t * P:256 + (t + 1) * P]
                            mmul(out, sa[:, t, h], m_r[:, o % 3, hn, 0, t, :], start=True, stop=False)
                            mmul(out, otok[:, 3, t, h], m_r[:, o % 3, hn, 1, t, :], start=False, stop=False)
                            for b in range(2):
                                at = (2 * oq + t) * P + b * C
                                mm = mmul(ps[h, 5, 256 + t * P + b * C:256 + t * P + (b + 1) * C], state[h, op % 2, 4 * oq + 2 * t + b, :],
                                          r[h, op % 2, at:at + C], start=False, stop=(b == 1))
                        mm.then_inc(y_done, 1)
                for stage in ("mean", "sum", "bc"):
                    group_norm(PAIRS - 1, stage)

            @block.scalar
            def _(act):
                copy = lambda out, x: nc.scalar.activation(out, x, ACT.Copy)

                def prepare(p, stage):
                    b = p % 2
                    if stage == "z":
                        act.wait_ge(z_mm, p + 1)
                        act.wait_ge(feat, p)
                        nc.scalar.activation(cum[:], side, ACT.Sigmoid, bias=self.param("a_w0", p)).then_inc(z_act, 1)
                    elif stage == "a":
                        act.wait_ge(a_mm, p + 1)
                        nc.scalar.activation(a[:, b, :], side, ACT.Sigmoid, bias=self.param("a_a0", p)).then_inc(a_act, 1)
                    elif stage == "sq":
                        act.wait_ge(kk_raw, p + 1)
                        if p >= 3:
                            act.wait_ge(gn_sum, p - 2)
                        nc.scalar.activation(sq[:], kk[:, b, :], ACT.Square).then_inc(kk_sq, 1)
                    elif stage == "exp":
                        act.wait_ge(cum_done, p + 1)
                        nc.scalar.activation(dec_upto, chunks(tmp[:]), ACT.Exp, scale=-DECAY)
                        nc.scalar.activation(cum[:], tmp[:], ACT.Exp, scale=DECAY).then_inc(dec_done, 1)
                    elif stage == "g":
                        act.wait_ge(g_mm, p + 1)
                        if p >= 2:
                            act.wait_ge(pair_done, p - 1)
                        copy(g[:, b, :], side).then_inc(g_act, 1)

                def piece(s, i):
                    act.wait_ge(piece_mm, 8 * s + i + 1)
                    copy(tok[:, s % 3, 2 * i:2 * i + 2].rearrange("p a t c -> p (a t c)"), ps[:, 3, :]).then_inc(piece_act, 1)

                def group_square(p):
                    act.wait_ge(gn_centred, p + 1)
                    if p + 2 < PAIRS:
                        act.wait_ge(kk_sum, p + 3)
                    nc.scalar.activation(sq[:], y[:, p % 2, :], ACT.Square).then_inc(gn_sq, 1)

                act.wait_ge(lora_in, 7 * 16)
                nc.scalar.activation(lora[0:HD, :], lora[0:HD, :], ACT.Tanh)
                nc.scalar.activation(gate0[:], gate0[:], ACT.Sigmoid)
                nc.scalar.activation(gate1[:], gate1[:], ACT.Sigmoid).then_inc(lora_ready, 1)
                for stage in ("z", "a", "sq", "exp", "g"):
                    prepare(0, stage)
                piece(0, 0)
                piece(0, 1)
                for s in range(S + 1):
                    p, q = s // STEPS, s % STEPS
                    side_work = {(0, 1): ("z",), (0, 2): ("a",), (0, 3): ("sq",), (0, 5): ("exp",), (3, 1): ("g",)}
                    for l in range(1, LEVELS + 1):
                        n = LEVELS * s + l - 1
                        if s < S:
                            act.wait_ge(u_done, n + 1)
                            act.wait_ge(xt_done, n)
                            copy(flat(um[:]), ps[:, 0, :]).then_inc(u_copied, 1)
                        if s + 1 < S and l == 1:
                            piece(s + 1, 0)
                            piece(s + 1, 1)
                        if s < S and l == 5:
                            act.wait_ge(mv_done, s + 1)
                            copy(flat(mv[:]), ps[:, 3, 0:4 * HD]).then_inc(mv_copied, 1)
                        if s < S and p + 1 < PAIRS:
                            for stage in side_work.get((q, l), ()):
                                prepare(p + 1, stage)
                        if s < S and (q, l) == (1, 2) and p >= 1:
                            group_square(p - 1)
                    if s < S:
                        act.wait_ge(bars_done, s + 1)
                        if s:
                            act.wait_ge(sa_added, 4 * s)
                        copy(flat(abar[:]), ps[:, 1, 0:2 * P])
                        copy(flat(vbar[:]), ps[:, 2, 0:4 * HD]).then_inc(bars_copied, 1)
                    if s:
                        o = s - 1
                        act.wait_ge(y_done, s)
                        copy(y[:, (o // STEPS) % 2, (o % STEPS) * 2 * P:(o % STEPS + 1) * 2 * P], ps[:, 5, 256:512]).then_inc(y_copied, 1)
                group_square(PAIRS - 1)

            @block.gpsimd
            def _(pool):
                def rsqrt(ready, buffer, done, p):
                    pool.wait_ge(ready, p + 1)
                    nc.gpsimd.tensor_tensor(buffer[:, 1, :], buffer[:, 0, :], self.const("minus_half"), ALU.pow).then_inc(done, 1)

                rsqrt(kk_ms, small, kk_rn, 0)
                for s in range(S):
                    p, q = s // STEPS, s % STEPS
                    pool.wait_ge(piece_dve, 6 * s + 4)
                    for l in range(1, LEVELS + 1):
                        n = LEVELS * s + l - 1
                        if n >= 2:
                            pool.wait_ge(u_done, n - 1)
                        nc.gpsimd.tensor_tensor(join[:, n % 2].rearrange("p (h t) c -> p h t c", h=2), m_a[:, s % 2, :, 0],
                                                self.mask4(f"join{l}"), ALU.mult).then_inc(join_done, 1)
                        if (q, l) == (1, 1) and p + 1 < PAIRS:
                            rsqrt(kk_ms, small, kk_rn, p + 1)
                        if (q, l) == (1, 5) and p >= 1:
                            rsqrt(gn_ms, small_gn, gn_rn, p - 1)
                rsqrt(gn_ms, small_gn, gn_rn, PAIRS - 1)

            @block.vector
            def _(dve):
                link = self.linker(dve, self.vector_link)
                tt, stt, ts = nc.vector.tensor_tensor, nc.vector.scalar_tensor_tensor, nc.vector.tensor_scalar

                def prepare(p, stage):
                    b = p % 2
                    rp, kp, vp, kkp, ap = r[:, b, :], k[:, b, :], v[:, b, :], kk[:, b, :], a[:, b, :]
                    if stage == "kk_raw":
                        dve.wait_ge(kv_in, 32 * (p + 1))
                        ts(kkp, kp, self.param("a_k_k", p), None, ALU.mult).then_inc(kk_raw, 1)
                    elif stage == "scan":
                        dve.wait_ge(z_act, p + 1)
                        dve.wait_ge(rk_sum, p)
                        for c in range(NC):
                            i = nc.vector.tensor_tensor_scan(tmp[:, c * C:(c + 1) * C], ones[:], cum[:, c * C:(c + 1) * C], 0.0, ALU.mult, ALU.add)
                        i.then_inc(cum_done, 1)
                    elif stage == "decay":
                        dve.wait_ge(dec_done, p + 1)
                        nc.vector.tensor_copy(chunk_decay[:, b, :], dec[:, :, C])
                    elif stage == "k":
                        dve.wait_ge(a_act, p + 1)
                        dve.wait_ge(dec_done, p + 1)
                        link(ts(tmp[:], ap, 1.0, self.param("a_k_a", p), ALU.subtract, ALU.mult))
                        link(stt(out=kp, in0=tmp[:], scalar=1.0, in1=kp, op0=ALU.add, op1=ALU.mult))
                    elif stage == "kk_ms":
                        dve.wait_ge(kk_sum, p + 1)
                        ts(small[:, 0, :], ps[:, 6, 0:16], 1e-24, None, ALU.max).then_inc(kk_ms, 1)
                    elif stage == "rk":
                        dve.wait_ge(r_in, 16 * (p + 1))
                        stt(out=tmp[:], in0=rp, scalar=self.param("a_r_k", p), in1=kp, op0=ALU.mult, op1=ALU.mult).then_inc(rk_done, 1)
                    elif stage == "kk":
                        dve.wait_ge(kk_bc, p + 1)
                        tt(kkp, kkp, side, ALU.mult).then_inc(kk_used, 1)
                        dve.wait_ge(kk_used, p + 1)
                    elif stage == "b":
                        link(tt(ap, kkp, ap, ALU.mult))
                        tt(ap, ap, cum[:], ALU.mult)
                    elif stage == "K":
                        tt(kp, kp, cum[:], ALU.mult)
                    elif stage == "R":
                        tt(chunks(rp), chunks(rp), dec_upto, ALU.mult)
                    elif stage == "A":
                        stt(out=chunks(kkp), in0=chunks(kkp), scalar=-1.0, in1=dec_before, op0=ALU.mult, op1=ALU.mult).then_inc(feat, 1)
                    elif stage == "bonus":
                        dve.wait_ge(rk_sum, p + 1)
                        tt(bonus[:, b, :], vp, side, ALU.mult).then_inc(bonus_done, 1)

                def group_norm(p, stage):
                    yp = y[:, p % 2, :]
                    if stage == "centre":
                        dve.wait_ge(gn_mean, p + 1)
                        stt(out=yp, in0=side, scalar=-1.0 / HD, in1=yp, op0=ALU.mult, op1=ALU.add).then_inc(gn_centred, 1)
                    elif stage == "ms":
                        dve.wait_ge(gn_sum, p + 1)
                        ts(small_gn[:, 0, :], ps[:, 6, 0:16], 1.0 / HD, GN_EPS, ALU.mult, ALU.add).then_inc(gn_ms, 1)
                    elif stage == "scale":
                        dve.wait_ge(gn_bc, p + 1)
                        tt(yp, yp, side, ALU.mult).then_inc(gn_scaled, 1)
                        dve.wait_ge(gn_scaled, p + 1)
                        link(ts(yp, yp, self.param("a_lnx_g", p), self.param("a_lnx_b", p), ALU.mult, ALU.add))
                    elif stage == "out":
                        link(tt(yp, yp, bonus[:, p % 2, :], ALU.add))
                        dve.wait_ge(g_act, p + 1)
                        tt(self.X[:, p, :], yp, g[:, p % 2, :], ALU.mult).then_inc(pair_done, 1)

                def piece(s, i):
                    h, kind = (i - 2) // 3, (i - 2) % 3
                    dve.wait_ge(piece_mm, 8 * s + i + 1)
                    quad = ps[:, 3, :].rearrange("p (a t c) -> p a t c", a=2, t=2)
                    if kind == 0:
                        done = tt(m_a[:, s % 2, h, 0:2], quad, self.mask4("before"), ALU.mult)
                    elif kind == 1:
                        done = tt(m_a[:, s % 2, h, 2], quad[:, 0], self.mask("pair0", 2), ALU.mult)
                    else:
                        done = tt(m_r[:, s % 3, h], quad, self.mask4("upto"), ALU.mult)
                    done.then_inc(piece_dve, 1)

                def zero_state(p):
                    nc.vector.memset(state[:, p % 2, 0, :], 0.0).then_inc(st_new, 1)

                nc.vector.memset(dec[:, :, 0:1], 1.0)
                link(nc.vector.memset(ones[:], 1.0))
                for stage in ("kk_raw", "scan", "k", "kk_ms", "rk", "kk", "decay", "b", "K", "bonus", "R", "A"):
                    prepare(0, stage)
                for i in range(2, 8):
                    piece(0, i)
                for s in range(S + 1):
                    p, q = s // STEPS, s % STEPS
                    side_work = {(0, 1): ("kk_raw",), (0, 3): ("scan",), (0, 5): ("kk_ms",), (1, 1): ("k",), (1, 2): ("decay",),
                                 (1, 3): ("rk",), (1, 4): ("kk",), (1, 5): ("b",), (2, 1): ("K",), (2, 4): ("bonus", "R"), (2, 5): ("A",)}
                    gn_work = {(1, 2): ("centre",), (1, 5): ("ms",), (2, 2): ("scale",), (2, 3): ("out",)}
                    o, op, oq = s - 1, (s - 1) // STEPS, (s - 1) % STEPS
                    if s < S:
                        dve.wait_ge(piece_dve, 6 * (s + 1))
                        if s:
                            dve.wait_ge(bars_done, s)
                        four = lambda x: x.rearrange("p (h t) c -> p h t c", h=2)
                        link(tt(four(inv_t[:]), m_a[:, s % 2, :, 0], self.mask4("join0"), ALU.mult))
                        tt(four(inv_m[:]), m_a[:, s % 2, :, 2], self.mask4("ident"), ALU.add)
                        tt(four(inv_t[:]), four(inv_t[:]), self.mask4("ident"), ALU.add).then_inc(x0, 1)
                    if o >= 0 and oq == 0:
                        zero_state(op)
                    for l in range(1, LEVELS + 1):
                        n = LEVELS * s + l
                        c = l - 1
                        t, b = c // 2, slice((c % 2) * C, (c % 2 + 1) * C)
                        if s and l <= 4:
                            dve.wait_ge(sa_done, 4 * o + c + 1)
                            if c == 0:
                                dve.wait_ge(bars_copied, s)
                            tt(sa[b, t, :].rearrange("p (h c) -> p h c", h=2), ps[b, 4:6, c * HD:(c + 1) * HD],
                               vbar[b].rearrange("p (h t) c -> p h t c", h=2)[:, :, t, :], ALU.add).then_inc(sa_added, 1)
                        if s + 1 < S and 2 <= l <= 4:
                            piece(s + 1, 2 * l - 2)
                        if s < S:
                            if l < LEVELS:
                                dve.wait_ge(xm_done, (LEVELS - 1) * s + l)
                                tt(inv_m[:], inv_m[:], ps[:, 1, :].rearrange("p (i c) -> p i c", i=4), ALU.add).then_inc(xm_added, 1)
                            dve.wait_ge(xt_done, n)
                            tt(inv_t[:], inv_t[:], ps[:, 2, :].rearrange("p (i c) -> p i c", i=4), ALU.add).then_inc(xt_added, 1)
                        if s and l <= 4:
                            ci = 4 * oq + c
                            dve.wait_ge(st_done, 4 * o + c + 1)
                            link(tt(stmp[:], ps[:, 4, 256 + c * HD:256 + (c + 1) * HD], state[:, op % 2, ci, :], ALU.add))
                            ts(state[:, op % 2, ci + 1, :], stmp[:], chunk_decay[:, op % 2, ci:ci + 1], None, ALU.mult).then_inc(st_new, 1)
                            dve.wait_ge(st_new, 4 * o + c + op + 2)
                        if s + 1 < S and 2 <= l <= 4:
                            piece(s + 1, 2 * l - 1)
                        if s < S and p + 1 < PAIRS:
                            for stage in side_work.get((q, l), ()):
                                prepare(p + 1, stage)
                        if s < S and p >= 1:
                            for stage in gn_work.get((q, l), ()):
                                group_norm(p - 1, stage)
                for stage in ("centre", "ms", "scale", "out"):
                    group_norm(PAIRS - 1, stage)
        self.phase_over()

    def spread(self, cols, slot, tiles=TT):
        nc, ps = self.nc, self.ps
        for t in range(tiles):
            for h in range(2):
                mm = nc.tensor.matmul(ps[h * HD:(h + 1) * HD, 2 * slot + t // 4, (t % 4) * P:(t % 4 + 1) * P],
                                      cols[:, 2 * t + h:2 * t + h + 1].broadcast_to([P, HD]), self.const("ident"), start=True, stop=True)
        return mm


    def phase_fox(self):
        pairs = [dict(q=p, k=self.kv_dram[p], v=self.kv_dram[6 + p], gate=6 + p, out=p) for p in range(PAIRS)]
        self.phase_attention("fox", pairs, T, causal=True)

    def phase_mem_attention(self, layer, q_at):
        pairs = [dict(q=q_at + p, k=self.memk_dram[2 * layer + p], v=self.memv_dram[2 * layer + p], gate=None, out=PAIRS + p)
                 for p in range(MEM_PAIRS)]
        self.phase_attention(f"mem{layer}", pairs, M, causal=False)

    def phase_attention(self, name, pairs, width, causal):
        nc, ps = self.nc, self.ps
        with ExitStack() as ctx:
            sb = lambda n, shape: self.sb(ctx, f"{name}_{n}", shape)
            self.phase_begins(name)
            sg = self.sem
            q, k, v = sb("q", [P, 2, T]), sb("k", [P, 2, width]), sb("v", [P, 2, width // P, P])
            gate = sb("gate", [P, 2, T])
            negc = sb("negc", [P, 2, 2, T if causal else 1])
            prob = sb("prob", [P, 2, width])
            prob_t = sb("prob_t", [P, 2, width // P, P])
            stat = sb("stat", [P, 4, 4])
            o = sb("o", [P, 2, P])
            mask_parts = self.sb(ctx, f"{name}_mask", [P, 2, P], F32R)
            qk_in, rest_in, mask_ready = sg("qk_in"), sg("rest_in"), sg("mask_ready")
            scored, maxed, exped, turned, pt_d, pt_a, pv, o_norm, ot, stored = (
                sg(n) for n in ("scored", "maxed", "exped", "turned", "pt_d", "pt_a", "pv", "o_norm", "ot", "stored"))
            block = ctx.enter_context(nc.Block())
            N = len(pairs)
            refill = range(self.split_upto, self.first["out0"] + RING) if name == "mem0" else range(0)
            order = range(TT - 1, -1, -1) if causal else range(TT)
            units = [(p, t, h) for p in range(N) for t in order for h in range(2)]
            G, U = len(units), 2 * TT
            keys = lambda g: (units[g][1] + 1) * P if causal else width
            second_bank = lambda n: sum(1 for g in range(n) if keys(g) > HALF)
            rests = 3 if causal else 1
            hs = (slice(0, HD), slice(HD, P))

            @block.sync
            def _(sp):
                for strip in refill:
                    self.load_strip(sp, strip)
                for p, pr in enumerate(pairs):
                    b = p % 2
                    if p >= 2:
                        sp.wait_ge(stored, TT * (p - 1))
                    sp.dma_start(q[:, b, :], self.u_dram[pr["q"]]).then_inc(qk_in, 16)
                    sp.dma_start(k[:, b, :], pr["k"]).then_inc(qk_in, 16)
                    if causal:
                        sp.dma_start(negc[:, b, :, :], self.negc_dram[2 * p:2 * p + 2, :].partition_broadcast(P)).then_inc(rest_in, 16)
                        sp.dma_start(gate[:, b, :], self.u_dram[pr["gate"]]).then_inc(rest_in, 16)
                    sp.dma_start(v[:, b].rearrange("p a c -> p (a c)"), pr["v"]).then_inc(rest_in, 16)
                    sp.wait_ge(qk_in, 32 * (p + 1))
                    sp.wait_ge(rest_in, 16 * rests * (p + 1))

            @block.tensor
            def _(pe):
                mmul = nc.tensor.matmul
                if causal:
                    pe.wait_ge(mask_ready, 1)
                for i in range(G + 4):
                    g = i
                    if g < G:
                        p, t, h = units[g]
                        b = p % 2
                        if g % U == 0:
                            pe.wait_ge(qk_in, 32 * (p + 1))
                        if g >= 2:
                            pe.wait_ge((maxed if causal else exped), g - 1)
                        nk = keys(g)
                        for c in range(0, nk, HALF):
                            w = min(HALF, nk - c)
                            last = c + w == nk
                            mm = mmul(ps[:, 2 * (g % 2) + c // HALF, 0:w], q[hs[h], b, t * P:(t + 1) * P], k[hs[h], b, c:c + w],
                                      start=True, stop=not (causal and last))
                            if causal and last:
                                mm = mmul(ps[:, 2 * (g % 2) + c // HALF, w - P:w], mask_parts[:, 0, :], mask_parts[:, 1, :],
                                          start=False, stop=True)
                        mm.then_inc(scored, 1)
                    g = i - 1
                    if 0 <= g < G:
                        pe.wait_ge(exped, g + 1)
                        pe.wait_ge(pt_d, g)
                        pe.wait_ge(pt_a, second_bank(g))
                        for j in range(keys(g) // P):
                            mm = nc.tensor.transpose(ps[:, 4 + j // 4, (j % 4) * P:(j % 4 + 1) * P], prob[:, g % 2, j * P:(j + 1) * P],
                                                     self.const("ident"))
                        mm.then_inc(turned, 1)
                    g = i - 2
                    if 0 <= g < G:
                        p, t, h = units[g]
                        pe.wait_ge(pt_d, g + 1)
                        pe.wait_ge(pt_a, second_bank(g + 1))
                        pe.wait_ge(o_norm, g)
                        if g % U == 0:
                            pe.wait_ge(rest_in, 16 * rests * (p + 1))
                        nj = keys(g) // P
                        for j in range(nj):
                            mm = mmul(ps[:, 6, 0:HD], prob_t[:, g % 2, j, :], v[:, p % 2, j, hs[h]], start=(j == 0), stop=(j == nj - 1))
                        mm.then_inc(pv, 1)
                    g = i - 3
                    if 0 <= g < G and g % 2:
                        pe.wait_ge(o_norm, g + 1)
                        pe.wait_ge(stored, (g + 1) // 2 - 1)
                        nc.tensor.transpose(ps[:, 7, 0:P], o[:, (g // 2) % 2, :], self.const("ident")).then_inc(ot, 1)

            @block.scalar
            def _(act):
                for i in range(G + 4):
                    g = i
                    if g < G:
                        nk = keys(g)
                        act.wait_ge(maxed, g + 1)
                        src = prob[:, g % 2, 0:nk] if causal else ps[:, 2 * (g % 2), 0:nk]
                        if g >= 2 and not causal:
                            act.wait_ge(turned, g - 1)
                        if g >= 4:
                            act.wait_ge(o_norm, g - 3)
                        nc.scalar.activation(prob[:, g % 2, 0:nk], src, ACT.Exp, bias=stat[:, g % 4, 1:2],
                                             accum_out=stat[:, g % 4, 2:3]).then_inc(exped, 1)
                    g = i - 1
                    if 0 <= g < G and keys(g) > HALF:
                        nj = keys(g) // P
                        act.wait_ge(turned, g + 1)
                        if g >= 2:
                            act.wait_ge(pv, g - 1)
                        nc.scalar.activation(prob_t[:, g % 2, 4:nj, :].rearrange("p a c -> p (a c)"), ps[:, 5, 0:(nj - 4) * P], ACT.Copy).then_inc(pt_a, 1)

            @block.gpsimd
            def _(pool):
                for strip in refill:
                    self.split_strip(pool, strip)

            @block.vector
            def _(dve):
                link = self.linker(dve, self.vector_link)
                if causal:
                    nc.vector.tensor_copy(mask_parts[:, 0, :], self.const("ident"))
                    nc.vector.tensor_copy(mask_parts[:, 1, :], self.const("future")).then_inc(mask_ready, 1)
                for i in range(G + 4):
                    g = i
                    if g < G:
                        p, t, h = units[g]
                        nk = keys(g)
                        if g % U == 0:
                            dve.wait_ge(rest_in, 16 * rests * (p + 1))
                        dve.wait_ge(scored, g + 1)
                        s4 = stat[:, g % 4]
                        if causal:
                            if g >= 2:
                                dve.wait_ge(turned, g - 1)
                            link(nc.vector.tensor_tensor_reduce(
                                out=prob[:, g % 2, 0:nk], in0=self.bank2(g % 2)[:, 0:nk], in1=negc[:, p % 2, h, 0:nk], scale=1.0, scalar=-3e38,
                                op0=ALU.add, op1=ALU.max, accum_out=s4[:, 0:1]))
                        else:
                            link(nc.vector.tensor_reduce(s4[:, 0:1], ps[:, 2 * (g % 2), 0:nk], AX_X, ALU.max))
                        nc.vector.tensor_scalar(s4[:, 1:2], s4[:, 0:1], -1.0, None, ALU.mult).then_inc(maxed, 1)
                    g = i - 1
                    if 0 <= g < G:
                        nj = min(4, keys(g) // P)
                        dve.wait_ge(turned, g + 1)
                        if g >= 2:
                            dve.wait_ge(pv, g - 1)
                        nc.vector.tensor_copy(prob_t[:, g % 2, 0:nj, :].rearrange("p a c -> p (a c)"), ps[:, 4, 0:nj * P]).then_inc(pt_d, 1)
                    g = i - 2
                    if 0 <= g < G:
                        h = units[g][2]
                        s4 = stat[:, g % 4]
                        link(nc.vector.reciprocal(s4[:, 3:4], s4[:, 2:3]))
                        dve.wait_ge(pv, g + 1)
                        if h == 0 and g >= 4:
                            dve.wait_ge(ot, g // 2 - 1)
                        nc.vector.tensor_scalar(o[:, (g // 2) % 2, hs[h]], ps[:, 6, 0:HD], s4[:, 3:4], None, ALU.mult).then_inc(o_norm, 1)
                    g = i - 3
                    if 0 <= g < G and g % 2:
                        p, t, _ = units[g]
                        dve.wait_ge(ot, (g + 1) // 2)
                        dst = self.X[:, pairs[p]["out"], t * P:(t + 1) * P]
                        if causal:
                            nc.vector.tensor_tensor(dst, ps[:, 7, 0:P], gate[:, p % 2, t * P:(t + 1) * P], ALU.mult).then_inc(stored, 1)
                        else:
                            nc.vector.tensor_copy(dst, ps[:, 7, 0:P]).then_inc(stored, 1)
        self.split_upto = max(self.split_upto, refill.stop)
        self.raw_upto = max(self.raw_upto, refill.stop)
        self.phase_over()


    def phase_out_and_ffn(self, l):
        nc, ps = self.nc, self.ps
        with ExitStack() as scope:
            self.alloc_h(scope, f"f{l}")
            s0 = self.first[f"out{l}"]
            split_from, split_to = self.split_upto, s0 + KT + RING - 1
            with ExitStack() as ctx:
                self.phase_begins(f"out{l}")
                block = ctx.enter_context(nc.Block())

                @block.sync
                def _(sp):
                    for i in range(KT):
                        self.load_strip(sp, s0 + i + RING)
                        if i == 0:
                            sp.wait_ge(self.h_hi, KT)
                            sp.wait_ge(self.h_lo, KT)
                            sp.dma_start(self.X[:], self.x_dram).then_inc(self.loaded, 16)
                    sp.wait_ge(self.loaded, 16)

                @block.gpsimd
                def _(pool):
                    for s in range(split_from, split_to):
                        self.split_strip(pool, s)

                @block.scalar
                def _(act):
                    for k in range(KT):
                        nc.scalar.activation(self.hh[:, k, :], self.X[:, k, :], ACT.Copy).then_inc(self.h_hi, 1)

                @block.vector
                def _(dve):
                    link = self.linker(dve, self.vector_link)
                    for k in range(KT):
                        dve.wait_ge(self.h_hi, k + 1)
                        nc.vector.tensor_tensor(self.hl[:, k, :], self.X[:, k, :], self.hh[:, k, :].bitcast(F32), ALU.subtract).then_inc(self.h_lo, 1)
                    dve.wait_ge(self.loaded, 16)
                    for i in range(KT):
                        dve.wait_ge(self.strip_done, s0 + i + 1)
                        nc.vector.tensor_tensor(self.X[:, i, :], self.X[:, i, :], self.bank2(i % 3), ALU.add).then_inc(self.psum_free, 1)

                @block.tensor
                def _(pe):
                    for i in range(KT):
                        if i >= 3:
                            pe.wait_ge(self.psum_free, i - 2)
                        self.gemm_strip(pe, s0 + i, i % 3, self.hh, self.hl, "fm", T,
                                        (lambda k: pe.wait_ge(self.h_lo, k + 1)) if i == 0 else None)
            self.split_upto, self.raw_upto = split_to, s0 + KT + RING
            self.phase_over()
            self.phase_ffn(scope, l)

    def phase_ffn(self, scope, l):
        nc, ps = self.nc, self.ps
        GM = max(FF_GROUPS)
        s0 = self.first[f"up{l}0"]
        plan, f = [], 0
        for g, n in enumerate(FF_GROUPS):
            for j in range(n):
                plan += [("gate", f, j), ("up", f, j)]
                f += 1
            plan += [("down", c, (n, f)) for c in range(KT)]
        with ExitStack() as ctx:
            ah = self.sb(ctx, f"act_hi{l}", [P, GM, T], F32R)
            al = self.sb(ctx, f"act_lo{l}", [P, GM, T], F32R)
            silu = self.sb(ctx, f"silu{l}", [P, 2, T])
            full = self.sb(ctx, f"full_f{l}", [P, 2, T])
            rms = self.sb(ctx, f"rms_f{l}", [P, T])
            self.phase_begins(f"ffn{l}")
            sg = self.sem
            silu_done, act_full, act_hi, act_lo = sg("silu"), sg("act_full"), sg("act_hi"), sg("act_lo")
            block = ctx.enter_context(nc.Block())
            split_from = self.split_upto
            load_from, load_to = self.raw_upto, min(s0 + len(plan) + RING, len(self.strips))
            split_to = min(s0 + len(plan) + RING - 1, len(self.strips))

            @block.sync
            def _(sp):
                for s in range(load_from, load_to):
                    self.load_strip(sp, s)

            @block.gpsimd
            def _(pool):
                for s in range(split_from, split_to):
                    self.split_strip(pool, s)

            @block.scalar
            def _(act):
                self.norm_act(act, f"ffn_norm{l}", silu)
                for i, (kind, f, j) in enumerate(plan):
                    if kind == "gate":
                        act.wait_ge(self.psum_free, i + 1)
                        nc.scalar.activation(silu[:, f % 2, :], silu[:, f % 2, :], ACT.Silu).then_inc(silu_done, 1)
                    elif kind == "up":
                        act.wait_ge(act_full, f + 1)
                        nc.scalar.activation(ah[:, j, :], full[:, f % 2, :], ACT.Copy).then_inc(act_hi, 1)

            @block.vector
            def _(dve):
                link = self.linker(dve, self.vector_link)
                self.norm_dve(dve, f"ffn_norm{l}", silu, rms)
                for i, (kind, f, j) in enumerate(plan):
                    if kind == "gate":
                        dve.wait_ge(self.strip_done, s0 + i + 1)
                        nc.vector.tensor_tensor(silu[:, f % 2, :], self.bank2(i % 3), rms[:], ALU.mult).then_inc(self.psum_free, 1)
                    elif kind == "up":
                        dve.wait_ge(self.strip_done, s0 + i + 1)
                        nc.vector.tensor_tensor(full[:, f % 2, :], self.bank2(i % 3), rms[:], ALU.mult).then_inc(self.psum_free, 1)
                        dve.wait_ge(self.psum_free, i + 1)
                        dve.wait_ge(silu_done, f + 1)
                        nc.vector.tensor_tensor(full[:, f % 2, :], full[:, f % 2, :], silu[:, f % 2, :], ALU.mult).then_inc(act_full, 1)
                        dve.wait_ge(act_full, f + 1)
                        dve.wait_ge(act_hi, f + 1)
                        nc.vector.tensor_tensor(al[:, j, :], full[:, f % 2, :], ah[:, j, :].bitcast(F32), ALU.subtract).then_inc(act_lo, 1)
                    elif kind == "down":
                        dve.wait_ge(self.strip_done, s0 + i + 1)
                        if j[1] != FF_GROUPS[0]:
                            dve.wait_ge(self.psum_free, i)
                        nc.vector.tensor_tensor(self.X[:, f, :], self.X[:, f, :], self.bank2(i % 3), ALU.add).then_inc(self.psum_free, 1)

            @block.tensor
            def _(pe):
                for i, (kind, f, j) in enumerate(plan):
                    if i >= 3:
                        pe.wait_ge(self.psum_free, i - 2)
                    if kind != "down":
                        self.gemm_strip(pe, s0 + i, i % 3, self.hh, self.hl, "fm", T, self.norm_before(pe, i, rms))
                    else:
                        n, upto = j
                        self.gemm_strip(pe, s0 + i, i % 3, ah, al, "fm", T,
                                        (lambda k: pe.wait_ge(act_lo, upto - n + k + 1)) if f == 0 else None)
        self.split_upto, self.raw_upto = split_to, load_to
        self.phase_over()


    def phase_store(self):
        nc, ps = self.nc, self.ps
        with ExitStack() as ctx:
            xo = self.sb(ctx, "x_out", [P, TT, D])
            self.phase_begins("store")
            turned, even_out, odd_out = (self.sem(n) for n in ("turned", "even_out", "odd_out"))
            out_stored = self.out_stored
            block = ctx.enter_context(nc.Block())

            @block.tensor
            def _(pe):
                for t in range(TT):
                    if t >= 4:
                        pe.wait_ge((even_out if t % 2 == 0 else odd_out), (t - 4) // 2 + 1)
                    for k in range(KT):
                        mm = nc.tensor.transpose(ps[:, 2 * (t % 4) + k // 4, (k % 4) * P:(k % 4 + 1) * P],
                                                 self.X[:, k, t * P:(t + 1) * P], self.const("ident"))
                    mm.then_inc(turned, 1)

            @block.vector
            def _(dve):
                link = self.linker(dve, self.vector_link)
                for t in range(0, TT, 2):
                    dve.wait_ge(turned, t + 1)
                    nc.vector.tensor_copy(xo[:, t, :], self.bank2(t % 4)).then_inc(even_out, 1)

            @block.scalar
            def _(act):
                for t in range(1, TT, 2):
                    act.wait_ge(turned, t + 1)
                    nc.scalar.activation(xo[:, t, :], self.bank2(t % 4), ACT.Copy).then_inc(odd_out, 1)

            @block.sync
            def _(sp):
                for t in range(TT):
                    sp.wait_ge((even_out if t % 2 == 0 else odd_out), t // 2 + 1)
                    sp.dma_start(self.out[0, t * P:(t + 1) * P, :], xo[:, t, :]).then_inc(out_stored, 16)
                sp.wait_ge(out_stored, 16 * TT)


_INS = ["x", "mem", "mix_norm", "w_out", "mem_norm", "w_mem_kv", "mem_q_gain", "mem_k_gain", "ffn_norm", "w_gate_up", "w_down",
        "a_w_in", "a_mu", "a_w0", "a_w_up", "a_a0", "a_a_up", "a_g_up", "a_k_k", "a_k_a", "a_r_k", "a_lnx_g", "a_lnx_b",
        "kv_norm", "w_kv", "b_f", "k_gain", "b_w_in", "b_q_gain"]


def kernel(**inputs):
    import concourse.bacc as bacc
    from concourse.bass_utils import run_bass_kernel_spmd

    nc = bacc.Bacc("TRN2", target_bir_lowering=False, num_devices=1)
    consts, place = shape_constants()
    arrays, aps = {}, {}
    for name, a in [(n, inputs[n]) for n in _INS] + [("consts", consts)]:
        a = np.ascontiguousarray(a)
        arrays[f"in_{name}"] = a
        aps[name] = nc.dram_tensor(f"in_{name}", a.shape, F32, kind="ExternalInput").ap()
    out = nc.dram_tensor("out_x", (1, T, D), F32, kind="ExternalOutput").ap()
    program = Program(nc, aps, out)
    program.place = place
    program.build()
    result = run_bass_kernel_spmd(nc, [arrays], core_ids=[0])
    return result.results[0]["out_x"]
```
